# Optimizing a Trainium2 kernel written in Bass

```python
import math
import jax
import jax.numpy as jnp
from jax import lax
import numpy as np

D_MODEL = 1024
BATCH = 1
SEQ = 256
DEPTH = 2

GRID_W = 64
CTX_LEN = 256
N_MLSTM_HEADS = 4
MLSTM_HEAD_DIM = 64
MLSTM_WIDTH = N_MLSTM_HEADS * MLSTM_HEAD_DIM
MLSTM_CHUNK = 64
N_DIFF_HEADS = 4
DIFF_QK_DIM = 64
DIFF_V_DIM = 2 * DIFF_QK_DIM
DIFF_WIDTH = N_DIFF_HEADS * DIFF_V_DIM
Q_BLOCK = 128
ROPE_BASE = 10000.0
CONV_WIDTH = 256
CONV_KERNEL = 31
MIX_WIDTH = MLSTM_WIDTH + DIFF_WIDTH + CONV_WIDTH
IN_SPLITS = (MLSTM_WIDTH, MLSTM_WIDTH, MLSTM_WIDTH, MLSTM_WIDTH, 4 * N_MLSTM_HEADS,
             2 * N_DIFF_HEADS * DIFF_QK_DIM, 2 * N_DIFF_HEADS * DIFF_QK_DIM, DIFF_WIDTH,
             2 * CONV_WIDTH)
D_IN = sum(IN_SPLITS)
D_FF = 2816
N_EXPERTS = 8
TOP_K = 2
D_FF_EXPERT = 1408
EPS = 1e-6
M_INIT = -1e30

kernel_name = 'hymba_style_mlstm_diffattn_conformer_moe_dit'

F32 = jnp.float32

def rmsnorm(x, g):
    x32 = x.astype(F32)
    y = x32 * lax.rsqrt(jnp.mean(x32 * x32, axis=-1, keepdims=True) + EPS)
    return (y * g.astype(F32)).astype(x.dtype)

def layernorm_f32(x, g, b):
    x32 = x.astype(F32)
    mu = jnp.mean(x32, axis=-1, keepdims=True)
    var = jnp.mean(jnp.square(x32 - mu), axis=-1, keepdims=True)
    return (x32 - mu) * lax.rsqrt(var + EPS) * g.astype(F32) + b.astype(F32)

def modulate(h, shift, scale):
    return h * (1 + scale) + shift

def split_cols(p):
    return jnp.split(p, np.cumsum(IN_SPLITS)[:-1].tolist(), axis=-1)

def rope_tables(n_tokens):
    rows = n_tokens // GRID_W
    row = jnp.repeat(jnp.arange(rows, dtype=F32), GRID_W)
    col = jnp.tile(jnp.arange(GRID_W, dtype=F32), rows)
    per_axis = DIFF_QK_DIM // 2
    inv = ROPE_BASE ** (-jnp.arange(0, per_axis, 2, dtype=F32) / per_axis)
    ang = jnp.stack([row[:, None] * inv, col[:, None] * inv], axis=1)
    return jnp.cos(ang), jnp.sin(ang)

def apply_axial_rope(x, cos, sin):
    shp = x.shape
    xr = x.astype(F32).reshape(shp[:-1] + (2, 2, DIFF_QK_DIM // 4))
    x1, x2 = xr[..., 0, :], xr[..., 1, :]
    out = jnp.stack([x1 * cos - x2 * sin, x2 * cos + x1 * sin], axis=-2)
    return out.reshape(shp).astype(x.dtype)

def mlstm_scan(q, k, v, log_i, log_f, state):
    bsz, nh, t_len, dh = q.shape
    nc = t_len // MLSTM_CHUNK
    lower = jnp.tril(jnp.ones((MLSTM_CHUNK, MLSTM_CHUNK), dtype=bool))

    def to_chunks(a):
        return jnp.moveaxis(a.reshape(a.shape[:2] + (nc, MLSTM_CHUNK) + a.shape[3:]), 2, 0)

    def step(carry, inp):
        c_st, n_st, m_st = carry
        qc, kc, vc, lic, lfc = inp
        b = jnp.cumsum(lfc, axis=-1)
        dmat = b[..., :, None] - b[..., None, :] + lic[..., None, :]
        dmat = jnp.where(lower, dmat, -jnp.inf)
        inter = b + m_st[..., None]
        m_t = jnp.maximum(inter, jnp.max(dmat, axis=-1))
        w = jnp.exp(dmat - m_t[..., None]) * jnp.einsum('bhld,bhsd->bhls', qc, kc)
        e_inter = jnp.exp(inter - m_t)
        num = (e_inter[..., None] * jnp.einsum('bhvd,bhld->bhlv', c_st, qc)
               + jnp.einsum('bhls,bhsv->bhlv', w, vc))
        den = e_inter * jnp.einsum('bhd,bhld->bhl', n_st, qc) + jnp.sum(w, axis=-1)
        h = num / jnp.maximum(jnp.abs(den), jnp.exp(-m_t))[..., None]
        b_last = b[..., -1]
        g = b_last[..., None] - b + lic
        m_new = jnp.maximum(b_last + m_st, jnp.max(g, axis=-1))
        e_old = jnp.exp(b_last + m_st - m_new)
        e_g = jnp.exp(g - m_new[..., None])
        c_new = e_old[..., None, None] * c_st + jnp.einsum('bhs,bhsv,bhsd->bhvd', e_g, vc, kc)
        n_new = e_old[..., None] * n_st + jnp.einsum('bhs,bhsd->bhd', e_g, kc)
        return (c_new, n_new, m_new), h

    state, hs = lax.scan(step, state, (to_chunks(q), to_chunks(k), to_chunks(v),
                                       to_chunks(log_i), to_chunks(log_f)))
    return jnp.moveaxis(hs, 0, 2).reshape(bsz, nh, t_len, dh), state

def mlstm_mixer(lat, cx, b_gates, g_head, need_ctx):
    def prep(q, k, v, gates):
        bsz, n, _ = q.shape

        def heads(t):
            return t.astype(F32).reshape(bsz, n, N_MLSTM_HEADS, MLSTM_HEAD_DIM).transpose(0, 2, 1, 3)

        g = (gates.astype(F32) + b_gates.astype(F32)).transpose(0, 2, 1)
        i_f, f_f, i_b, f_b = jnp.split(g, 4, axis=1)
        return (heads(q), heads(k) * MLSTM_HEAD_DIM ** -0.5, heads(v),
                (i_f, jax.nn.log_sigmoid(f_f)), (i_b, jax.nn.log_sigmoid(f_b)))

    def flip(a):
        return jnp.flip(a, axis=2)

    def run(q, k, v, gates, state, reverse):
        li, lf = gates
        if reverse:
            h, st = mlstm_scan(flip(q), flip(k), flip(v), flip(li), flip(lf), state)
            return flip(h), st
        return mlstm_scan(q, k, v, li, lf, state)

    def finish(h, o_pre):
        bsz, nh, n, dh = h.shape
        mu = jnp.mean(h, axis=-1, keepdims=True)
        var = jnp.mean(jnp.square(h - mu), axis=-1, keepdims=True)
        hn = ((h - mu) * lax.rsqrt(var + EPS)).transpose(0, 2, 1, 3).reshape(bsz, n, nh * dh)
        return (jax.nn.sigmoid(o_pre.astype(F32)) * hn * g_head.astype(F32)).astype(o_pre.dtype)

    ql, kl, vl, fwd_l, bwd_l = prep(lat[0], lat[1], lat[2], lat[4])
    qc, kc, vc, fwd_c, bwd_c = prep(cx[0], cx[1], cx[2], cx[4])
    bsz = ql.shape[0]
    init = (jnp.zeros((bsz, N_MLSTM_HEADS, MLSTM_HEAD_DIM, MLSTM_HEAD_DIM), F32),
            jnp.zeros((bsz, N_MLSTM_HEADS, MLSTM_HEAD_DIM), F32),
            jnp.full((bsz, N_MLSTM_HEADS), M_INIT, F32))
    h_cf, st_f = run(qc, kc, vc, fwd_c, init, False)
    h_cb, st_b = run(qc, kc, vc, bwd_c, init, True)
    h_lf, _ = run(ql, kl, vl, fwd_l, st_f, False)
    h_lb, _ = run(ql, kl, vl, bwd_l, st_b, True)
    out_l = finish(h_lf + h_lb, lat[3])
    out_c = finish(h_cf + h_cb, cx[3]) if need_ctx else None
    return out_l, out_c

def diff_attention(q_lat, k_lat, v_lat, q_ctx, k_ctx, v_ctx, lam, lam_init, g_subln, need_ctx):
    bsz, s_len, _ = q_lat.shape

    def heads_qk(t):
        n = t.shape[1]
        return t.reshape(bsz, n, N_DIFF_HEADS, 2, DIFF_QK_DIM).transpose(0, 2, 3, 1, 4)

    def heads_v(t):
        n = t.shape[1]
        return t.reshape(bsz, n, N_DIFF_HEADS, DIFF_V_DIM).transpose(0, 2, 1, 3)

    cos, sin = rope_tables(s_len)
    ql = apply_axial_rope(heads_qk(q_lat), cos, sin)
    kl = apply_axial_rope(heads_qk(k_lat), cos, sin)
    kc = heads_qk(k_ctx)
    vc = heads_v(v_ctx)
    k_all = jnp.concatenate([kl, kc], axis=3)
    v_all = jnp.concatenate([heads_v(v_lat), vc], axis=2)
    scale = DIFF_QK_DIM ** -0.5

    def attend(q, k, v):
        s = jnp.einsum('bhcqd,bhckd->bhcqk', q, k, preferred_element_type=F32) * scale
        p = jax.nn.softmax(s, axis=-1)
        a = p[:, :, 0] - lam * p[:, :, 1]
        return jnp.einsum('bhqk,bhkv->bhqv', a, v.astype(F32))

    def finish(o):
        n = o.shape[2]
        o = rmsnorm(o, g_subln) * (1.0 - lam_init)
        return o.transpose(0, 2, 1, 3).reshape(bsz, n, DIFF_WIDTH).astype(q_lat.dtype)

    nb = s_len // Q_BLOCK
    qb = jnp.moveaxis(ql.reshape(bsz, N_DIFF_HEADS, 2, nb, Q_BLOCK, DIFF_QK_DIM), 3, 0)
    ob = lax.map(lambda qblk: attend(qblk, k_all, v_all), qb)
    o_lat = finish(jnp.moveaxis(ob, 0, 2).reshape(bsz, N_DIFF_HEADS, s_len, DIFF_V_DIM))
    o_ctx = finish(attend(heads_qk(q_ctx), kc, vc)) if need_ctx else None
    return o_lat, o_ctx

def conv_mixer(p, w_dw, b_dw, g_ln, b_ln):
    a, gt = jnp.split(p, 2, axis=-1)
    u = a * jax.nn.sigmoid(gt)
    y = lax.conv_general_dilated(u, w_dw[:, None, :], window_strides=(1,),
                                 padding=[(CONV_KERNEL // 2, CONV_KERNEL // 2)],
                                 dimension_numbers=('NWC', 'WIO', 'NWC'),
                                 feature_group_count=CONV_WIDTH) + b_dw
    return jax.nn.silu(layernorm_f32(y, g_ln, b_ln)).astype(p.dtype)

def swiglu(h, wg, wu, wd):
    return (jax.nn.silu(h @ wg) * (h @ wu)) @ wd

def moe_swiglu(h, w_r, b_r, wg, wu, wd):
    logits = (h @ w_r + b_r).astype(F32)
    probs = jax.nn.softmax(logits, axis=-1)
    top_v, top_i = lax.top_k(probs, TOP_K)
    top_v = top_v / jnp.sum(top_v, axis=-1, keepdims=True)
    combine = jnp.sum(jax.nn.one_hot(top_i, N_EXPERTS, dtype=F32) * top_v[..., None], axis=-2)
    combine = combine.astype(h.dtype)
    y = jnp.zeros_like(h)
    for e in range(N_EXPERTS):
        y = y + combine[..., e:e + 1] * swiglu(h, wg[e], wu[e], wd[e])
    return y

def setup_inputs(seed: int = 0) -> dict:
    key = jax.random.key(seed)
    ks = jax.random.split(key, 32)
    n_dense = (DEPTH + 1) // 2
    n_moe = DEPTH // 2

    def nrm(k, shape, scale):
        return jax.random.normal(k, shape, F32) * scale

    gate_offset = jnp.tile(jnp.repeat(jnp.array([0.0, 3.0], F32), N_MLSTM_HEADS), 2)
    return {
        'x': nrm(ks[0], (BATCH, SEQ, D_MODEL), 1.0),
        'c': nrm(ks[1], (BATCH, D_MODEL), 1.0),
        'ctx': nrm(ks[2], (BATCH, CTX_LEN, D_MODEL), 1.0),
        'c_ctx': nrm(ks[3], (D_MODEL,), 1.0),
        'w_mod': nrm(ks[4], (DEPTH, D_MODEL, 6 * D_MODEL), 0.5 * D_MODEL ** -0.5),
        'b_mod': nrm(ks[5], (DEPTH, 6 * D_MODEL), 0.02),
        'g_norm1': 1.0 + nrm(ks[6], (DEPTH, D_MODEL), 0.02),
        'w_in': nrm(ks[7], (DEPTH, D_MODEL, D_IN), D_MODEL ** -0.5),
        'b_gates': nrm(ks[8], (DEPTH, 4 * N_MLSTM_HEADS), 0.1) + gate_offset,
        'g_mlstm': 1.0 + nrm(ks[9], (DEPTH, MLSTM_WIDTH), 0.02),
        'lambda_q1': nrm(ks[10], (DEPTH, DIFF_QK_DIM), 0.1),
        'lambda_k1': nrm(ks[11], (DEPTH, DIFF_QK_DIM), 0.1),
        'lambda_q2': nrm(ks[12], (DEPTH, DIFF_QK_DIM), 0.1),
        'lambda_k2': nrm(ks[13], (DEPTH, DIFF_QK_DIM), 0.1),
        'g_subln': 1.0 + nrm(ks[14], (DEPTH, DIFF_V_DIM), 0.02),
        'w_dw': nrm(ks[15], (DEPTH, CONV_KERNEL, CONV_WIDTH), CONV_KERNEL ** -0.5),
        'b_dw': nrm(ks[16], (DEPTH, CONV_WIDTH), 0.02),
        'g_conv_ln': 1.0 + nrm(ks[17], (DEPTH, CONV_WIDTH), 0.02),
        'b_conv_ln': nrm(ks[18], (DEPTH, CONV_WIDTH), 0.02),
        'w_out': nrm(ks[19], (DEPTH, MIX_WIDTH, D_MODEL), MIX_WIDTH ** -0.5),
        'g_norm2': 1.0 + nrm(ks[20], (DEPTH, D_MODEL), 0.02),
        'w_ffn_gate': nrm(ks[21], (n_dense, D_MODEL, D_FF), D_MODEL ** -0.5),
        'w_ffn_up': nrm(ks[22], (n_dense, D_MODEL, D_FF), D_MODEL ** -0.5),
        'w_ffn_down': nrm(ks[23], (n_dense, D_FF, D_MODEL), D_FF ** -0.5),
        'w_router': nrm(ks[24], (n_moe, D_MODEL, N_EXPERTS), D_MODEL ** -0.5),
        'b_router': nrm(ks[25], (n_moe, N_EXPERTS), 0.01),
        'w_exp_gate': nrm(ks[26], (n_moe, N_EXPERTS, D_MODEL, D_FF_EXPERT), D_MODEL ** -0.5),
        'w_exp_up': nrm(ks[27], (n_moe, N_EXPERTS, D_MODEL, D_FF_EXPERT), D_MODEL ** -0.5),
        'w_exp_down': nrm(ks[28], (n_moe, N_EXPERTS, D_FF_EXPERT, D_MODEL), D_FF_EXPERT ** -0.5),
        'g_final': 1.0 + nrm(ks[29], (D_MODEL,), 0.02),
    }

def reference(x, c, ctx, c_ctx, w_mod, b_mod, g_norm1, w_in, b_gates, g_mlstm,
              lambda_q1, lambda_k1, lambda_q2, lambda_k2, g_subln, w_dw, b_dw,
              g_conv_ln, b_conv_ln, w_out, g_norm2, w_ffn_gate, w_ffn_up, w_ffn_down,
              w_router, b_router, w_exp_gate, w_exp_up, w_exp_down, g_final):
    cond_x = jax.nn.silu(c)
    cond_c = jax.nn.silu(c_ctx)
    h_ctx = ctx
    for l in range(DEPTH):
        last = l == DEPTH - 1
        mod_x = jnp.split((cond_x @ w_mod[l] + b_mod[l])[:, None, :], 6, axis=-1)
        mod_c = jnp.split((cond_c @ w_mod[l] + b_mod[l])[None, None, :], 6, axis=-1)

        hx = modulate(rmsnorm(x, g_norm1[l]), mod_x[0], mod_x[1])
        hc = modulate(rmsnorm(h_ctx, g_norm1[l]), mod_c[0], mod_c[1])
        px = split_cols(hx @ w_in[l])
        pc = split_cols(hc @ w_in[l])

        m_x, m_c = mlstm_mixer(px[0:5], pc[0:5], b_gates[l], g_mlstm[l], not last)

        lam_init = 0.8 - 0.6 * math.exp(-0.3 * l)
        lam = (jnp.exp(jnp.dot(lambda_q1[l].astype(F32), lambda_k1[l].astype(F32)))
               - jnp.exp(jnp.dot(lambda_q2[l].astype(F32), lambda_k2[l].astype(F32))) + lam_init)
        d_x, d_c = diff_attention(px[5], px[6], px[7], pc[5], pc[6], pc[7],
                                  lam, lam_init, g_subln[l], not last)

        c_x = conv_mixer(px[8], w_dw[l], b_dw[l], g_conv_ln[l], b_conv_ln[l])
        x = x + mod_x[2] * (jnp.concatenate([m_x, d_x, c_x], axis=-1) @ w_out[l])
        if not last:
            c_c = conv_mixer(pc[8], w_dw[l], b_dw[l], g_conv_ln[l], b_conv_ln[l])
            h_ctx = h_ctx + mod_c[2] * (jnp.concatenate([m_c, d_c, c_c], axis=-1) @ w_out[l])

        j = l // 2
        if l % 2 == 0:
            def ffn(h):
                return swiglu(h, w_ffn_gate[j], w_ffn_up[j], w_ffn_down[j])
        else:
            def ffn(h):
                return moe_swiglu(h, w_router[j], b_router[j], w_exp_gate[j], w_exp_up[j], w_exp_down[j])
        x = x + mod_x[5] * ffn(modulate(rmsnorm(x, g_norm2[l]), mod_x[3], mod_x[4]))
        if not last:
            h_ctx = h_ctx + mod_c[5] * ffn(modulate(rmsnorm(h_ctx, g_norm2[l]), mod_c[3], mod_c[4]))
    return rmsnorm(x, g_final)


_drawn_inputs = setup_inputs


def setup_inputs(seed=0):
    import zlib

    import numpy as np

    out = dict(_drawn_inputs(seed))
    spreads = {}
    factors = {'g_norm1': 4.804,
     'g_mlstm': 8.0,
     'lambda_q1': 4.246,
     'lambda_k1': 6.836,
     'g_subln': 8.0,
     'b_dw': 6.063,
     'g_conv_ln': 8.0,
     'b_conv_ln': 8.0,
     'g_norm2': 3.851,
     'b_router': 6.247,
     'g_final': 24.574,
     'lambda_q2': 44.448}
    for name, (base, spread) in spreads.items():
        noise = np.random.default_rng([zlib.crc32(name.encode()), seed]).standard_normal(out[name].shape)
        drawn = base * np.exp(spread * noise) if base else spread * noise
        out[name] = jnp.asarray(drawn.astype(out[name].dtype))
    for name, factor in factors.items():
        out[name] = (out[name] * factor).astype(out[name].dtype)
    return out
```

```python
import math
from contextlib import ExitStack

import numpy as np
import concourse.bass as bass
from concourse import mybir

F32 = mybir.dt.float32
ALU = mybir.AluOpType
ACT = mybir.ActivationFunctionType
AX_X = mybir.AxisListType.X

P = 128
D = 1024
KD = D // P
SEQ = 256
CTX = 256
T = CTX + SEQ
NB = T // P
DEPTH = 2
NH = 4
DH = 64
DV = 128
MW = NH * DH
CW = 256
TAPS = 31
PAD = TAPS // 2
FF = 2816
FT = FF // P
NE = 8
FE = 1408
ET = FE // P
EPS = 1e-6
NEG = -1e30

CHUNK = 256
SLOT = KD * CHUNK
RING = 8
ESLOT = 3 * KD * P
NBANK = 7
MOD_CHUNKS = 6 * D // CHUNK
GATE_ROWS = 100

IN_ORDER = ["mk", "mq", "mv", "ak0", "ak1", "aq0", "aq1", "av0", "av1", "cg", "ca", "mo"]
IN_COL = {"mq": 0, "mk": 256, "mv": 512, "mo": 768, "aq0": 1040, "aq1": 1296, "ak0": 1552,
          "ak1": 1808, "av0": 2064, "av1": 2320, "ca": 2576, "cg": 2832}
GATE_COL = 1024


def fields(sizes):
    at, out = 0, {}
    for name, n in sizes:
        out[name] = (at, n)
        at += n
    return out, at


CONST, NCONST = fields([("ident", P), ("ones", P), ("mask_f", P), ("mask_b", P), ("cos", SEQ), ("sin", SEQ),
                        ("reset", T), ("pick", NH * 2 * P), ("order", NE), ("eps", 1), ("one", 1)])
SMALL, NSMALL = fields([("c", 2 * KD), ("b_mod", DEPTH * 48), ("g1", DEPTH * KD), ("g2", DEPTH * KD),
                        ("b_gates", DEPTH), ("g_mlstm", DEPTH * 2), ("lam", DEPTH * 4 * DH), ("g_sub", DEPTH),
                        ("w_dw", DEPTH * 2 * TAPS), ("b_dw", DEPTH * 2), ("g_ln", DEPTH * 2), ("b_ln", DEPTH * 2),
                        ("g_final", KD), ("w_router", KD * NE), ("b_router", NE)])


def sequence_block(direction, block):
    return block if direction == 0 else [1, 0, 3, 2][block]


def block_pairs(direction, source, layer):
    low = 0 if layer < DEPTH - 1 else 2
    j = sequence_block(direction, source)
    targets = [t for t in range(low, NB) if sequence_block(direction, t) >= j]
    runs = []
    for t in targets:
        if runs and runs[-1][1] == t:
            runs[-1][1] = t + 1
        else:
            runs.append([t, t + 1])
    return runs


class Signal:

    def __init__(self, plan, handle, name):
        self.plan, self.handle, self.name, self.count = plan, handle, name, 0

    def tick(self, key):
        self.count += 1
        self.plan[self.name, key] = self.count
        return self.handle, 1

    def at(self, key):
        return self.handle, self.plan[self.name, key] if self.plan.get("complete") else 1


def build(nc, A, plan):
    with ExitStack() as ctx:
        def sb(name, shape):
            return ctx.enter_context(nc.sbuf_tensor("sb_" + name, shape, F32))

        def signal(name):
            return Signal(plan, ctx.enter_context(nc.semaphore(name)), name)

        def semaphore(name):
            return ctx.enter_context(nc.semaphore(name))

        X = sb("X", [P, KD, T])
        H = sb("H", [P, KD * T])
        arena = sb("arena", [P, ET * ESLOT])
        con = sb("con", [P, NCONST])
        small = sb("small", [P, NSMALL])
        rstd = sb("rstd", [P, T])
        modc = sb("modc", [P, DEPTH, 48, 2])
        gain = sb("gain", [P, DEPTH, 2, KD, 2])
        cond = sb("cond", [P, KD, 2])
        kq = sb("kq", [P, NB, T])
        rows_n = sb("rows_n", [P, 6, T])
        cols = sb("cols", [P, 2, NB, 64])
        tiny = sb("tiny", [P, 512])
        ps = ctx.enter_context(nc.psum_tensor("ps", [P, 8, 512], F32))

        hT = H[:, :].rearrange("p (k t) -> p k t", k=KD)
        mix = hT
        hsum = H[:, 6 * T:8 * T].rearrange("p (b h v) -> p b h v", b=NB, h=NH)
        h2 = H[:, 0:KD * SEQ].rearrange("p (k t) -> p k t", k=KD)
        comb = H[:, KD * SEQ:2 * KD * SEQ].rearrange("p (e t) -> p e t", e=NE)
        ring = arena[:, 0:RING * SLOT].rearrange("p (s n) -> p s n", s=RING)
        experts = arena[:, :].rearrange("p (f n) -> p f n", f=ET)
        work = arena[:, RING * SLOT:ET * ESLOT]
        sq = work[:, 0:KD * T].rearrange("p (k t) -> p k t", k=KD)
        U = work[:, 0:FT * T].rearrange("p (f t) -> p f t", f=FT)
        top = [0]

        def take(n):
            top[0] += n
            return work[:, top[0] - n:top[0]]

        mq = take(2 * T).rearrange("p (m t) -> p m t", m=2)
        mk = take(2 * T).rearrange("p (m t) -> p m t", m=2)
        mo = take(2 * T).rearrange("p (m t) -> p m t", m=2)
        aq = take(4 * T).rearrange("p (m t) -> p m t", m=4)
        ak = take(4 * T).rearrange("p (m t) -> p m t", m=4)
        vm = take(NB * NH * (DH + 1)).rearrange("p (b h v) -> p b h v", b=NB, h=NH)
        va = take(NB * NH * DV).rearrange("p (b n) -> p b n", b=NB)
        upad = take(2 * 2 * (SEQ + 2 * PAD)).rearrange("p (m s t) -> p m s t", m=2, s=2)
        assert top[0] >= FT * T
        cy = take(2 * T)
        w_gates = cy[:, 0:KD * GATE_ROWS].rearrange("p (k n) -> p k n", k=KD)
        cy = cy.rearrange("p (m t) -> p m t", m=2)
        tap = take(T)
        scratch = take(2 * NB * T)
        gate_raw = scratch[:, 0:T]
        gate_ls = scratch[:, T:2 * T]
        li = scratch[0:64, 2 * T:3 * T]
        lf = scratch[0:64, 3 * T:4 * T]
        row_r = scratch[0:64, 4 * T:8 * T].rearrange("p (j t) -> p j t", j=NB)
        row_a, row_em = kq[0:64, 0, :], kq[0:64, 1, :]
        row_b, row_m = kq[0:64, 2, :], kq[0:64, 3, :]
        W = scratch.rearrange("p (u b t) -> p u b t", u=2, b=NB)
        prob = scratch[:, 0:4 * T].rearrange("p (u c t) -> p u c t", u=2, c=2)
        probT = scratch[:, 4 * T:6 * T].rearrange("p (u b q) -> p u b q", u=2, b=NB)
        osq = scratch[:, 0:4 * T].rearrange("p (h t) -> p h t", h=NH)
        hsq = kq[:, 0:2, :].rearrange("p a t -> p (a t)")
        ehid = rows_n[:, 0:2, :].rearrange("p a t -> p (a t)").rearrange("p (u t) -> p u t", u=4)
        esilu = rows_n[:, 2:4, :].rearrange("p a t -> p (a t)").rearrange("p (u t) -> p u t", u=4)
        zeros = rows_n[:, 4, :]
        combT = rows_n[0:64, 5, 0:SEQ]

        def field(t, table, name):
            a, n = table[name]
            return t[:, a:a + n]

        def par(name, l=None):
            t = field(small, SMALL, name)
            return t if l is None else t.rearrange("p (l n) -> p l n", l=DEPTH)[:, l]

        ident, ones = field(con, CONST, "ident"), field(con, CONST, "ones")
        mask = [field(con, CONST, "mask_f"), field(con, CONST, "mask_b")]
        cos, sin = field(con, CONST, "cos"), field(con, CONST, "sin")
        reset = field(con, CONST, "reset")[0:64, :]
        pick = field(con, CONST, "pick").rearrange("p (i n) -> p i n", i=2 * NH)[0:64]
        order = field(con, CONST, "order")
        eps, one = field(con, CONST, "eps"), field(con, CONST, "one")
        lam = tiny[:, 0:8].rearrange("p (l n) -> p l n", l=DEPTH)
        rs = tiny[:, 8:32].rearrange("p (u n) -> p u n", u=2)
        den = tiny[:, 32:64].rearrange("p (a b) -> p a b", a=2 * NH)
        stat = tiny[:, 64:128].rearrange("p (a n) -> p a n", a=4)
        rt = tiny[:, 128:256].rearrange("p (a b e) -> p a b e", a=8, b=2)
        rc = tiny[:, 256:384].rearrange("p (b r) -> p b r", b=2)
        r1 = tiny[:, 384:400].rearrange("p (a b) -> p a b", a=8)
        lprod = tiny[:, 0:512]

        sem_small = semaphore("parameters_loaded")
        sem_con = semaphore("constants_loaded")
        sem_x = semaphore("tokens_loaded")
        sem_gw = [semaphore(f"gate_weights_loaded_{l}") for l in range(DEPTH)]
        sem_slot = [semaphore(f"ring_slot_loaded_{s}") for s in range(RING)]
        sem_exp = [semaphore(f"expert_tile_loaded_{f}") for f in range(ET)]
        sem_out = semaphore("output_stored")
        pe_done = signal("pe_done")
        act_drained = signal("act_drained")
        dve_drained = signal("dve_drained")
        act_done = signal("act_done")
        dve_done = signal("dve_done")
        pool_done = signal("pool_done")
        gu_full = semaphore("gate_up_full")
        silu_done = semaphore("silu_done")
        glu_done = semaphore("glu_done")
        hidden_ready = semaphore("hidden_ready")
        down_done = semaphore("down_done")

        block = ctx.enter_context(nc.Block())

        chunks = [("mod", 0, i) for i in range(MOD_CHUNKS)]
        for l in range(DEPTH):
            chunks += [("in", l, n) for n in IN_ORDER]
            if l == 0:
                chunks += [("mod", 1, i) for i in range(MOD_CHUNKS)]
            chunks += [("out", l, i) for i in range(D // CHUNK)]
            if l == 0:
                chunks += [(k, 0, i) for i in range(FF // CHUNK) for k in ("gate", "up")]
                chunks += [("down", 0, (i, j)) for i in range(D // CHUNK) for j in range(3)]
        slot_of = {c: n for n, c in enumerate(chunks)}

        def last_product(chunk):
            kind, l, i = chunk
            if kind == "in":
                return (i, l, NB - 1) if i in ("mv", "av0", "av1") else (i, l, 1)
            if kind == "out":
                return ("y", l, 2 * i + 1)
            if kind == "down":
                return chunk if i[1] < 2 else ("ffn", 2 * i[0] + 1)
            return (kind, 2 * i + 1) if kind in ("gate", "up") else chunk

        def low(l):
            return 0 if l < DEPTH - 1 else CTX

        @block.sync
        def _(sp):
            sp.dma_start(small[:, :], A["small"]).then_inc(sem_small, 16)
            for n, (kind, l, i) in enumerate(chunks):
                if n == 4:
                    sp.dma_start(con[:, :], A["con"]).then_inc(sem_con, 16)
                    sp.dma_start(X[:, :, :], A["x"].rearrange("p (k t) -> p k t", k=KD)).then_inc(sem_x, 16)
                if kind == "in" and i == IN_ORDER[0]:
                    if l > 0:
                        sp.wait_ge(*pe_done.at(("cvar", l - 1)))
                        sp.wait_ge(*dve_done.at(("cn", l - 1)))
                        sp.wait_ge(*act_done.at(("mix_conv", l - 1)))
                    sp.dma_start(w_gates, A["gates"][l].rearrange("p (k n) -> p k n", k=KD)).then_inc(sem_gw[l], 16)
                if n >= RING:
                    sp.wait_ge(*pe_done.at(last_product(chunks[n - RING])))
                width = SLOT
                if kind == "mod":
                    src = A["mod"][l, i]
                elif kind == "in":
                    src = A["in"][l, IN_ORDER.index(i)]
                elif kind == "out":
                    src = A["out"][l, i]
                elif kind in ("gate", "up"):
                    src = A[kind][i]
                else:
                    src = A["down"][i[0], i[1]]
                    width = min(KD, FT - KD * i[1]) * CHUNK
                sp.dma_start(ring[:, n % RING, 0:width], src[:, 0:width]).then_inc(sem_slot[n % RING], 16)

            sp.wait_ge(*act_done.at(("h", 1, 1)))
            for f in range(ET):
                sp.dma_start(experts[:, f, :], A["experts"][0, f]).then_inc(sem_exp[f], 16)
            with sp.Fori(1, NE) as e:
                for f in range(ET):
                    sp.wait_ge(down_done, e * ET + (f + 1 - ET))
                    sp.dma_start(experts[:, f, :], A["experts"][bass.ds(e, 1), f].rearrange("a p n -> (a p) n"))\
                      .then_inc(sem_exp[f], 16)
            sp.wait_ge(*dve_done.at("final"))
            sp.dma_start(A["out_0"].rearrange("p (k t) -> p k t", k=KD), h2).then_inc(sem_out, 16)
            sp.wait_ge(sem_out, 16)

        @block.tensor
        def _(pe):
            opened = []

            def open_bank(key):
                n = len(opened)
                if n >= NBANK:
                    last = opened[n - NBANK]
                    drainer = act_drained if ("act_drained", last) in plan else dve_drained
                    pe.wait_ge(*drainer.at(last))
                opened.append(key)
                plan["bank", key] = n % NBANK
                return ps[:, n % NBANK, :]

            def loaded(chunk):
                n = slot_of[chunk]
                pe.wait_ge(sem_slot[n % RING], 16 * (n // RING + 1))
                return ring[:, n % RING, :].rearrange("p (k n) -> p k n", k=KD)

            def modulation(l, i):
                w = loaded(("mod", l, i))
                if i == 0 and l == 0:
                    pe.wait_ge(*act_done.at("cond"))
                if i == 0 and l > 0:
                    pe.wait_ge(*dve_done.at(("modc", l - 1)))
                for m in range(2):
                    at = 2 * (2 * i + m)
                    for k in range(KD):
                        ins = pe.matmul(ps[:, 7, at:at + 2], w[:, k, m * P:(m + 1) * P], cond[:, k, :],
                                        start=(k == 0), stop=(k == KD - 1))
                ins.then_inc(*pe_done.tick(("mod", l, i)))

            def norm(l, which):
                lo = low(l) if which else 0
                if l == 0:
                    pe.wait_ge(sem_con, 16)
                for half in range(2):
                    pe.wait_ge(*act_done.at(("sq", l, which, half)))
                    if half == 0:
                        o = open_bank(("ssq", l, which))
                    for k in range(4 * half, 4 * half + 4):
                        ins = pe.matmul(o[:, 0:T - lo], ones, sq[:, k, 0:T - lo], start=(k == 0), stop=(k == KD - 1))
                ins.then_inc(*pe_done.tick(("ssq", l, which)))

            def project(l):
                pe.wait_ge(*act_done.at(("h", l, 0)))
                pe.wait_ge(sem_gw[l], 16)
                o = open_bank(("gates", l))
                for k in range(KD):
                    ins = pe.matmul(o[0:GATE_ROWS, :], w_gates[:, k, :], hT[:, k, :], start=(k == 0), stop=(k == KD - 1))
                ins.then_inc(*pe_done.tick(("gates", l)))
                for name in IN_ORDER:
                    w = loaded(("in", l, name))
                    if name in ("mv", "av0", "av1"):
                        for b in range(NB):
                            o = open_bank((name, l, b))
                            for k in range(KD):
                                ins = pe.matmul(o[:, 0:CHUNK], hT[:, k, b * P:(b + 1) * P], w[:, k, :],
                                                start=(k == 0), stop=(k == KD - 1))
                            ins.then_inc(*pe_done.tick((name, l, b)))
                    else:
                        a = 0 if name in ("mk", "ak0", "ak1") else low(l)
                        for m in range(2):
                            o = open_bank((name, l, m))
                            for k in range(KD):
                                ins = pe.matmul(o[:, a:T], w[:, k, m * P:(m + 1) * P], hT[:, k, a:T],
                                                start=(k == 0), stop=(k == KD - 1))
                            ins.then_inc(*pe_done.tick((name, l, m)))

            filler = {0: [(1, i) for i in range(MOD_CHUNKS)], 1: []}

            def fill(l, n):
                for _ in range(n):
                    if filler[l]:
                        modulation(*filler[l].pop(0))

            def mlstm(l):
                pe.wait_ge(*dve_done.at(("rows", l)))
                o = open_bank(("cols", l)).rearrange("p (a b r) -> p a b r", a=2, b=NB)
                for a in range(2):
                    for b in range(NB):
                        ins = pe.transpose(o[:, a, b, :], rows_n[0:64, 4 + a, b * P:(b + 1) * P], ident[0:64, 0:64])
                ins.then_inc(*pe_done.tick(("cols", l)))

                def products(h):
                    r0, m = DH * (h % 2), h // 2
                    for s in range(NB):
                        a = max(low(l), CTX if s >= 2 else 0)
                        o = open_bank(("kq", l, h, s))
                        pe.matmul(o[:, a:T], mk[r0:r0 + DH, m, s * P:(s + 1) * P], mq[r0:r0 + DH, m, a:T],
                                  start=True, stop=True).then_inc(*pe_done.tick(("kq", l, h, s)))
                    for d in range(2):
                        row = d * NH + h
                        for s in range(NB):
                            j = sequence_block(d, s)
                            o = open_bank(("dec", l, h, d, s))
                            for a, b in block_pairs(d, s, l):
                                spans = [(a, b)]
                                if a <= s < b:
                                    spans = [(x, y) for x, y in ((a, s), (s + 1, b)) if y > x]
                                    pe.matmul(o[:, s * P:(s + 1) * P], pick[:, row, :],
                                              rows_n[0:64, j, s * P:(s + 1) * P], start=True, stop=False)
                                    ins = pe.matmul(o[:, s * P:(s + 1) * P], ident, mask[d], start=False, stop=True)
                                for x, y in spans:
                                    ins = pe.matmul(o[:, x * P:y * P], pick[:, row, :],
                                                    rows_n[0:64, j, x * P:y * P], start=True, stop=True)
                            ins.then_inc(*pe_done.tick(("dec", l, h, d, s)))

                def sums(h):
                    for d in range(2):
                        pe.wait_ge(*dve_done.at(("w", l, h, d, NB - 1)))
                        o = open_bank(("pv", l, h, d)).rearrange("p (b c) -> p b c", b=NB)
                        for t in range(low(l) // P, NB):
                            src = [s for s in range(NB) if sequence_block(d, s) <= sequence_block(d, t)]
                            for s in src:
                                ins = pe.matmul(o[:, t, 0:DH + 1], W[:, d, s, t * P:(t + 1) * P], vm[:, s, h, :],
                                                start=(s == src[0]), stop=(s == src[-1]))
                        ins.then_inc(*pe_done.tick(("pv", l, h, d)))

                pe.wait_ge(*act_drained.at(("mq", l, 1)))
                for h in range(NH):
                    products(h)
                    fill(l, 2)
                    if h == 0:
                        pe.wait_ge(*act_drained.at(("mv", l, NB - 1)))
                        pe.wait_ge(*pool_done.at(("pads", l)))
                    sums(h)
                pe.wait_ge(*dve_done.at(("hn", l)))
                for m in range(2):
                    o = open_bank(("hT", l, m))
                    for b in range(low(l) // P, NB):
                        ins = pe.transpose(o[:, b * P:(b + 1) * P],
                                           hsum[:, b, 2 * m:2 * m + 2, :].rearrange("p h v -> p (h v)"), ident)
                    ins.then_inc(*pe_done.tick(("hT", l, m)))

            def attention(l):
                units = [(h, t) for h in range(NH) for t in range(low(l) // P, NB)]

                def scores(n):
                    h, t = units[n]
                    nk = CTX if t < 2 else T
                    for c in range(2):
                        o = open_bank(("s", l, h, t, c))
                        pe.matmul(o[:, 0:nk], aq[c * DH:(c + 1) * DH, h, t * P:(t + 1) * P],
                                  ak[c * DH:(c + 1) * DH, h, 0:nk], start=True, stop=True)\
                          .then_inc(*pe_done.tick(("s", l, h, t, c)))

                def turn(n):
                    h, t = units[n]
                    nk = CTX if t < 2 else T
                    pe.wait_ge(*dve_done.at(("a", l, h, t)))
                    o = open_bank(("aT", l, h, t))
                    for b in range(nk // P):
                        ins = pe.transpose(o[:, b * P:(b + 1) * P], prob[:, n % 2, 0, b * P:(b + 1) * P], ident)
                    ins.then_inc(*pe_done.tick(("aT", l, h, t)))

                def values(n):
                    h, t = units[n]
                    nb = 2 if t < 2 else NB
                    pe.wait_ge(*act_drained.at(("aT", l, h, t)))
                    o = open_bank(("o", l, h, t))
                    for b in range(nb):
                        ins = pe.matmul(o[:, 0:P], va[:, b, h * DV:(h + 1) * DV], probT[:, n % 2, b, :],
                                        start=(b == 0), stop=(b == nb - 1))
                    ins.then_inc(*pe_done.tick(("o", l, h, t)))

                pe.wait_ge(*dve_done.at(("rope", l, "aq1")))
                pe.wait_ge(*act_drained.at(("av1", l, NB - 1)))
                for n in range(len(units) + 2):
                    if n < len(units):
                        scores(n)
                    fill(l, 1)
                    if 1 <= n <= len(units):
                        turn(n - 1)
                    if n >= 2:
                        values(n - 2)
                fill(l, MOD_CHUNKS)
                lo = low(l)
                for h in range(NH):
                    pe.wait_ge(*act_done.at(("osq", l, h)))
                    o = open_bank(("osum", l, h))
                    pe.matmul(o[:, lo:T], ones, osq[:, h, lo:T], start=True, stop=True)\
                      .then_inc(*pe_done.tick(("osum", l, h)))

            def conv_norm(l):
                lo = low(l)
                pe.wait_ge(*pool_done.at(("conv", l)))
                o = open_bank(("cmean", l))
                for m in range(2):
                    ins = pe.matmul(o[:, lo:T], ones, cy[:, m, lo:T], start=(m == 0), stop=(m == 1))
                ins.then_inc(*pe_done.tick(("cmean", l)))
                pe.wait_ge(*act_done.at(("csq", l)))
                o = open_bank(("cvar", l))
                for m in range(2):
                    ins = pe.matmul(o[:, lo:T], ones, kq[:, m, lo:T], start=(m == 0), stop=(m == 1))
                ins.then_inc(*pe_done.tick(("cvar", l)))

            def output(l):
                lo = low(l)
                pe.wait_ge(*act_done.at(("mix_conv", l)))
                pe.wait_ge(*dve_done.at(("mix_attn", l)))
                pe.wait_ge(*dve_drained.at(("hT", l, 1)))
                for i in range(D // CHUNK):
                    w = loaded(("out", l, i))
                    for m in range(2):
                        o = open_bank(("y", l, 2 * i + m))
                        for k in range(KD):
                            ins = pe.matmul(o[:, lo:T], w[:, k, m * P:(m + 1) * P], mix[:, k, lo:T],
                                            start=(k == 0), stop=(k == KD - 1))
                        ins.then_inc(*pe_done.tick(("y", l, 2 * i + m)))

            def dense():
                pe.wait_ge(*act_done.at(("h", 0, 1)))
                for i in range(FF // CHUNK):
                    w = {k: loaded((k, 0, i)) for k in ("gate", "up")}
                    for m in range(2):
                        for kind in ("gate", "up"):
                            o = open_bank((kind, 2 * i + m))
                            for k in range(KD):
                                ins = pe.matmul(o, w[kind][:, k, m * P:(m + 1) * P], hT[:, k, :],
                                                start=(k == 0), stop=(k == KD - 1))
                            ins.then_inc(*pe_done.tick((kind, 2 * i + m)))
                pe.wait_ge(*dve_drained.at(("up", FT - 1)))
                for i in range(D // CHUNK):
                    o = [open_bank(("ffn", 2 * i + m)) for m in range(2)]
                    for j in range(3):
                        w = loaded(("down", 0, (i, j)))
                        for m in range(2):
                            for k in range(KD * j, min(FT, KD * j + KD)):
                                ins = pe.matmul(o[m], w[:, k - KD * j, m * P:(m + 1) * P], U[:, k, :],
                                                start=(k == 0), stop=(k == FT - 1))
                            if j == 2 and m == 0:
                                ins.then_inc(*pe_done.tick(("ffn", 2 * i)))
                        if j < 2:
                            ins.then_inc(*pe_done.tick(("down", 0, (i, j))))
                    ins.then_inc(*pe_done.tick(("ffn", 2 * i + 1)))

            def router():
                pe.wait_ge(*act_done.at(("h", 1, 1)))
                o = open_bank("logits")
                w = par("w_router").rearrange("p (k e) -> p k e", k=KD)
                for b in range(2):
                    for k in range(KD):
                        ins = pe.matmul(o[:, b * NE:(b + 1) * NE], h2[:, k, b * P:(b + 1) * P], w[:, k, :],
                                        start=(k == 0), stop=(k == KD - 1))
                ins.then_inc(*pe_done.tick("logits"))
                pe.wait_ge(*dve_done.at("combine"))
                o = open_bank("combT")
                for b in range(2):
                    ins = pe.transpose(o[0:64, b * P:(b + 1) * P], rc[:, b, :], ident)
                ins.then_inc(*pe_done.tick("combT"))
                pe.wait_ge(*dve_drained.at("combT"))
                for e in range(0, NE, 2):
                    o = open_bank(("comb", e))
                    for i in range(2):
                        ins = pe.matmul(o[:, i * SEQ:(i + 1) * SEQ], pick[:, e + i, :], combT, start=True, stop=True)
                    ins.then_inc(*pe_done.tick(("comb", e)))

            def moe():
                pe.wait_ge(*dve_drained.at(("comb", NE - 2)))
                for b in range(4):
                    pe.matmul(ps[:, 4 + b, :], zeros[:, 0:P], zeros, start=True, stop=False, skip_group_check=True)

                def expert(e, first):
                    def down(f):
                        pe.wait_ge(hidden_ready, f + 1 if first else e * ET + (f + 1))
                        wd = experts[:, f, 2 * KD * P:3 * KD * P]
                        for m in range(KD):
                            ins = pe.matmul(ps[:, 4 + m // 2, (m % 2) * SEQ:(m % 2 + 1) * SEQ], wd[:, m * P:(m + 1) * P],
                                            ehid[:, f % 4, :], start=False, stop=False, skip_group_check=True)
                        ins.then_inc(down_done, 1)

                    for f in range(ET):
                        pe.wait_ge(sem_exp[f], 16 if first else e * 16 + 16)
                        if f >= 4:
                            pe.wait_ge(glu_done, f - 3 if first else e * ET + (f - 3))
                        elif not first:
                            last = max(x for x in range(ET) if x % 4 == f)
                            pe.wait_ge(glu_done, e * ET + (last + 1 - ET))
                        for i in range(2):
                            w = experts[:, f, i * KD * P:(i + 1) * KD * P].rearrange("p (k n) -> p k n", k=KD)
                            for k in range(KD):
                                ins = pe.matmul(ps[:, f % 4, i * SEQ:(i + 1) * SEQ], w[:, k, :], h2[:, k, :],
                                                start=(k == 0), stop=(k == KD - 1))
                        ins.then_inc(gu_full, 1)
                        if f:
                            down(f - 1)
                    down(ET - 1)

                expert(0, True)
                with pe.Fori(1, NE) as e:
                    expert(e, False)

            for i in range(MOD_CHUNKS):
                modulation(0, i)
            for l in range(DEPTH):
                norm(l, 0)
                project(l)
                mlstm(l)
                attention(l)
                conv_norm(l)
                output(l)
                norm(l, 1)
                if l == 0:
                    dense()
            router()
            moe()
            pe.wait_ge(*act_done.at("final_sq"))
            for k in range(KD):
                ins = pe.matmul(ps[:, 0, 0:SEQ], ones, experts[:, 0, k * SEQ:(k + 1) * SEQ],
                                start=(k == 0), stop=(k == KD - 1))
            ins.then_inc(*pe_done.tick("final_ssq"))

        @block.scalar
        def _(act):
            f = nc.scalar.activation

            def full(key):
                act.wait_ge(*pe_done.at(key))
                return ps[:, plan.get(("bank", key), 0), :]

            def norm(l, which):
                lo = low(l) if which else 0
                if which == 1:
                    act.wait_ge(*dve_drained.at(("y", l, KD - 1)))
                elif l == 0:
                    act.wait_ge(sem_con, 16)
                    act.wait_ge(sem_x, 16)
                else:
                    act.wait_ge(*dve_drained.at(("ffn", KD - 1)))
                for half in range(2):
                    k = slice(4 * half, 4 * half + 4)
                    f(sq[:, k, 0:T - lo], X[:, k, lo:T], ACT.Square).then_inc(*act_done.tick(("sq", l, which, half)))
                o = full(("ssq", l, which))
                f(rstd[:, 0:T - lo], o[:, 0:T - lo], ACT.Sqrt, scale=1.0 / D, bias=eps)\
                    .then_inc(*act_drained.tick(("ssq", l, which)))
                if which == 0:
                    act.wait_ge(*dve_done.at(("modc", l)))
                dst = h2 if lo else hT
                for k in range(KD):
                    act.wait_ge(*dve_done.at(("xn", l, which, k)))
                    for s in range(lo // CTX, 2):
                        a = s * SEQ - lo
                        ins = f(dst[:, k, a:a + SEQ], sq[:, k, a:a + SEQ], ACT.Identity,
                                scale=gain[:, l, which, k, s:s + 1], bias=modc[:, l, 24 * which + k, s:s + 1])
                ins.then_inc(*act_done.tick(("h", l, which)))

            def project(l):
                lo, R = low(l), GATE_ROWS
                o = full(("gates", l))
                f(gate_raw[0:R, :], o[0:R, :], ACT.Identity, bias=par("b_gates")[0:R, l:l + 1])\
                    .then_inc(*act_drained.tick(("gates", l)))
                act.wait_ge(*act_drained.at(("gates", l)))
                f(gate_ls[0:R, :], gate_raw[0:R, :], ACT.Abs).then_inc(*act_done.tick(("gabs", l)))
                act.wait_ge(*act_done.at(("gabs", l)))
                f(gate_ls[0:R, :], gate_ls[0:R, :], ACT.Exp, scale=-1.0).then_inc(*act_done.tick(("gexp", l)))
                act.wait_ge(*act_done.at(("gexp", l)))
                f(gate_ls[0:R, :], gate_ls[0:R, :], ACT.Ln, bias=one[0:R, :]).then_inc(*act_done.tick(("gln", l)))
                for name in IN_ORDER:
                    if name == "mv":
                        for b in range(NB):
                            o = full((name, l, b))
                            f(vm[:, b, :, 0:DH], o[:, 0:MW].rearrange("p (h v) -> p h v", h=NH), ACT.Copy)\
                                .then_inc(*act_drained.tick((name, l, b)))
                        act.wait_ge(*dve_done.at(("row_m", l)))
                        f(row_em, row_m, ACT.Exp, scale=-1.0).then_inc(*act_done.tick(("row_em", l)))
                    elif name in ("av0", "av1"):
                        for b in range(NB):
                            o = full((name, l, b))
                            i = CHUNK * int(name[-1])
                            f(va[:, b, i:i + CHUNK], o[:, 0:CHUNK], ACT.Copy).then_inc(*act_drained.tick((name, l, b)))
                    elif name == "ca":
                        continue
                    else:
                        for m in range(2):
                            o = full((name, l, m))
                            if name == "mk":
                                f(mk[:, m, :], o, ACT.Copy, scale=DH ** -0.5).then_inc(*act_drained.tick((name, l, m)))
                            elif name == "mq":
                                f(mq[:, m, lo:T], o[:, lo:T], ACT.Copy).then_inc(*act_drained.tick((name, l, m)))
                            elif name in ("ak0", "ak1"):
                                f(ak[:, 2 * int(name[-1]) + m, :], o, ACT.Copy).then_inc(*act_drained.tick((name, l, m)))
                            elif name in ("aq0", "aq1"):
                                f(aq[:, 2 * int(name[-1]) + m, lo:T], o[:, lo:T], ACT.Copy)\
                                    .then_inc(*act_drained.tick((name, l, m)))
                            elif name == "cg":
                                f(mo[:, m, lo:T], o[:, lo:T], ACT.Sigmoid).then_inc(*act_drained.tick((name, l, m)))
                            else:
                                act.wait_ge(*dve_drained.at(("ca", l, m)))
                                f(mo[:, m, lo:T], o[:, lo:T], ACT.Sigmoid).then_inc(*act_drained.tick((name, l, m)))

            def mlstm(l):
                lo = low(l)
                for h in range(NH):
                    for s in range(NB):
                        a = max(lo, CTX if s >= 2 else 0)
                        o = full(("kq", l, h, s))
                        if h and s == 0:
                            act.wait_ge(*dve_done.at(("w", l, h - 1, 1, NB - 1)))
                        f(kq[:, s, a:T], o[:, a:T], ACT.Copy).then_inc(*act_drained.tick(("kq", l, h, s)))
                    for d in range(2):
                        col = 32 * d + h
                        if h:
                            act.wait_ge(*pe_done.at(("pv", l, h - 1, d)))
                        elif d == 0:
                            act.wait_ge(*dve_drained.at(("cols", l)))
                        for s in range(NB):
                            o = full(("dec", l, h, d, s))
                            for a, b in block_pairs(d, s, l):
                                ins = f(W[:, d, s, a * P:b * P], o[:, a * P:b * P], ACT.Exp,
                                        bias=cols[:, 0, s, col:col + 1])
                            ins.then_inc(*act_drained.tick(("dec", l, h, d, s)))
                act.wait_ge(*dve_done.at(("hvar", l)))
                g = (NB - lo // P) * NH
                f(stat[:, 2, 0:g], stat[:, 1, 0:g], ACT.Sqrt, scale=1.0 / DH, bias=eps).then_inc(*act_done.tick(("hstd", l)))

            def attention(l):
                lo = low(l)
                units = [(h, t) for h in range(NH) for t in range(lo // P, NB)]
                scale = DH ** -0.5
                for n in range(len(units) + 2):
                    if n < len(units):
                        h, t = units[n]
                        nk = CTX if t < 2 else T
                        if n == 0:
                            act.wait_ge(*pe_done.at(("pv", l, NH - 1, 1)))
                        if n >= 2:
                            act.wait_ge(*pe_done.at(("aT", l) + units[n - 2]))
                        for c in range(2):
                            o = full(("s", l, h, t, c))
                            act.wait_ge(*dve_done.at(("smax", l, h, t, c)))
                            f(prob[:, n % 2, c, 0:nk], o[:, 0:nk], ACT.Exp, scale=scale, bias=rs[:, n % 2, 2 + c:3 + c],
                              accum_out=rs[:, n % 2, 4 + c:5 + c]).then_inc(*act_drained.tick(("s", l, h, t, c)))
                    if 1 <= n <= len(units):
                        h, t = units[n - 1]
                        nk = CTX if t < 2 else T
                        o = full(("aT", l, h, t))
                        if n >= 3:
                            act.wait_ge(*pe_done.at(("o", l) + units[n - 3]))
                        f(probT[:, (n - 1) % 2, 0:nk // P, :], o[:, 0:nk].rearrange("p (b q) -> p b q", q=P), ACT.Copy)\
                            .then_inc(*act_drained.tick(("aT", l, h, t)))
                    if n >= 2:
                        h, t = units[n - 2]
                        o = full(("o", l, h, t))
                        f(mix[:, 2 + h, t * P:(t + 1) * P], o[:, 0:P], ACT.Copy).then_inc(*act_drained.tick(("o", l, h, t)))
                for h in range(NH):
                    act.wait_ge(*act_drained.at(("o", l, h, NB - 1)))
                    f(osq[:, h, lo:T], mix[:, 2 + h, lo:T], ACT.Square).then_inc(*act_done.tick(("osq", l, h)))
                for h in range(NH):
                    o = full(("osum", l, h))
                    if h:
                        act.wait_ge(*dve_done.at(("on", l, h - 1)))
                    f(rstd[:, lo:T], o[:, lo:T], ACT.Sqrt, scale=1.0 / DV, bias=eps)\
                        .then_inc(*act_drained.tick(("osum", l, h)))

            def conv_norm(l):
                lo = low(l)
                act.wait_ge(*dve_drained.at(("cmean", l)))
                f(kq[:, 0:2, lo:T], cy[:, :, lo:T], ACT.Square).then_inc(*act_done.tick(("csq", l)))
                o = full(("cvar", l))
                act.wait_ge(*dve_done.at(("on", l, NH - 1)))
                f(rstd[:, lo:T], o[:, lo:T], ACT.Sqrt, scale=1.0 / CW, bias=eps).then_inc(*act_drained.tick(("cvar", l)))
                act.wait_ge(*dve_done.at(("cn", l)))
                act.wait_ge(*pe_done.at(("hT", l, 1)))
                for m in range(2):
                    ins = f(mix[:, 6 + m, lo:T], cy[:, m, lo:T], ACT.Silu, scale=par("g_ln", l)[:, m:m + 1],
                            bias=par("b_ln", l)[:, m:m + 1])
                ins.then_inc(*act_done.tick(("mix_conv", l)))

            def dense():
                for i in range(FT):
                    o = full(("gate", i))
                    f(U[:, i, :], o, ACT.Silu).then_inc(*act_drained.tick(("gate", i)))

            def moe():
                def expert(e, first):
                    for t in range(ET):
                        act.wait_ge(gu_full, t + 1 if first else e * ET + (t + 1))
                        if t >= 4:
                            act.wait_ge(glu_done, t - 3 if first else e * ET + (t - 3))
                        elif not first:
                            last = max(x for x in range(ET) if x % 4 == t)
                            act.wait_ge(glu_done, e * ET + (last + 1 - ET))
                        f(esilu[:, t % 4, :], ps[:, t % 4, 0:SEQ], ACT.Silu).then_inc(silu_done, 1)

                expert(0, True)
                with act.Fori(1, NE) as e:
                    expert(e, False)

            act.wait_ge(sem_small, 16)
            f(cond[:, :, :], par("c").rearrange("p (k s) -> p k s", k=KD), ACT.Silu).then_inc(*act_done.tick("cond"))
            act.wait_ge(*dve_done.at("lamdot"))
            for l in range(DEPTH):
                ins = f(lam[:, l, 0:2], lam[:, l, 2:4], ACT.Exp)
            ins.then_inc(*act_done.tick("lamexp"))
            for l in range(DEPTH):
                norm(l, 0)
                project(l)
                mlstm(l)
                attention(l)
                conv_norm(l)
                norm(l, 1)
                if l == 0:
                    dense()
            act.wait_ge(*dve_drained.at("logits"))
            f(rt[:, 1], rt[:, 0], ACT.Exp).then_inc(*act_done.tick("router_exp"))
            moe()
            act.wait_ge(*dve_done.at("x_final"))
            act.wait_ge(down_done, NE * ET)
            f(experts[:, 0, 0:KD * SEQ].rearrange("p (k t) -> p k t", k=KD), X[:, :, CTX:T], ACT.Square)\
                .then_inc(*act_done.tick("final_sq"))
            act.wait_ge(*pe_done.at("final_ssq"))
            f(rstd[:, 0:SEQ], ps[:, 0, 0:SEQ], ACT.Sqrt, scale=1.0 / D, bias=eps).then_inc(*act_done.tick("final_std"))

        @block.vector
        def _(dve):
            v = nc.vector

            def full(key):
                dve.wait_ge(*pe_done.at(key))
                return ps[:, plan.get(("bank", key), 0), :]

            def settled(ins, key):
                ins.then_inc(*dve_done.tick(key))
                dve.wait_ge(*dve_done.at(key))

            def modulation(l):
                dve.wait_ge(*pe_done.at(("mod", l, MOD_CHUNKS - 1)))
                b = par("b_mod", l).unsqueeze(2).to_broadcast([P, 48, 2])
                settled(v.tensor_tensor(modc[:, l], ps[:, 7, 0:96].rearrange("p (m s) -> p m s", s=2), b, ALU.add),
                        ("modv", l))
                for which, g in ((0, "g1"), (1, "g2")):
                    at = 24 * which + KD
                    ins = v.scalar_tensor_tensor(gain[:, l, which], modc[:, l, at:at + KD, :], 1.0,
                                                 par(g, l).unsqueeze(2).to_broadcast([P, KD, 2]), ALU.add, ALU.mult)
                ins.then_inc(*dve_done.tick(("modc", l)))

            def norm(l, which):
                lo = low(l) if which else 0
                dve.wait_ge(*act_drained.at(("ssq", l, which)))
                settled(v.reciprocal(rstd[:, 0:T - lo], rstd[:, 0:T - lo]), ("rstd", l, which))
                dve.wait_ge(*pe_done.at(("ssq", l, which)))
                for k in range(KD):
                    v.tensor_tensor(sq[:, k, 0:T - lo], X[:, k, lo:T], rstd[:, 0:T - lo], ALU.mult)\
                        .then_inc(*dve_done.tick(("xn", l, which, k)))

            def gate_rows(l):
                R = GATE_ROWS
                settled(v.memset(scratch[0:64, 2 * T:8 * T], 0.0), ("clear", l))
                dve.wait_ge(*act_done.at(("gln", l)))
                settled(v.scalar_tensor_tensor(gate_ls[0:R, :], gate_raw[0:R, :], 0.0, gate_ls[0:R, :],
                                               ALU.min, ALU.subtract), ("logsig", l))
                v.tensor_copy(li[0:NH, :], gate_raw[0:NH, :])
                v.tensor_copy(lf[0:NH, :], gate_ls[32:32 + NH, :])
                for s in range(2):
                    seg = slice(s * SEQ, (s + 1) * SEQ)
                    v.tensor_copy(li[32:32 + NH, seg], gate_raw[64:64 + NH, seg][:, ::-1])
                    ins = v.tensor_copy(lf[32:32 + NH, seg], gate_ls[96:96 + NH, seg][:, ::-1])
                settled(ins, ("gates_seq", l))
                settled(v.tensor_tensor_scan(row_b, reset, lf, 0.0, ALU.mult, ALU.add), ("row_b", l))
                settled(v.tensor_tensor_scan(row_m, lf, li, NEG, ALU.add, ALU.max), ("row_m", l))
                v.tensor_tensor(row_a, li, row_b, ALU.subtract)
                for j in range(NB):
                    blk = slice(j * P, (j + 1) * P)
                    ins = v.tensor_tensor(row_r[:, j, blk], row_b[:, blk], row_m[:, blk], ALU.subtract)
                settled(ins, ("row_r", l))
                for j in reversed(range(NB - 1)):
                    later = slice((j + 1) * P, T)
                    settled(v.tensor_scalar(row_r[:, j, later], row_r[:, j + 1, later],
                                            row_b[:, (j + 1) * P - 1:(j + 1) * P], None, ALU.add), ("row_r", l, j))
                dve.wait_ge(*act_done.at(("row_em", l)))
                v.tensor_copy(rows_n[0:32, 0:4, :], row_r[0:32])
                v.tensor_copy(rows_n[0:32, 4:6, :], kq[0:32, 0:2, :])
                for s in range(2):
                    seg = slice(s * SEQ, (s + 1) * SEQ)
                    v.tensor_copy(rows_n[32:64, 0:4, seg], row_r[32:64, :, seg][:, :, ::-1])
                    ins = v.tensor_copy(rows_n[32:64, 4:6, seg], kq[32:64, 0:2, seg][:, :, ::-1])
                ins.then_inc(*dve_done.tick(("rows", l)))

            def rope(l, name):
                x = (ak if name[:2] == "ak" else aq)[:, 2 * int(name[-1]):2 * int(name[-1]) + 2, CTX:T]
                y = rstd[:, :].rearrange("p (m t) -> p m t", m=2)
                dve.wait_ge(*act_drained.at((name, l, 1)))
                if name == "ak0":
                    dve.wait_ge(*act_done.at(("h", l, 0)))
                settled(v.stream_shuffle(y, x, [i ^ 16 for i in range(32)]), ("partner", l, name))
                v.tensor_tensor(x, x, cos.unsqueeze(1).to_broadcast([P, 2, SEQ]), ALU.mult)
                settled(v.tensor_tensor(y, y, sin.unsqueeze(1).to_broadcast([P, 2, SEQ]), ALU.mult), ("ropesin", l, name))
                settled(v.tensor_tensor(x, x, y, ALU.add), ("rope", l, name))

            def project(l):
                gate_rows(l)
                for name in ("ak0", "ak1", "aq0", "aq1"):
                    rope(l, name)
                dve.wait_ge(*pool_done.at(("pads", l)))
                for m in range(2):
                    o = full(("ca", l, m))
                    dve.wait_ge(*act_drained.at(("cg", l, m)))
                    s = slice(low(l) // CTX, 2)
                    v.tensor_tensor(upad[:, m, s, PAD:PAD + SEQ], o.rearrange("p (s t) -> p s t", s=2)[:, s],
                                    mo[:, m, :].rearrange("p (s t) -> p s t", s=2)[:, s], ALU.mult)\
                        .then_inc(*dve_drained.tick(("ca", l, m)))

            def mlstm(l):
                t0 = low(l) // P
                o = full(("cols", l))
                v.tensor_copy(cols[:, :, :, :].rearrange("p a b r -> p (a b r)"), o).then_inc(*dve_drained.tick(("cols", l)))
                dve.wait_ge(*dve_drained.at(("cols", l)))

                def head_sums(h):
                    for d in range(2):
                        i, col = 2 * h + d, 32 * d + h
                        o = full(("pv", l, h, d)).rearrange("p (b c) -> p b c", b=NB)
                        settled(v.scalar_tensor_tensor(den[:, i, t0:NB], o[:, t0:NB, DH], -1.0, cols[:, 1, t0:NB, col],
                                                       ALU.mult, ALU.max), ("nden", l, h, d))
                        settled(v.tensor_tensor(den[:, i, t0:NB], o[:, t0:NB, DH], den[:, i, t0:NB], ALU.max),
                                ("den", l, h, d))
                        settled(v.reciprocal(den[:, i, t0:NB], den[:, i, t0:NB]), ("rden", l, h, d))
                        for t in range(t0, NB):
                            if d == 0:
                                ins = v.tensor_scalar(hsum[:, t, h, :], o[:, t, 0:DH], den[:, i, t:t + 1], None, ALU.mult)
                            else:
                                ins = v.scalar_tensor_tensor(hsum[:, t, h, :], o[:, t, 0:DH], den[:, i, t:t + 1],
                                                             hsum[:, t, h, :], ALU.mult, ALU.add)
                        ins.then_inc(*dve_drained.tick(("pv", l, h, d)))
                        dve.wait_ge(*dve_drained.at(("pv", l, h, d)))

                for h in range(NH):
                    for d in range(2):
                        for s in range(NB):
                            dve.wait_ge(*act_drained.at(("dec", l, h, d, s)))
                            for a, b in block_pairs(d, s, l):
                                w = W[:, d, s, a * P:b * P]
                                ins = v.tensor_tensor(w, w, kq[:, s, a * P:b * P], ALU.mult)
                            ins.then_inc(*dve_done.tick(("w", l, h, d, s)))
                    if h == 0:
                        dve.wait_ge(*pe_done.at(("mo", l, 1)))
                    head_sums(h)
                g = (NB - t0) * NH
                x = hsum.rearrange("p b h v -> p (b h) v")[:, t0 * NH:NB * NH, :]
                x2 = hsq.rearrange("p (g v) -> p g v", v=DH)[:, 0:g, :]

                def spread(i):
                    return stat[:, i, 0:g].unsqueeze(2).to_broadcast([P, g, DH])

                settled(v.tensor_reduce(stat[:, 0, 0:g], x, AX_X, ALU.add), ("hsum", l))
                settled(v.tensor_scalar(stat[:, 0, 0:g], stat[:, 0, 0:g], 1.0 / DH, None, ALU.mult), ("hmean", l))
                settled(v.tensor_tensor(x, x, spread(0), ALU.subtract), ("hcen", l))
                settled(v.tensor_tensor(x2, x, x, ALU.mult), ("hsq", l))
                settled(v.tensor_reduce(stat[:, 1, 0:g], x2, AX_X, ALU.add), ("hvar", l))
                dve.wait_ge(*act_done.at(("hstd", l)))
                settled(v.reciprocal(stat[:, 3, 0:g], stat[:, 2, 0:g]), ("hrstd", l))
                v.tensor_tensor(x, x, spread(3), ALU.mult).then_inc(*dve_done.tick(("hn", l)))
                lo = low(l)
                for m in range(2):
                    o = full(("hT", l, m))
                    dve.wait_ge(*act_drained.at(("mo", l, m)))
                    v.scalar_tensor_tensor(mix[:, m, lo:T], o[:, lo:T], par("g_mlstm", l)[:, m:m + 1], mo[:, m, lo:T],
                                           ALU.mult, ALU.mult).then_inc(*dve_drained.tick(("hT", l, m)))

            def attention(l):
                lo = low(l)
                units = [(h, t) for h in range(NH) for t in range(lo // P, NB)]

                def maxima(n):
                    h, t = units[n]
                    nk = CTX if t < 2 else T
                    u = n % 2
                    for c in range(2):
                        o = full(("s", l, h, t, c))
                        settled(v.tensor_reduce(rs[:, u, c:c + 1], o[:, 0:nk], AX_X, ALU.max), ("max", l, h, t, c))
                        v.tensor_scalar(rs[:, u, 2 + c:3 + c], rs[:, u, c:c + 1], -DH ** -0.5, None, ALU.mult)\
                            .then_inc(*dve_done.tick(("smax", l, h, t, c)))

                def combine(n):
                    h, t = units[n]
                    nk = CTX if t < 2 else T
                    u = n % 2
                    dve.wait_ge(*act_drained.at(("s", l, h, t, 1)))
                    settled(v.reciprocal(rs[:, u, 6:8], rs[:, u, 4:6]), ("rsum", l, h, t))
                    settled(v.tensor_tensor(rs[:, u, 8:9], rs[:, u, 7:8], nlam(l), ALU.mult), ("lsum", l, h, t))
                    p = prob[:, u]
                    settled(v.tensor_scalar(p[:, 1, 0:nk], p[:, 1, 0:nk], rs[:, u, 8:9], None, ALU.mult), ("p1", l, h, t))
                    v.scalar_tensor_tensor(p[:, 0, 0:nk], p[:, 0, 0:nk], rs[:, u, 6:7], p[:, 1, 0:nk],
                                           ALU.mult, ALU.add).then_inc(*dve_done.tick(("a", l, h, t)))

                for n in range(len(units) + 1):
                    if n < len(units):
                        maxima(n)
                    if n:
                        combine(n - 1)
                lam_init = 0.8 - 0.6 * math.exp(-0.3 * l)
                settled(v.tensor_scalar(stat[:, 0, 0:1], par("g_sub", l)[:, 0:1], 1.0 - lam_init, None, ALU.mult),
                        ("g_sub", l))
                for h in range(NH):
                    dve.wait_ge(*act_drained.at(("osum", l, h)))
                    settled(v.reciprocal(rstd[:, lo:T], rstd[:, lo:T]), ("orstd", l, h))
                    v.scalar_tensor_tensor(mix[:, 2 + h, lo:T], mix[:, 2 + h, lo:T], stat[:, 0, 0:1], rstd[:, lo:T],
                                           ALU.mult, ALU.mult).then_inc(*dve_done.tick(("on", l, h)))
                dve.wait_ge(*dve_done.at(("on", l, NH - 1)))
                v.tensor_copy(stat[:, 1, 0:1], stat[:, 0, 0:1]).then_inc(*dve_done.tick(("mix_attn", l)))

            def conv_norm(l):
                lo = low(l)
                o = full(("cmean", l))
                for m in range(2):
                    ins = v.scalar_tensor_tensor(cy[:, m, lo:T], o[:, lo:T], -1.0 / CW, cy[:, m, lo:T], ALU.mult, ALU.add)
                ins.then_inc(*dve_drained.tick(("cmean", l)))
                dve.wait_ge(*act_drained.at(("cvar", l)))
                settled(v.reciprocal(rstd[:, lo:T], rstd[:, lo:T]), ("crstd", l))
                for m in range(2):
                    ins = v.tensor_tensor(cy[:, m, lo:T], cy[:, m, lo:T], rstd[:, lo:T], ALU.mult)
                ins.then_inc(*dve_done.tick(("cn", l)))

            def residual(l, kind, gate, key):
                for m in range(KD):
                    o = full(key(m))
                    for s in range(low(l) // CTX, 2):
                        seg = slice(s * SEQ, (s + 1) * SEQ)
                        ins = v.scalar_tensor_tensor(X[:, m, seg], o[:, seg], modc[:, l, gate + m, s:s + 1], X[:, m, seg],
                                                     ALU.mult, ALU.add)
                    ins.then_inc(*dve_drained.tick(key(m)))

            def dense():
                for i in range(FT):
                    o = full(("up", i))
                    dve.wait_ge(*act_drained.at(("gate", i)))
                    v.tensor_tensor(U[:, i, :], U[:, i, :], o, ALU.mult).then_inc(*dve_drained.tick(("up", i)))

            def router():
                o = full("logits")[:, 0:2 * NE].rearrange("p (b e) -> p b e", b=2)

                def wide(t):
                    return t.unsqueeze(2).to_broadcast([P, 2, NE])

                ordb = order.unsqueeze(1).to_broadcast([P, 2, NE])
                settled(v.tensor_tensor(rt[:, 0], o, par("b_router").unsqueeze(1).to_broadcast([P, 2, NE]), ALU.add), "bias")
                settled(v.tensor_reduce(r1[:, 0], rt[:, 0], AX_X, ALU.max), "lmax")
                v.tensor_tensor(rt[:, 0], rt[:, 0], wide(r1[:, 0]), ALU.subtract).then_inc(*dve_drained.tick("logits"))
                dve.wait_ge(*act_done.at("router_exp"))
                settled(v.tensor_reduce(r1[:, 1], rt[:, 1], AX_X, ALU.add), "psum")
                settled(v.reciprocal(r1[:, 1], r1[:, 1]), "rpsum")
                settled(v.tensor_tensor(rt[:, 2], rt[:, 1], wide(r1[:, 1]), ALU.mult), "probs")
                for i in range(2):
                    settled(v.tensor_reduce(r1[:, 2 + i], rt[:, 2], AX_X, ALU.max), ("top", i))
                    settled(v.tensor_tensor(rt[:, 3], rt[:, 2], wide(r1[:, 2 + i]), ALU.is_ge), ("is_top", i))
                    settled(v.tensor_tensor(rt[:, 3], rt[:, 3], ordb, ALU.mult), ("rank", i))
                    settled(v.tensor_reduce(r1[:, 4], rt[:, 3], AX_X, ALU.max), ("first", i))
                    settled(v.tensor_tensor(rt[:, 4 + i], rt[:, 3], wide(r1[:, 4]), ALU.is_equal), ("chosen", i))
                    if i == 0:
                        settled(v.scalar_tensor_tensor(rt[:, 2], rt[:, 4], -2.0, rt[:, 2], ALU.mult, ALU.add), "out")
                settled(v.tensor_tensor(r1[:, 5], r1[:, 2], r1[:, 3], ALU.add), "topsum")
                settled(v.reciprocal(r1[:, 5], r1[:, 5]), "rtopsum")
                for i in range(2):
                    settled(v.tensor_tensor(r1[:, 6 + i], r1[:, 2 + i], r1[:, 5], ALU.mult), ("share", i))
                    settled(v.tensor_tensor(rt[:, 4 + i], rt[:, 4 + i], wide(r1[:, 6 + i]), ALU.mult), ("shares", i))
                settled(v.memset(rc, 0.0), "rc0")
                for i in range(2):
                    ins = v.tensor_tensor(rc[:, :, 32 * i:32 * i + 4], rt[:, 4, :, 4 * i:4 * i + 4],
                                          rt[:, 5, :, 4 * i:4 * i + 4], ALU.add)
                ins.then_inc(*dve_done.tick("combine"))
                o = full("combT")
                v.memset(zeros, 0.0)
                v.tensor_copy(combT, o[0:64, 0:SEQ]).then_inc(*dve_drained.tick("combT"))
                for e in range(0, NE, 2):
                    o = full(("comb", e))
                    v.tensor_copy(comb[:, e:e + 2, :], o.rearrange("p (e t) -> p e t", e=2))\
                        .then_inc(*dve_drained.tick(("comb", e)))
                dve.wait_ge(*dve_drained.at(("comb", NE - 2)))

            def moe():
                def expert(e, first):
                    def base(n):
                        return n if first else e * ET + n

                    for t in range(ET):
                        if t >= 4:
                            dve.wait_ge(down_done, base(t - 3))
                        elif not first:
                            last = max(x for x in range(ET) if x % 4 == t)
                            dve.wait_ge(down_done, e * ET + (last + 1 - ET))
                        dve.wait_ge(silu_done, base(t + 1))
                        v.tensor_tensor(ehid[:, t % 4, :], esilu[:, t % 4, :], ps[:, t % 4, SEQ:2 * SEQ], ALU.mult)\
                            .then_inc(glu_done, 1)
                        dve.wait_ge(glu_done, base(t + 1))
                        c = comb[:, 0, :] if first else comb[:, bass.ds(e, 1), :].rearrange("p a t -> p (a t)")
                        v.tensor_tensor(ehid[:, t % 4, :], ehid[:, t % 4, :], c, ALU.mult).then_inc(hidden_ready, 1)

                expert(0, True)
                with dve.Fori(1, NE) as e:
                    expert(e, False)
                dve.wait_ge(down_done, NE * ET)
                for m in range(KD):
                    ins = v.scalar_tensor_tensor(X[:, m, CTX:T], ps[:, 4 + m // 2, (m % 2) * SEQ:(m % 2 + 1) * SEQ],
                                                 modc[:, 1, 40 + m, 1:2], X[:, m, CTX:T], ALU.mult, ALU.add)
                settled(ins, "x_final")

            def nlam(l):
                return lam[:, l, 0:1]

            dve.wait_ge(sem_small, 16)
            q = par("lam").rearrange("p (l a d) -> p l a d", l=DEPTH, a=4)
            pr = lprod[:, 256:512].rearrange("p (a d) -> p a d", a=2 * DEPTH)
            for l in range(DEPTH):
                for i in range(2):
                    ins = v.tensor_tensor(pr[:, 2 * l + i], q[:, l, 2 * i], q[:, l, 2 * i + 1], ALU.mult)
            settled(ins, "lamprod")
            for l in range(DEPTH):
                ins = v.tensor_reduce(lam[:, l, 2:4], pr[:, 2 * l:2 * l + 2], AX_X, ALU.add)
            settled(ins, "lamdot")
            dve.wait_ge(*act_done.at("lamexp"))
            for l in range(DEPTH):
                lam_init = 0.8 - 0.6 * math.exp(-0.3 * l)
                settled(v.tensor_tensor(lam[:, l, 2:3], lam[:, l, 1:2], lam[:, l, 0:1], ALU.subtract), ("lamdiff", l))
                settled(v.tensor_scalar(lam[:, l, 0:1], lam[:, l, 2:3], -lam_init, None, ALU.add), ("nlam", l))
            for l in range(DEPTH):
                if l == 0:
                    modulation(0)
                norm(l, 0)
                project(l)
                mlstm(l)
                attention(l)
                conv_norm(l)
                if l == 0:
                    modulation(1)
                residual(l, "y", 16, lambda m: ("y", l, m))
                dve.wait_ge(*dve_drained.at(("y", l, KD - 1)))
                norm(l, 1)
                if l == 0:
                    dense()
                    residual(0, "ffn", 40, lambda m: ("ffn", m))
                    dve.wait_ge(*dve_drained.at(("ffn", KD - 1)))
            router()
            moe()
            dve.wait_ge(*act_done.at("final_std"))
            settled(v.reciprocal(rstd[:, 0:SEQ], rstd[:, 0:SEQ]), "final_rstd")
            for k in range(KD):
                ins = v.scalar_tensor_tensor(h2[:, k, :], X[:, k, CTX:T], par("g_final")[:, k:k + 1], rstd[:, 0:SEQ],
                                             ALU.mult, ALU.mult)
            ins.then_inc(*dve_done.tick("final"))

        @block.gpsimd
        def _(pool):
            g = nc.gpsimd
            for l in range(DEPTH):
                s0 = low(l) // CTX
                pool.wait_ge(*act_done.at(("h", l, 0)))
                g.memset(upad[:, :, :, 0:PAD], 0.0)
                g.memset(upad[:, :, :, PAD + SEQ:], 0.0)
                g.memset(vm[:, :, :, DH:DH + 1], 1.0).then_inc(*pool_done.tick(("pads", l)))
                for m in range(2):
                    pool.wait_ge(*dve_drained.at(("ca", l, m)))
                    w = par("w_dw", l).rearrange("p (m j) -> p m j", m=2)[:, m]
                    y = cy[:, m, :].rearrange("p (s t) -> p s t", s=2)[:, s0:2]
                    for j in range(TAPS):
                        u = upad[:, m, s0:2, j:j + SEQ]
                        if j:
                            pool.wait_ge(*pool_done.at(("tap", l, m, j - 1)))
                        if j == 0:
                            ins = g.tensor_scalar(y, u, w[:, 0:1], par("b_dw", l)[:, m:m + 1], ALU.mult, ALU.add)
                        else:
                            p = tap.rearrange("p (s t) -> p s t", s=2)[:, s0:2]
                            g.tensor_scalar(p, u, w[:, j:j + 1], None, ALU.mult)\
                             .then_inc(*pool_done.tick(("product", l, m, j)))
                            pool.wait_ge(*pool_done.at(("product", l, m, j)))
                            ins = g.tensor_tensor(y, y, p, ALU.add)
                        ins.then_inc(*pool_done.tick(("tap", l, m, j) if (m, j) != (1, TAPS - 1) else ("conv", l)))


def constants():
    con = np.zeros((P, NCONST), np.float32)

    def put(name, value):
        a, n = CONST[name]
        con[:value.shape[0], a:a + n] = value.reshape(value.shape[0], n)

    put("ident", np.eye(P, dtype=np.float32))
    put("ones", np.ones((P, P), np.float32))
    i = np.arange(P)
    put("mask_f", np.where(i[None, :] >= i[:, None], 0.0, NEG).astype(np.float32))
    put("mask_b", np.where(i[None, :] <= i[:, None], 0.0, NEG).astype(np.float32))
    axis, half, n = (i % 64) // 32, (i % 32) // 16, i % 16
    inv = (np.float32(10000.0) ** (-(2 * n).astype(np.float32) / np.float32(32))).astype(np.float32)
    t = np.arange(SEQ)
    pos = np.where(axis[:, None] == 0, (t // 64)[None, :], (t % 64)[None, :]).astype(np.float32)
    ang = pos * inv[:, None]
    put("cos", np.cos(ang).astype(np.float32))
    put("sin", (np.where(half[:, None] == 0, -1.0, 1.0) * np.sin(ang)).astype(np.float32))
    put("reset", np.broadcast_to((np.arange(T) % P != 0).astype(np.float32), (P, T)))
    pick = np.zeros((P, 2 * NH, P), np.float32)
    for r in range(2 * NH):
        pick[32 * (r // NH) + r % NH, r] = 1.0
    put("pick", pick)
    put("order", np.broadcast_to(np.arange(NE, 0, -1).astype(np.float32), (P, NE)))
    put("eps", np.full((P, 1), EPS, np.float32))
    put("one", np.ones((P, 1), np.float32))
    return con


def column_chunks(w, width):
    return w.reshape(KD, P, -1, width).transpose(2, 1, 0, 3).reshape(-1, P, KD * width)


def feature_major(v):
    v = v.reshape(v.shape[:-1] + (v.shape[-1] // P, P))
    return np.moveaxis(v, -1, 0).reshape(P, -1)


def lay_out(i):
    small = np.zeros((P, NSMALL), np.float32)

    def put(name, value):
        a, n = SMALL[name]
        small[:value.shape[0], a:a + n] = value.reshape(value.shape[0], n)

    put("c", np.stack([feature_major(i["c_ctx"]), feature_major(i["c"][0])], axis=-1))
    for name, src in (("b_mod", "b_mod"), ("g1", "g_norm1"), ("g2", "g_norm2"), ("g_mlstm", "g_mlstm"),
                      ("g_sub", "g_subln"), ("b_dw", "b_dw"), ("g_ln", "g_conv_ln"), ("b_ln", "b_conv_ln"),
                      ("g_final", "g_final")):
        put(name, feature_major(i[src]))
    bg = np.zeros((P, DEPTH), np.float32)
    gates = np.zeros((DEPTH, P, KD, GATE_ROWS), np.float32)
    for r in range(4):
        bg[32 * r:32 * r + NH] = i["b_gates"][:, NH * r:NH * (r + 1)].T
        cols = i["w_in"][:, :, GATE_COL + NH * r:GATE_COL + NH * (r + 1)]
        gates[:, :, :, 32 * r:32 * r + NH] = cols.reshape(DEPTH, KD, P, NH).transpose(0, 2, 1, 3)
    put("b_gates", bg)
    lam = np.stack([i["lambda_q1"], i["lambda_k1"], i["lambda_q2"], i["lambda_k2"]], axis=1)
    put("lam", np.broadcast_to(lam.reshape(1, -1), (P, lam.size)))
    put("w_dw", i["w_dw"].reshape(DEPTH, TAPS, 2, P).transpose(3, 0, 2, 1).reshape(P, -1))
    put("w_router", i["w_router"][0].reshape(KD, P, NE).transpose(1, 0, 2).reshape(P, -1))
    put("b_router", np.broadcast_to(i["b_router"][0], (P, NE)))
    x = np.concatenate([i["ctx"][0], i["x"][0]], axis=0)
    down = np.zeros((3 * KD * P, D), np.float32)
    down[:FF] = i["w_ffn_down"][0]
    exp_gu = [i[n][0].reshape(NE, KD, P, ET, P).transpose(0, 3, 2, 1, 4).reshape(NE, ET, P, KD * P)
              for n in ("w_exp_gate", "w_exp_up")]
    exp_dn = i["w_exp_down"][0].reshape(NE, ET, P, D)
    return {
        "con": constants(),
        "small": small,
        "x": x.T.reshape(KD, P, T).transpose(1, 0, 2).reshape(P, KD * T),
        "gates": gates.reshape(DEPTH, P, KD * GATE_ROWS),
        "mod": np.stack([column_chunks(w, CHUNK) for w in i["w_mod"]]),
        "in": np.stack([np.concatenate([column_chunks(w[:, IN_COL[n]:IN_COL[n] + CHUNK], CHUNK) for n in IN_ORDER])
                        for w in i["w_in"]]),
        "out": np.stack([column_chunks(w, CHUNK) for w in i["w_out"]]),
        "gate": column_chunks(i["w_ffn_gate"][0], CHUNK),
        "up": column_chunks(i["w_ffn_up"][0], CHUNK),
        "down": down.reshape(3, KD, P, D // CHUNK, CHUNK).transpose(3, 0, 2, 1, 4).reshape(D // CHUNK, 3, P, SLOT),
        "experts": np.concatenate(exp_gu + [exp_dn], axis=3),
    }


def kernel(**inputs):
    import concourse.bacc as _bacc
    from concourse.bass_utils import run_bass_kernel_spmd as _run

    arrays = {k: np.ascontiguousarray(v) for k, v in lay_out({k: np.asarray(v) for k, v in inputs.items()}).items()}
    plan = {}
    for complete in (False, True):
        nc = _bacc.Bacc("TRN2", target_bir_lowering=False, num_devices=1)
        A = {n: nc.dram_tensor(n, a.shape, F32, kind="ExternalInput").ap() for n, a in arrays.items()}
        A["out_0"] = nc.dram_tensor("out_0", (P, KD * SEQ), F32, kind="ExternalOutput").ap()
        plan["complete"] = complete
        build(nc, A, plan)
    r = _run(nc, [arrays], core_ids=[0])
    y = r.results[0]["out_0"].reshape(P, KD, SEQ)
    return y.transpose(2, 1, 0).reshape(1, SEQ, D)
```

```python
import math
from contextlib import ExitStack

import numpy as np
import concourse.bass as bass
from concourse import mybir

F32 = mybir.dt.float32
ALU = mybir.AluOpType
ACT = mybir.ActivationFunctionType
AX_X = mybir.AxisListType.X

P = 128
D = 1024
KD = D // P
SEQ = 256
CTX = 256
T = CTX + SEQ
NB = T // P
DEPTH = 2
NH = 4
DH = 64
DV = 128
MW = NH * DH
CW = 256
TAPS = 31
PAD = TAPS // 2
FF = 2816
FT = FF // P
NE = 8
FE = 1408
ET = FE // P
EPS = 1e-6
NEG = -1e30

CHUNK = 256
SLOT = KD * CHUNK
RING = 8
ESLOT = 3 * KD * P
NBANK = 7
MOD_CHUNKS = 6 * D // CHUNK
VCOLS = 96
VPAD = VCOLS - (DH + 1)
GATE_ROWS = 100

IN_ORDER = ["mk", "mq", "mv", "ak0", "ak1", "aq0", "aq1", "av0", "av1", "cg", "ca", "mo"]
IN_COL = {"mq": 0, "mk": 256, "mv": 512, "mo": 768, "aq0": 1040, "aq1": 1296, "ak0": 1552,
          "ak1": 1808, "av0": 2064, "av1": 2320, "ca": 2576, "cg": 2832}
GATE_COL = 1024


def fields(sizes):
    at, out = 0, {}
    for name, n in sizes:
        out[name] = (at, n)
        at += n
    return out, at


CONST, NCONST = fields([("ident", P), ("ones", P), ("mask_f", P), ("mask_b", P), ("cos", SEQ), ("sin", SEQ),
                        ("reset", T), ("pick", NH * 2 * P), ("before", P), ("slots", P), ("order", NE), ("eps", 1), ("one", 1)])
SMALL, NSMALL = fields([("c", 2 * KD), ("b_mod", DEPTH * 48), ("g1", DEPTH * KD), ("g2", DEPTH * KD),
                        ("b_gates", DEPTH), ("g_mlstm", DEPTH * 2), ("lam", DEPTH * 4 * DH), ("g_sub", DEPTH),
                        ("w_dw", DEPTH * 2 * TAPS), ("b_dw", DEPTH * 2), ("g_ln", DEPTH * 2), ("b_ln", DEPTH * 2),
                        ("g_final", KD), ("w_router", KD * NE), ("b_router", NE)])


def sequence_block(direction, block):
    return block if direction == 0 else [1, 0, 3, 2][block]


def block_pairs(direction, source, layer):
    low = 0 if layer < DEPTH - 1 else 2
    j = sequence_block(direction, source)
    targets = [t for t in range(low, NB) if sequence_block(direction, t) >= j]
    runs = []
    for t in targets:
        if runs and runs[-1][1] == t:
            runs[-1][1] = t + 1
        else:
            runs.append([t, t + 1])
    return runs


class Signal:

    def __init__(self, plan, handle, name):
        self.plan, self.handle, self.name, self.count = plan, handle, name, 0

    def tick(self, key):
        self.count += 1
        self.plan[self.name, key] = self.count
        return self.handle, 1

    def at(self, key):
        return self.handle, self.plan[self.name, key] if self.plan.get("complete") else 1


def build(nc, A, plan):
    with ExitStack() as ctx:
        def sb(name, shape):
            return ctx.enter_context(nc.sbuf_tensor("sb_" + name, shape, F32))

        def signal(name):
            return Signal(plan, ctx.enter_context(nc.semaphore(name)), name)

        def semaphore(name):
            return ctx.enter_context(nc.semaphore(name))

        X = sb("X", [P, KD, T])
        H = sb("H", [P, KD * T])
        arena = sb("arena", [P, ET * ESLOT])
        con = sb("con", [P, NCONST])
        small = sb("small", [P, NSMALL])
        rstd = sb("rstd", [P, T])
        modc = sb("modc", [P, DEPTH, 48, 2])
        gain = sb("gain", [P, DEPTH, 2, KD, 2])
        cond = sb("cond", [P, KD, 2])
        kq = sb("kq", [P, NB, T])
        rows_n = sb("rows_n", [P, 6, T])
        cols = sb("cols", [P, 2, NB, 64])
        tiny = sb("tiny", [P, 512])
        ps = ctx.enter_context(nc.psum_tensor("ps", [P, 8, 512], F32))

        hT = H[:, :].rearrange("p (k t) -> p k t", k=KD)
        mix = hT
        hsum = H[:, 6 * T:8 * T].rearrange("p (b h v) -> p b h v", b=NB, h=NH)
        h2 = H[:, 0:KD * SEQ].rearrange("p (k t) -> p k t", k=KD)
        comb = H[:, KD * SEQ:2 * KD * SEQ].rearrange("p (e t) -> p e t", e=NE)
        ring = arena[:, 0:RING * SLOT].rearrange("p (s n) -> p s n", s=RING)
        experts = arena[:, :].rearrange("p (f n) -> p f n", f=ET)
        work = arena[:, RING * SLOT:ET * ESLOT]
        sq = work[:, 0:KD * T].rearrange("p (k t) -> p k t", k=KD)
        U = work[:, 0:FT * T].rearrange("p (f t) -> p f t", f=FT)
        top = [0]

        def take(n):
            top[0] += n
            return work[:, top[0] - n:top[0]]

        mq = take(2 * T).rearrange("p (m t) -> p m t", m=2)
        mk = take(2 * T).rearrange("p (m t) -> p m t", m=2)
        mo = take(2 * T).rearrange("p (m t) -> p m t", m=2)
        aq = take(4 * T).rearrange("p (m t) -> p m t", m=4)
        ak = take(4 * T).rearrange("p (m t) -> p m t", m=4)
        vm_all = take(NB * NH * (DH + 1) + VPAD)
        vm = vm_all[:, 0:NB * NH * (DH + 1)].rearrange("p (b h v) -> p b h v", b=NB, h=NH)
        va = take(NB * NH * DV).rearrange("p (b n) -> p b n", b=NB)
        upad = take(2 * 2 * (SEQ + 2 * PAD)).rearrange("p (m s t) -> p m s t", m=2, s=2)
        assert top[0] >= FT * T
        cy = take(2 * T)
        w_gates = cy[:, 0:KD * GATE_ROWS].rearrange("p (k n) -> p k n", k=KD)
        cy = cy.rearrange("p (m t) -> p m t", m=2)
        tap = take(T)
        scratch = take(2 * NB * T)
        gate_raw = scratch[:, 0:T]
        gate_ls = scratch[:, T:2 * T]
        li = scratch[0:64, 2 * T:3 * T]
        lf = scratch[0:64, 3 * T:4 * T]
        row_r = scratch[0:64, 4 * T:8 * T].rearrange("p (j t) -> p j t", j=NB)
        row_a, row_em = kq[0:64, 0, :], kq[0:64, 1, :]
        row_b, row_m = kq[0:64, 2, :], kq[0:64, 3, :]
        W = scratch.rearrange("p (u b t) -> p u b t", u=2, b=NB)
        prob = scratch[:, 0:4 * T].rearrange("p (u c t) -> p u c t", u=2, c=2)
        probT = scratch[:, 4 * T:6 * T].rearrange("p (u b q) -> p u b q", u=2, b=NB)
        osq = scratch[:, 0:4 * T].rearrange("p (h t) -> p h t", h=NH)
        hsq = kq[:, 0:2, :].rearrange("p a t -> p (a t)")
        modrow = rows_n[64:66, :, :].rearrange("p a t -> p (a t)").rearrange("p (u n) -> p u n", n=CHUNK)
        ehid = rows_n[:, 0, :].rearrange("p (u t) -> p u t", u=4)
        esilu = rows_n[:, 1, :].rearrange("p (u t) -> p u t", u=4)
        h_tok = H[:, KD * SEQ:2 * KD * SEQ].rearrange("p (b n) -> p b n", b=2)
        h_slot = H[:, 0:KD * P].rearrange("p (k n) -> p k n", k=KD)
        y_slot = H[:, KD * P:2 * KD * P]
        to_slot = kq[:, 0, 0:2 * P].rearrange("p (b n) -> p b n", b=2)
        shares = kq[:, 1, 0:2 * P].rearrange("p (b n) -> p b n", b=2)
        from_slot = kq[:, 2, 0:2 * P]
        PASSES = SEQ // P

        def field(t, table, name):
            a, n = table[name]
            return t[:, a:a + n]

        def par(name, l=None):
            t = field(small, SMALL, name)
            return t if l is None else t.rearrange("p (l n) -> p l n", l=DEPTH)[:, l]

        ident, ones = field(con, CONST, "ident"), field(con, CONST, "ones")
        mask = [field(con, CONST, "mask_f"), field(con, CONST, "mask_b")]
        cos, sin = field(con, CONST, "cos"), field(con, CONST, "sin")
        reset = field(con, CONST, "reset")[0:64, :]
        pick = field(con, CONST, "pick").rearrange("p (i n) -> p i n", i=2 * NH)[0:64]
        order = field(con, CONST, "order")
        eps, one = field(con, CONST, "eps"), field(con, CONST, "one")
        lam = tiny[:, 0:8].rearrange("p (l n) -> p l n", l=DEPTH)
        rs = tiny[:, 8:32].rearrange("p (u n) -> p u n", u=2)
        den = tiny[:, 32:64].rearrange("p (a b) -> p a b", a=2 * NH)
        stat = tiny[:, 64:128].rearrange("p (a n) -> p a n", a=4)
        rt = tiny[:, 128:256].rearrange("p (a b e) -> p a b e", a=8, b=2)
        slot_no = tiny[:, 256:256 + 2 * (PASSES * NE + 1)].rearrange("p (i b) -> p i b", b=2)
        share = tiny[:, 300:300 + 2 * (PASSES * NE + 1)].rearrange("p (i b) -> p i b", b=2)
        trips = tiny[:, 344:345].bitcast(mybir.dt.int32)
        r1 = tiny[:, 384:400].rearrange("p (a b) -> p a b", a=8)
        lprod = tiny[:, 0:512]

        sem_small = semaphore("parameters_loaded")
        sem_con = semaphore("constants_loaded")
        sem_x = semaphore("tokens_loaded")
        sem_gw = [semaphore(f"gate_weights_loaded_{l}") for l in range(DEPTH)]
        sem_slot = [semaphore(f"ring_slot_loaded_{s}") for s in range(RING)]
        sem_exp = [semaphore(f"expert_tile_loaded_{f}") for f in range(ET)]
        sem_out = semaphore("output_stored")
        pe_done = signal("pe_done")
        act_drained = signal("act_drained")
        dve_drained = signal("dve_drained")
        act_done = signal("act_done")
        dve_done = signal("dve_done")
        pool_done = signal("pool_done")
        gu_full = semaphore("gate_up_full")
        silu_done = semaphore("silu_done")
        glu_done = semaphore("glu_done")
        down_done = semaphore("down_done")
        slots_built = semaphore("slots_built")
        gathered = semaphore("gathered")
        h_act = semaphore("h_slot_act")
        h_dve = semaphore("h_slot_dve")
        shares_built = semaphore("shares_built")
        shares_turned = semaphore("shares_turned")
        from_slot_ready = semaphore("from_slot_ready")
        y_act = semaphore("y_slot_act")
        y_dve = semaphore("y_slot_dve")
        scattered = semaphore("scattered")
        x_added = semaphore("x_added")

        block = ctx.enter_context(nc.Block())

        chunks = [("mod", 0, i) for i in range(MOD_CHUNKS)]
        for l in range(DEPTH):
            chunks += [("in", l, n) for n in IN_ORDER]
            if l == 0:
                chunks += [("mod", 1, i) for i in range(MOD_CHUNKS)]
            chunks += [("out", l, i) for i in range(D // CHUNK)]
            if l == 0:
                chunks += [(k, 0, i) for i in range(FF // CHUNK) for k in ("gate", "up")]
                chunks += [("down", 0, (i, j)) for i in range(D // CHUNK) for j in range(3)]
        slot_of = {c: n for n, c in enumerate(chunks)}

        def last_product(chunk):
            kind, l, i = chunk
            if kind == "in":
                return (i, l, NB - 1) if i in ("mv", "av0", "av1") else (i, l, 1)
            if kind == "out":
                return ("y", l, 2 * i + 1)
            if kind == "down":
                return chunk if i[1] < 2 else ("ffn", 2 * i[0] + 1)
            return (kind, 2 * i + 1) if kind in ("gate", "up") else chunk

        def low(l):
            return 0 if l < DEPTH - 1 else CTX

        @block.sync
        def _(sp):
            sp.dma_start(small[:, :], A["small"]).then_inc(sem_small, 16)
            for n, (kind, l, i) in enumerate(chunks):
                if n == 4:
                    sp.dma_start(con[:, :], A["con"]).then_inc(sem_con, 16)
                    sp.dma_start(X[:, :, :], A["x"].rearrange("p (k t) -> p k t", k=KD)).then_inc(sem_x, 16)
                if kind == "in" and i == IN_ORDER[0]:
                    if l > 0:
                        sp.wait_ge(*pe_done.at(("cvar", l - 1)))
                        sp.wait_ge(*dve_done.at(("cn", l - 1)))
                        sp.wait_ge(*act_done.at(("mix_conv", l - 1)))
                    sp.dma_start(w_gates, A["gates"][l].rearrange("p (k n) -> p k n", k=KD)).then_inc(sem_gw[l], 16)
                if n >= RING:
                    sp.wait_ge(*pe_done.at(last_product(chunks[n - RING])))
                width = SLOT
                if kind == "mod":
                    src = A["mod"][l, i]
                elif kind == "in":
                    src = A["in"][l, IN_ORDER.index(i)]
                elif kind == "out":
                    src = A["out"][l, i]
                elif kind in ("gate", "up"):
                    src = A[kind][i]
                else:
                    src = A["down"][i[0], i[1]]
                    width = min(KD, FT - KD * i[1]) * CHUNK
                sp.dma_start(ring[:, n % RING, 0:width], src[:, 0:width]).then_inc(sem_slot[n % RING], 16)

            sp.wait_ge(*act_done.at(("h", 1, 1)))
            for f in range(ET):
                sp.dma_start(experts[:, f, :], A["experts"][0, f]).then_inc(sem_exp[f], 16)
            sp.wait_ge(*dve_done.at("trips"))
            n = sp.value_load(trips[0:1, :], min_val=NE, max_val=PASSES * NE)
            with sp.Fori(1, n) as i:
                e = sp.snap(sp.to_reg(i & (NE - 1)), min_val=0, max_val=NE - 1)
                for f in range(ET):
                    sp.wait_ge(down_done, i * ET + (f + 1))
                    sp.dma_start(experts[:, f, :], A["experts"][bass.ds(e, 1), f].rearrange("a p n -> (a p) n"))\
                      .then_inc(sem_exp[f], 16)
            sp.wait_ge(*dve_done.at("final"))
            sp.dma_start(A["out_0"].rearrange("p (k t) -> p k t", k=KD), h2).then_inc(sem_out, 16)
            sp.wait_ge(sem_out, 16)

        @block.tensor
        def _(pe):
            opened = []

            def open_bank(key):
                n = len(opened)
                if n >= NBANK:
                    last = opened[n - NBANK]
                    drainer = act_drained if ("act_drained", last) in plan else dve_drained
                    pe.wait_ge(*drainer.at(last))
                opened.append(key)
                plan["bank", key] = n % NBANK
                return ps[:, n % NBANK, :]

            def loaded(chunk):
                n = slot_of[chunk]
                pe.wait_ge(sem_slot[n % RING], 16 * (n // RING + 1))
                return ring[:, n % RING, :].rearrange("p (k n) -> p k n", k=KD)

            def modulation(l, i):
                w = loaded(("mod", l, i))
                if i == 0 and l == 0:
                    pe.wait_ge(*act_done.at("cond"))
                o = open_bank(("mod", l, i))
                for k in range(KD):
                    ins = pe.matmul(o[0:2, 0:CHUNK], cond[:, k, :], w[:, k, :], start=(k == 0), stop=(k == KD - 1))
                ins.then_inc(*pe_done.tick(("mod", l, i)))
                if i:
                    turn_modulation(l, i - 1)
                if i == MOD_CHUNKS - 1:
                    turn_modulation(l, i)

            def turn_modulation(l, i):
                pe.wait_ge(*act_drained.at(("mod", l, i)))
                if i == 0 and l > 0:
                    pe.wait_ge(*dve_done.at(("modc", l - 1)))
                if i == 0 and l == 0:
                    pe.wait_ge(sem_con, 16)
                for m in range(2):
                    at = 2 * (2 * i + m)
                    ins = pe.transpose(ps[:, 7, at:at + 2], modrow[:, i % 12, m * P:(m + 1) * P], ident[64:66, 64:66])
                ins.then_inc(*pe_done.tick(("modT", l, i)))

            def norm(l, which):
                lo = low(l) if which else 0
                if l == 0:
                    pe.wait_ge(sem_con, 16)
                for half in range(2):
                    pe.wait_ge(*act_done.at(("sq", l, which, half)))
                    if half == 0:
                        o = open_bank(("ssq", l, which))
                    for k in range(4 * half, 4 * half + 4):
                        ins = pe.matmul(o[:, 0:T - lo], ones, sq[:, k, 0:T - lo], start=(k == 0), stop=(k == KD - 1))
                ins.then_inc(*pe_done.tick(("ssq", l, which)))

            def project(l):
                pe.wait_ge(*act_done.at(("h", l, 0)))
                pe.wait_ge(sem_gw[l], 16)
                o = open_bank(("gates", l))
                for k in range(KD):
                    ins = pe.matmul(o[0:GATE_ROWS, :], w_gates[:, k, :], hT[:, k, :], start=(k == 0), stop=(k == KD - 1))
                ins.then_inc(*pe_done.tick(("gates", l)))
                for name in IN_ORDER:
                    w = loaded(("in", l, name))
                    if name in ("mv", "av0", "av1"):
                        for b in range(NB):
                            o = open_bank((name, l, b))
                            for k in range(KD):
                                ins = pe.matmul(o[:, 0:CHUNK], hT[:, k, b * P:(b + 1) * P], w[:, k, :],
                                                start=(k == 0), stop=(k == KD - 1))
                            ins.then_inc(*pe_done.tick((name, l, b)))
                    else:
                        a = 0 if name in ("mk", "ak0", "ak1") else low(l)
                        for m in range(2):
                            o = open_bank((name, l, m))
                            for k in range(KD):
                                ins = pe.matmul(o[:, a:T], w[:, k, m * P:(m + 1) * P], hT[:, k, a:T],
                                                start=(k == 0), stop=(k == KD - 1))
                            ins.then_inc(*pe_done.tick((name, l, m)))

            filler = {0: [(1, i) for i in range(MOD_CHUNKS)], 1: []}

            def fill(l, n):
                for _ in range(n):
                    if filler[l]:
                        modulation(*filler[l].pop(0))

            def mlstm(l):
                pe.wait_ge(*dve_done.at(("rows", l)))
                o = open_bank(("cols", l)).rearrange("p (a b r) -> p a b r", a=2, b=NB)
                for a in range(2):
                    for b in range(NB):
                        ins = pe.transpose(o[:, a, b, :], rows_n[0:64, 4 + a, b * P:(b + 1) * P], ident[0:64, 0:64])
                ins.then_inc(*pe_done.tick(("cols", l)))

                def products(h):
                    r0, m = DH * (h % 2), h // 2
                    for s in range(NB):
                        a = max(low(l), CTX if s >= 2 else 0)
                        o = open_bank(("kq", l, h, s))
                        pe.matmul(o[:, a:T], mk[r0:r0 + DH, m, s * P:(s + 1) * P], mq[r0:r0 + DH, m, a:T],
                                  start=True, stop=True).then_inc(*pe_done.tick(("kq", l, h, s)))
                    for d in range(2):
                        row = d * NH + h
                        for s in range(NB):
                            j = sequence_block(d, s)
                            o = open_bank(("dec", l, h, d, s))
                            for a, b in block_pairs(d, s, l):
                                spans = [(a, b)]
                                if a <= s < b:
                                    spans = [(x, y) for x, y in ((a, s), (s + 1, b)) if y > x]
                                    pe.matmul(o[:, s * P:(s + 1) * P], pick[:, row, :],
                                              rows_n[0:64, j, s * P:(s + 1) * P], start=True, stop=False)
                                    ins = pe.matmul(o[:, s * P:(s + 1) * P], ident, mask[d], start=False, stop=True)
                                for x, y in spans:
                                    ins = pe.matmul(o[:, x * P:y * P], pick[:, row, :],
                                                    rows_n[0:64, j, x * P:y * P], start=True, stop=True)
                            ins.then_inc(*pe_done.tick(("dec", l, h, d, s)))

                def sums(h):
                    for d in range(2):
                        pe.wait_ge(*dve_done.at(("w", l, h, d, NB - 1)))
                        o = open_bank(("pv", l, h, d)).rearrange("p (b c) -> p b c", b=NB)
                        for t in range(low(l) // P, NB):
                            src = [s for s in range(NB) if sequence_block(d, s) <= sequence_block(d, t)]
                            for s in src:
                                at = (s * NH + h) * (DH + 1)
                                ins = pe.matmul(o[:, t, 0:VCOLS], W[:, d, s, t * P:(t + 1) * P], vm_all[:, at:at + VCOLS],
                                                start=(s == src[0]), stop=(s == src[-1]))
                        ins.then_inc(*pe_done.tick(("pv", l, h, d)))

                pe.wait_ge(*act_drained.at(("mq", l, 1)))
                for h in range(NH):
                    products(h)
                    fill(l, 2)
                    if h == 0:
                        pe.wait_ge(*act_drained.at(("mv", l, NB - 1)))
                        pe.wait_ge(*pool_done.at(("pads", l)))
                    sums(h)
                pe.wait_ge(*dve_done.at(("hn", l)))
                for m in range(2):
                    o = open_bank(("hT", l, m))
                    for b in range(low(l) // P, NB):
                        ins = pe.transpose(o[:, b * P:(b + 1) * P],
                                           hsum[:, b, 2 * m:2 * m + 2, :].rearrange("p h v -> p (h v)"), ident)
                    ins.then_inc(*pe_done.tick(("hT", l, m)))

            def attention(l):
                units = [(h, t) for h in range(NH) for t in range(low(l) // P, NB)]

                def scores(n):
                    h, t = units[n]
                    nk = CTX if t < 2 else T
                    for c in range(2):
                        o = open_bank(("s", l, h, t, c))
                        pe.matmul(o[:, 0:nk], aq[c * DH:(c + 1) * DH, h, t * P:(t + 1) * P],
                                  ak[c * DH:(c + 1) * DH, h, 0:nk], start=True, stop=True)\
                          .then_inc(*pe_done.tick(("s", l, h, t, c)))

                def turn(n):
                    h, t = units[n]
                    nk = CTX if t < 2 else T
                    pe.wait_ge(*dve_done.at(("a", l, h, t)))
                    o = open_bank(("aT", l, h, t))
                    for b in range(nk // P):
                        ins = pe.transpose(o[:, b * P:(b + 1) * P], prob[:, n % 2, 0, b * P:(b + 1) * P], ident)
                    ins.then_inc(*pe_done.tick(("aT", l, h, t)))

                def values(n):
                    h, t = units[n]
                    nb = 2 if t < 2 else NB
                    pe.wait_ge(*act_drained.at(("aT", l, h, t)))
                    o = open_bank(("o", l, h, t))
                    for b in range(nb):
                        ins = pe.matmul(o[:, 0:P], va[:, b, h * DV:(h + 1) * DV], probT[:, n % 2, b, :],
                                        start=(b == 0), stop=(b == nb - 1))
                    ins.then_inc(*pe_done.tick(("o", l, h, t)))

                pe.wait_ge(*dve_done.at(("rope", l, "aq1")))
                pe.wait_ge(*act_drained.at(("av1", l, NB - 1)))
                for n in range(len(units) + 2):
                    if n < len(units):
                        scores(n)
                    fill(l, 1)
                    if 1 <= n <= len(units):
                        turn(n - 1)
                    if n >= 2:
                        values(n - 2)
                fill(l, MOD_CHUNKS)
                lo = low(l)
                for h in range(NH):
                    pe.wait_ge(*act_done.at(("osq", l, h)))
                    o = open_bank(("osum", l, h))
                    pe.matmul(o[:, lo:T], ones, osq[:, h, lo:T], start=True, stop=True)\
                      .then_inc(*pe_done.tick(("osum", l, h)))

            def conv_norm(l):
                lo = low(l)
                pe.wait_ge(*pool_done.at(("conv", l)))
                o = open_bank(("cmean", l))
                for m in range(2):
                    ins = pe.matmul(o[:, lo:T], ones, cy[:, m, lo:T], start=(m == 0), stop=(m == 1))
                ins.then_inc(*pe_done.tick(("cmean", l)))
                pe.wait_ge(*act_done.at(("csq", l)))
                o = open_bank(("cvar", l))
                for m in range(2):
                    ins = pe.matmul(o[:, lo:T], ones, kq[:, m, lo:T], start=(m == 0), stop=(m == 1))
                ins.then_inc(*pe_done.tick(("cvar", l)))

            def output(l):
                lo = low(l)
                pe.wait_ge(*act_done.at(("mix_conv", l)))
                pe.wait_ge(*dve_done.at(("mix_attn", l)))
                pe.wait_ge(*dve_drained.at(("hT", l, 1)))
                for i in range(D // CHUNK):
                    w = loaded(("out", l, i))
                    for m in range(2):
                        o = open_bank(("y", l, 2 * i + m))
                        for k in range(KD):
                            ins = pe.matmul(o[:, lo:T], w[:, k, m * P:(m + 1) * P], mix[:, k, lo:T],
                                            start=(k == 0), stop=(k == KD - 1))
                        ins.then_inc(*pe_done.tick(("y", l, 2 * i + m)))

            def dense():
                pe.wait_ge(*act_done.at(("h", 0, 1)))
                for i in range(FF // CHUNK):
                    w = {k: loaded((k, 0, i)) for k in ("gate", "up")}
                    for m in range(2):
                        for kind in ("gate", "up"):
                            o = open_bank((kind, 2 * i + m))
                            for k in range(KD):
                                ins = pe.matmul(o, w[kind][:, k, m * P:(m + 1) * P], hT[:, k, :],
                                                start=(k == 0), stop=(k == KD - 1))
                            ins.then_inc(*pe_done.tick((kind, 2 * i + m)))
                pe.wait_ge(*dve_drained.at(("up", FT - 1)))
                for i in range(D // CHUNK):
                    o = [open_bank(("ffn", 2 * i + m)) for m in range(2)]
                    for j in range(3):
                        w = loaded(("down", 0, (i, j)))
                        for m in range(2):
                            for k in range(KD * j, min(FT, KD * j + KD)):
                                ins = pe.matmul(o[m], w[:, k - KD * j, m * P:(m + 1) * P], U[:, k, :],
                                                start=(k == 0), stop=(k == FT - 1))
                            if j == 2 and m == 0:
                                ins.then_inc(*pe_done.tick(("ffn", 2 * i)))
                        if j < 2:
                            ins.then_inc(*pe_done.tick(("down", 0, (i, j))))
                    ins.then_inc(*pe_done.tick(("ffn", 2 * i + 1)))

            def router():
                pe.wait_ge(*act_done.at(("h", 1, 1)))
                o = open_bank("logits")
                w = par("w_router").rearrange("p (k e) -> p k e", k=KD)
                for b in range(2):
                    for k in range(KD):
                        ins = pe.matmul(o[:, b * NE:(b + 1) * NE], h2[:, k, b * P:(b + 1) * P], w[:, k, :],
                                        start=(k == 0), stop=(k == KD - 1))
                ins.then_inc(*pe_done.tick("logits"))
                for k in range(KD):
                    o = open_bank(("h_tok", k))
                    for b in range(2):
                        ins = pe.transpose(o[:, b * P:(b + 1) * P], h2[:, k, b * P:(b + 1) * P], ident)
                    ins.then_inc(*pe_done.tick(("h_tok", k)))
                pe.wait_ge(*dve_done.at("chosen"))
                o = open_bank("rank")
                before = field(con, CONST, "before")
                pe.matmul(o[:, 0:NE], before, rt[:, 6, 0], start=True, stop=True)
                pe.matmul(o[:, NE:2 * NE], before, rt[:, 6, 1], start=True, stop=False)
                pe.matmul(o[:, NE:2 * NE], ones, rt[:, 6, 0], start=False, stop=True)
                for b in range(2):
                    ins = pe.matmul(o[:, 2 * NE:3 * NE], ones, rt[:, 6, b], start=(b == 0), stop=(b == 1))
                ins.then_inc(*pe_done.tick("rank"))

            def moe():
                pe.wait_ge(*dve_done.at("moe_start"))
                pe.wait_ge(*act_drained.at(("h_tok", KD - 1)))
                n = pe.value_load(trips[0:1, :], min_val=NE, max_val=PASSES * NE)
                pe.sem_inc(down_done, ET)
                pe.sem_inc(shares_turned, 1)

                def gather(count):
                    pe.wait_ge(slots_built, count)
                    for k in range(KD):
                        for b in range(2):
                            ins = pe.matmul(ps[:, 4 + k // 4, (k % 4) * P:(k % 4 + 1) * P], h_tok[:, b, k * P:(k + 1) * P],
                                            to_slot[:, b, :], start=(b == 0), stop=(b == 1))
                    ins.then_inc(gathered, 1)

                def scatter(i):
                    pe.wait_ge(from_slot_ready, i + 1)
                    for q in range(4):
                        pe.wait_ge(x_added, i * 4 + (q + 1))
                        for m in range(2):
                            ins = pe.matmul(ps[:, 6 + q % 2, m * SEQ:(m + 1) * SEQ], y_slot[:, (2 * q + m) * P:(2 * q + m + 1) * P],
                                            from_slot, start=True, stop=True)
                        ins.then_inc(scattered, 1)

                gather(1)
                with pe.Fori(0, n) as i:
                    def down(f):
                        pe.wait_ge(glu_done, i * ET + (ET + f + 1))
                        if f == 0:
                            pe.wait_ge(y_act, i + 1)
                            pe.wait_ge(y_dve, i + 1)
                        for m in range(2):
                            at = 2 * KD * P + m * 512
                            ins = pe.matmul(ps[:, m, :], ehid[:, f % 4, :], experts[:, f, at:at + 512],
                                            start=(f == 0), stop=(f == ET - 1))
                        ins.then_inc(down_done, 1)

                    for f in range(ET):
                        pe.wait_ge(sem_exp[f], i * 16 + 16)
                        if f == 0:
                            pe.wait_ge(h_act, i + 1)
                            pe.wait_ge(h_dve, i + 1)
                        last = f - 2 + ET if f >= 2 else max(x for x in range(ET) if x % 2 == f)
                        pe.wait_ge(glu_done, i * ET + (last + 1))
                        for a in range(2):
                            w = experts[:, f, a * KD * P:(a + 1) * KD * P].rearrange("p (k n) -> p k n", k=KD)
                            for k in range(KD):
                                ins = pe.matmul(ps[:, 2 + f % 2, a * P:(a + 1) * P], w[:, k, :], h_slot[:, k, :],
                                                start=(k == 0), stop=(k == KD - 1))
                        ins.then_inc(gu_full, 1)
                        if f:
                            down(f - 1)
                        if f == 2:
                            scatter(i)
                        if f == 5:
                            pe.wait_ge(shares_built, i + 1)
                            for b in range(2):
                                ins = pe.transpose(ps[:, 4, b * P:(b + 1) * P], shares[:, b, :], ident)
                            ins.then_inc(shares_turned, 1)
                    pe.wait_ge(from_slot_ready, i + 2)
                    gather(i + 2)
                    down(ET - 1)
                pe.wait_ge(y_act, n + 1)
                pe.wait_ge(y_dve, n + 1)
                scatter(n)

            for i in range(MOD_CHUNKS):
                modulation(0, i)
            for l in range(DEPTH):
                norm(l, 0)
                project(l)
                mlstm(l)
                attention(l)
                conv_norm(l)
                output(l)
                norm(l, 1)
                if l == 0:
                    dense()
            router()
            moe()
            pe.wait_ge(*act_done.at("final_sq"))
            for k in range(KD):
                ins = pe.matmul(ps[:, 0, 0:SEQ], ones, experts[:, 0, k * SEQ:(k + 1) * SEQ],
                                start=(k == 0), stop=(k == KD - 1))
            ins.then_inc(*pe_done.tick("final_ssq"))

        @block.scalar
        def _(act):
            f = nc.scalar.activation

            def full(key):
                act.wait_ge(*pe_done.at(key))
                return ps[:, plan.get(("bank", key), 0), :]

            def norm(l, which):
                lo = low(l) if which else 0
                if which == 1:
                    act.wait_ge(*dve_drained.at(("y", l, KD - 1)))
                elif l == 0:
                    act.wait_ge(sem_con, 16)
                    act.wait_ge(sem_x, 16)
                else:
                    act.wait_ge(*dve_drained.at(("ffn", KD - 1)))
                for half in range(2):
                    k = slice(4 * half, 4 * half + 4)
                    f(sq[:, k, 0:T - lo], X[:, k, lo:T], ACT.Square).then_inc(*act_done.tick(("sq", l, which, half)))
                o = full(("ssq", l, which))
                f(rstd[:, 0:T - lo], o[:, 0:T - lo], ACT.Sqrt, scale=1.0 / D, bias=eps)\
                    .then_inc(*act_drained.tick(("ssq", l, which)))
                if which == 0:
                    act.wait_ge(*dve_done.at(("modc", l)))
                dst = h2 if lo else hT
                for k in range(KD):
                    act.wait_ge(*dve_done.at(("xn", l, which, k)))
                    for s in range(lo // CTX, 2):
                        a = s * SEQ - lo
                        ins = f(dst[:, k, a:a + SEQ], sq[:, k, a:a + SEQ], ACT.Identity,
                                scale=gain[:, l, which, k, s:s + 1], bias=modc[:, l, 24 * which + k, s:s + 1])
                ins.then_inc(*act_done.tick(("h", l, which)))

            filler = {0: [(1, i) for i in range(MOD_CHUNKS)], 1: []}

            def modulation_rows(l, i):
                o = full(("mod", l, i))
                f(modrow[:, i % 12, :], o[0:2, 0:CHUNK], ACT.Copy).then_inc(*act_drained.tick(("mod", l, i)))

            def fill(l, n):
                for _ in range(n):
                    if filler[l]:
                        modulation_rows(*filler[l].pop(0))

            def project(l):
                lo, R = low(l), GATE_ROWS
                o = full(("gates", l))
                f(gate_raw[0:R, :], o[0:R, :], ACT.Identity, bias=par("b_gates")[0:R, l:l + 1])\
                    .then_inc(*act_drained.tick(("gates", l)))
                act.wait_ge(*act_drained.at(("gates", l)))
                f(gate_ls[0:R, :], gate_raw[0:R, :], ACT.Abs).then_inc(*act_done.tick(("gabs", l)))
                act.wait_ge(*act_done.at(("gabs", l)))
                f(gate_ls[0:R, :], gate_ls[0:R, :], ACT.Exp, scale=-1.0).then_inc(*act_done.tick(("gexp", l)))
                act.wait_ge(*act_done.at(("gexp", l)))
                f(gate_ls[0:R, :], gate_ls[0:R, :], ACT.Ln, bias=one[0:R, :]).then_inc(*act_done.tick(("gln", l)))
                for name in IN_ORDER:
                    if name == "mv":
                        for b in range(NB):
                            o = full((name, l, b))
                            f(vm[:, b, :, 0:DH], o[:, 0:MW].rearrange("p (h v) -> p h v", h=NH), ACT.Copy)\
                                .then_inc(*act_drained.tick((name, l, b)))
                        act.wait_ge(*dve_done.at(("row_m", l)))
                        f(row_em, row_m, ACT.Exp, scale=-1.0).then_inc(*act_done.tick(("row_em", l)))
                    elif name in ("av0", "av1"):
                        for b in range(NB):
                            o = full((name, l, b))
                            i = CHUNK * int(name[-1])
                            f(va[:, b, i:i + CHUNK], o[:, 0:CHUNK], ACT.Copy).then_inc(*act_drained.tick((name, l, b)))
                    elif name == "ca":
                        continue
                    else:
                        for m in range(2):
                            o = full((name, l, m))
                            if name == "mk":
                                f(mk[:, m, :], o, ACT.Copy, scale=DH ** -0.5).then_inc(*act_drained.tick((name, l, m)))
                            elif name == "mq":
                                f(mq[:, m, lo:T], o[:, lo:T], ACT.Copy).then_inc(*act_drained.tick((name, l, m)))
                            elif name in ("ak0", "ak1"):
                                f(ak[:, 2 * int(name[-1]) + m, :], o, ACT.Copy).then_inc(*act_drained.tick((name, l, m)))
                            elif name in ("aq0", "aq1"):
                                f(aq[:, 2 * int(name[-1]) + m, lo:T], o[:, lo:T], ACT.Copy)\
                                    .then_inc(*act_drained.tick((name, l, m)))
                            elif name == "cg":
                                f(mo[:, m, lo:T], o[:, lo:T], ACT.Sigmoid).then_inc(*act_drained.tick((name, l, m)))
                            else:
                                act.wait_ge(*dve_drained.at(("ca", l, m)))
                                f(mo[:, m, lo:T], o[:, lo:T], ACT.Sigmoid).then_inc(*act_drained.tick((name, l, m)))

            def mlstm(l):
                lo = low(l)
                for h in range(NH):
                    for s in range(NB):
                        a = max(lo, CTX if s >= 2 else 0)
                        o = full(("kq", l, h, s))
                        if h and s == 0:
                            act.wait_ge(*dve_done.at(("w", l, h - 1, 1, NB - 1)))
                        f(kq[:, s, a:T], o[:, a:T], ACT.Copy).then_inc(*act_drained.tick(("kq", l, h, s)))
                    for d in range(2):
                        col = 32 * d + h
                        if h:
                            act.wait_ge(*pe_done.at(("pv", l, h - 1, d)))
                        elif d == 0:
                            act.wait_ge(*dve_drained.at(("cols", l)))
                        for s in range(NB):
                            o = full(("dec", l, h, d, s))
                            for a, b in block_pairs(d, s, l):
                                ins = f(W[:, d, s, a * P:b * P], o[:, a * P:b * P], ACT.Exp,
                                        bias=cols[:, 0, s, col:col + 1])
                            ins.then_inc(*act_drained.tick(("dec", l, h, d, s)))
                    fill(l, 2)
                act.wait_ge(*dve_done.at(("hvar", l)))
                g = (NB - lo // P) * NH
                f(stat[:, 2, 0:g], stat[:, 1, 0:g], ACT.Sqrt, scale=1.0 / DH, bias=eps).then_inc(*act_done.tick(("hstd", l)))

            def attention(l):
                lo = low(l)
                units = [(h, t) for h in range(NH) for t in range(lo // P, NB)]
                scale = DH ** -0.5
                for n in range(len(units) + 2):
                    if n < len(units):
                        h, t = units[n]
                        nk = CTX if t < 2 else T
                        if n == 0:
                            act.wait_ge(*pe_done.at(("pv", l, NH - 1, 1)))
                        if n >= 2:
                            act.wait_ge(*pe_done.at(("aT", l) + units[n - 2]))
                        for c in range(2):
                            o = full(("s", l, h, t, c))
                            act.wait_ge(*dve_done.at(("smax", l, h, t, c)))
                            f(prob[:, n % 2, c, 0:nk], o[:, 0:nk], ACT.Exp, scale=scale, bias=rs[:, n % 2, 2 + c:3 + c],
                              accum_out=rs[:, n % 2, 4 + c:5 + c]).then_inc(*act_drained.tick(("s", l, h, t, c)))
                    fill(l, 1)
                    if 1 <= n <= len(units):
                        h, t = units[n - 1]
                        nk = CTX if t < 2 else T
                        o = full(("aT", l, h, t))
                        if n >= 3:
                            act.wait_ge(*pe_done.at(("o", l) + units[n - 3]))
                        f(probT[:, (n - 1) % 2, 0:nk // P, :], o[:, 0:nk].rearrange("p (b q) -> p b q", q=P), ACT.Copy)\
                            .then_inc(*act_drained.tick(("aT", l, h, t)))
                    if n >= 2:
                        h, t = units[n - 2]
                        o = full(("o", l, h, t))
                        f(mix[:, 2 + h, t * P:(t + 1) * P], o[:, 0:P], ACT.Copy).then_inc(*act_drained.tick(("o", l, h, t)))
                fill(l, MOD_CHUNKS)
                for h in range(NH):
                    act.wait_ge(*act_drained.at(("o", l, h, NB - 1)))
                    f(osq[:, h, lo:T], mix[:, 2 + h, lo:T], ACT.Square).then_inc(*act_done.tick(("osq", l, h)))
                for h in range(NH):
                    o = full(("osum", l, h))
                    if h:
                        act.wait_ge(*dve_done.at(("on", l, h - 1)))
                    f(rstd[:, lo:T], o[:, lo:T], ACT.Sqrt, scale=1.0 / DV, bias=eps)\
                        .then_inc(*act_drained.tick(("osum", l, h)))

            def conv_norm(l):
                lo = low(l)
                act.wait_ge(*dve_drained.at(("cmean", l)))
                f(kq[:, 0:2, lo:T], cy[:, :, lo:T], ACT.Square).then_inc(*act_done.tick(("csq", l)))
                o = full(("cvar", l))
                act.wait_ge(*dve_done.at(("on", l, NH - 1)))
                f(rstd[:, lo:T], o[:, lo:T], ACT.Sqrt, scale=1.0 / CW, bias=eps).then_inc(*act_drained.tick(("cvar", l)))
                act.wait_ge(*dve_done.at(("cn", l)))
                act.wait_ge(*pe_done.at(("hT", l, 1)))
                for m in range(2):
                    ins = f(mix[:, 6 + m, lo:T], cy[:, m, lo:T], ACT.Silu, scale=par("g_ln", l)[:, m:m + 1],
                            bias=par("b_ln", l)[:, m:m + 1])
                ins.then_inc(*act_done.tick(("mix_conv", l)))

            def dense():
                for i in range(FT):
                    o = full(("gate", i))
                    f(U[:, i, :], o, ACT.Silu).then_inc(*act_drained.tick(("gate", i)))

            def moe():
                act.wait_ge(*dve_done.at("moe_start"))
                n = act.value_load(trips[0:1, :], min_val=NE, max_val=PASSES * NE)
                act.sem_inc(y_act, 1)

                def take_input(count):
                    act.wait_ge(gathered, count)
                    f(h_slot[:, 0:4, :], ps[:, 4, :].rearrange("p (k n) -> p k n", k=4), ACT.Copy).then_inc(h_act, 1)

                take_input(1)
                with act.Fori(0, n) as i:
                    for t in range(ET):
                        act.wait_ge(gu_full, i * ET + (t + 1))
                        last = t - 4 + ET if t >= 4 else max(x for x in range(ET) if x % 4 == t)
                        act.wait_ge(glu_done, i * ET + (last + 1))
                        f(esilu[:, t % 4, :], ps[:, 2 + t % 2, 0:P], ACT.Silu).then_inc(silu_done, 1)
                    take_input(i + 2)
                    act.wait_ge(down_done, i * ET + 2 * ET)
                    f(y_slot[:, 0:512], ps[:, 0, :], ACT.Copy).then_inc(y_act, 1)

            act.wait_ge(sem_small, 16)
            f(cond[:, :, :], par("c").rearrange("p (k s) -> p k s", k=KD), ACT.Silu).then_inc(*act_done.tick("cond"))
            for i in range(MOD_CHUNKS):
                modulation_rows(0, i)
            act.wait_ge(*dve_done.at("lamdot"))
            for l in range(DEPTH):
                ins = f(lam[:, l, 0:2], lam[:, l, 2:4], ACT.Exp)
            ins.then_inc(*act_done.tick("lamexp"))
            for l in range(DEPTH):
                norm(l, 0)
                project(l)
                mlstm(l)
                attention(l)
                conv_norm(l)
                norm(l, 1)
                if l == 0:
                    dense()
            act.wait_ge(*dve_drained.at("logits"))
            f(rt[:, 1], rt[:, 0], ACT.Exp).then_inc(*act_done.tick("router_exp"))
            for k in range(KD):
                o = full(("h_tok", k))
                f(h_tok[:, :, k * P:(k + 1) * P], o[:, 0:2 * P].rearrange("p (b n) -> p b n", b=2), ACT.Copy)\
                    .then_inc(*act_drained.tick(("h_tok", k)))
            moe()
            act.wait_ge(*dve_done.at("x_final"))
            f(experts[:, 0, 0:KD * SEQ].rearrange("p (k t) -> p k t", k=KD), X[:, :, CTX:T], ACT.Square)\
                .then_inc(*act_done.tick("final_sq"))
            act.wait_ge(*pe_done.at("final_ssq"))
            f(rstd[:, 0:SEQ], ps[:, 0, 0:SEQ], ACT.Sqrt, scale=1.0 / D, bias=eps).then_inc(*act_done.tick("final_std"))

        @block.vector
        def _(dve):
            v = nc.vector

            def full(key):
                dve.wait_ge(*pe_done.at(key))
                return ps[:, plan.get(("bank", key), 0), :]

            def settled(ins, key):
                ins.then_inc(*dve_done.tick(key))
                dve.wait_ge(*dve_done.at(key))

            def modulation(l):
                dve.wait_ge(*pe_done.at(("modT", l, MOD_CHUNKS - 1)))
                b = par("b_mod", l).unsqueeze(2).to_broadcast([P, 48, 2])
                settled(v.tensor_tensor(modc[:, l], ps[:, 7, 0:96].rearrange("p (m s) -> p m s", s=2), b, ALU.add),
                        ("modv", l))
                for which, g in ((0, "g1"), (1, "g2")):
                    at = 24 * which + KD
                    ins = v.scalar_tensor_tensor(gain[:, l, which], modc[:, l, at:at + KD, :], 1.0,
                                                 par(g, l).unsqueeze(2).to_broadcast([P, KD, 2]), ALU.add, ALU.mult)
                ins.then_inc(*dve_done.tick(("modc", l)))

            def norm(l, which):
                lo = low(l) if which else 0
                dve.wait_ge(*act_drained.at(("ssq", l, which)))
                settled(v.reciprocal(rstd[:, 0:T - lo], rstd[:, 0:T - lo]), ("rstd", l, which))
                dve.wait_ge(*pe_done.at(("ssq", l, which)))
                for k in range(KD):
                    v.tensor_tensor(sq[:, k, 0:T - lo], X[:, k, lo:T], rstd[:, 0:T - lo], ALU.mult)\
                        .then_inc(*dve_done.tick(("xn", l, which, k)))

            def gate_rows(l):
                R = GATE_ROWS
                settled(v.memset(scratch[0:64, 2 * T:8 * T], 0.0), ("clear", l))
                dve.wait_ge(*act_done.at(("gln", l)))
                settled(v.scalar_tensor_tensor(gate_ls[0:R, :], gate_raw[0:R, :], 0.0, gate_ls[0:R, :],
                                               ALU.min, ALU.subtract), ("logsig", l))
                v.tensor_copy(li[0:NH, :], gate_raw[0:NH, :])
                v.tensor_copy(lf[0:NH, :], gate_ls[32:32 + NH, :])
                for s in range(2):
                    seg = slice(s * SEQ, (s + 1) * SEQ)
                    v.tensor_copy(li[32:32 + NH, seg], gate_raw[64:64 + NH, seg][:, ::-1])
                    ins = v.tensor_copy(lf[32:32 + NH, seg], gate_ls[96:96 + NH, seg][:, ::-1])
                settled(ins, ("gates_seq", l))
                settled(v.tensor_tensor_scan(row_b, reset, lf, 0.0, ALU.mult, ALU.add), ("row_b", l))
                settled(v.tensor_tensor_scan(row_m, lf, li, NEG, ALU.add, ALU.max), ("row_m", l))
                v.tensor_tensor(row_a, li, row_b, ALU.subtract)
                for j in range(NB):
                    blk = slice(j * P, (j + 1) * P)
                    ins = v.tensor_tensor(row_r[:, j, blk], row_b[:, blk], row_m[:, blk], ALU.subtract)
                settled(ins, ("row_r", l))
                for j in reversed(range(NB - 1)):
                    later = slice((j + 1) * P, T)
                    settled(v.tensor_scalar(row_r[:, j, later], row_r[:, j + 1, later],
                                            row_b[:, (j + 1) * P - 1:(j + 1) * P], None, ALU.add), ("row_r", l, j))
                dve.wait_ge(*act_done.at(("row_em", l)))
                v.tensor_copy(rows_n[0:32, 0:4, :], row_r[0:32])
                v.tensor_copy(rows_n[0:32, 4:6, :], kq[0:32, 0:2, :])
                for s in range(2):
                    seg = slice(s * SEQ, (s + 1) * SEQ)
                    v.tensor_copy(rows_n[32:64, 0:4, seg], row_r[32:64, :, seg][:, :, ::-1])
                    ins = v.tensor_copy(rows_n[32:64, 4:6, seg], kq[32:64, 0:2, seg][:, :, ::-1])
                ins.then_inc(*dve_done.tick(("rows", l)))

            def rope(l, name):
                x = (ak if name[:2] == "ak" else aq)[:, 2 * int(name[-1]):2 * int(name[-1]) + 2, CTX:T]
                y = rstd[:, :].rearrange("p (m t) -> p m t", m=2)
                dve.wait_ge(*act_drained.at((name, l, 1)))
                if name == "ak0":
                    dve.wait_ge(*act_done.at(("h", l, 0)))
                settled(v.stream_shuffle(y, x, [i ^ 16 for i in range(32)]), ("partner", l, name))
                v.tensor_tensor(x, x, cos.unsqueeze(1).to_broadcast([P, 2, SEQ]), ALU.mult)
                settled(v.tensor_tensor(y, y, sin.unsqueeze(1).to_broadcast([P, 2, SEQ]), ALU.mult), ("ropesin", l, name))
                settled(v.tensor_tensor(x, x, y, ALU.add), ("rope", l, name))

            def project(l):
                gate_rows(l)
                for name in ("ak0", "ak1", "aq0", "aq1"):
                    rope(l, name)
                dve.wait_ge(*pool_done.at(("pads", l)))
                for m in range(2):
                    o = full(("ca", l, m))
                    dve.wait_ge(*act_drained.at(("cg", l, m)))
                    s = slice(low(l) // CTX, 2)
                    v.tensor_tensor(upad[:, m, s, PAD:PAD + SEQ], o.rearrange("p (s t) -> p s t", s=2)[:, s],
                                    mo[:, m, :].rearrange("p (s t) -> p s t", s=2)[:, s], ALU.mult)\
                        .then_inc(*dve_drained.tick(("ca", l, m)))

            def mlstm(l):
                t0 = low(l) // P
                o = full(("cols", l))
                v.tensor_copy(cols[:, :, :, :].rearrange("p a b r -> p (a b r)"), o).then_inc(*dve_drained.tick(("cols", l)))
                dve.wait_ge(*dve_drained.at(("cols", l)))

                def head_sums(h):
                    for d in range(2):
                        i, col = 2 * h + d, 32 * d + h
                        o = full(("pv", l, h, d)).rearrange("p (b c) -> p b c", b=NB)
                        settled(v.scalar_tensor_tensor(den[:, i, t0:NB], o[:, t0:NB, DH], -1.0, cols[:, 1, t0:NB, col],
                                                       ALU.mult, ALU.max), ("nden", l, h, d))
                        settled(v.tensor_tensor(den[:, i, t0:NB], o[:, t0:NB, DH], den[:, i, t0:NB], ALU.max),
                                ("den", l, h, d))
                        settled(v.reciprocal(den[:, i, t0:NB], den[:, i, t0:NB]), ("rden", l, h, d))
                        for t in range(t0, NB):
                            if d == 0:
                                ins = v.tensor_scalar(hsum[:, t, h, :], o[:, t, 0:DH], den[:, i, t:t + 1], None, ALU.mult)
                            else:
                                ins = v.scalar_tensor_tensor(hsum[:, t, h, :], o[:, t, 0:DH], den[:, i, t:t + 1],
                                                             hsum[:, t, h, :], ALU.mult, ALU.add)
                        ins.then_inc(*dve_drained.tick(("pv", l, h, d)))
                        dve.wait_ge(*dve_drained.at(("pv", l, h, d)))

                for h in range(NH):
                    for d in range(2):
                        for s in range(NB):
                            dve.wait_ge(*act_drained.at(("dec", l, h, d, s)))
                            for a, b in block_pairs(d, s, l):
                                w = W[:, d, s, a * P:b * P]
                                ins = v.tensor_tensor(w, w, kq[:, s, a * P:b * P], ALU.mult)
                            ins.then_inc(*dve_done.tick(("w", l, h, d, s)))
                    if h == 0:
                        dve.wait_ge(*pe_done.at(("mo", l, 1)))
                    head_sums(h)
                g = (NB - t0) * NH
                x = hsum.rearrange("p b h v -> p (b h) v")[:, t0 * NH:NB * NH, :]
                x2 = hsq.rearrange("p (g v) -> p g v", v=DH)[:, 0:g, :]

                def spread(i):
                    return stat[:, i, 0:g].unsqueeze(2).to_broadcast([P, g, DH])

                settled(v.tensor_reduce(stat[:, 0, 0:g], x, AX_X, ALU.add), ("hsum", l))
                settled(v.tensor_scalar(stat[:, 0, 0:g], stat[:, 0, 0:g], 1.0 / DH, None, ALU.mult), ("hmean", l))
                settled(v.tensor_tensor(x, x, spread(0), ALU.subtract), ("hcen", l))
                settled(v.tensor_tensor(x2, x, x, ALU.mult), ("hsq", l))
                settled(v.tensor_reduce(stat[:, 1, 0:g], x2, AX_X, ALU.add), ("hvar", l))
                dve.wait_ge(*act_done.at(("hstd", l)))
                settled(v.reciprocal(stat[:, 3, 0:g], stat[:, 2, 0:g]), ("hrstd", l))
                v.tensor_tensor(x, x, spread(3), ALU.mult).then_inc(*dve_done.tick(("hn", l)))
                lo = low(l)
                for m in range(2):
                    o = full(("hT", l, m))
                    dve.wait_ge(*act_drained.at(("mo", l, m)))
                    v.scalar_tensor_tensor(mix[:, m, lo:T], o[:, lo:T], par("g_mlstm", l)[:, m:m + 1], mo[:, m, lo:T],
                                           ALU.mult, ALU.mult).then_inc(*dve_drained.tick(("hT", l, m)))

            def attention(l):
                lo = low(l)
                units = [(h, t) for h in range(NH) for t in range(lo // P, NB)]

                def maxima(n):
                    h, t = units[n]
                    nk = CTX if t < 2 else T
                    u = n % 2
                    for c in range(2):
                        o = full(("s", l, h, t, c))
                        settled(v.tensor_reduce(rs[:, u, c:c + 1], o[:, 0:nk], AX_X, ALU.max), ("max", l, h, t, c))
                        v.tensor_scalar(rs[:, u, 2 + c:3 + c], rs[:, u, c:c + 1], -DH ** -0.5, None, ALU.mult)\
                            .then_inc(*dve_done.tick(("smax", l, h, t, c)))

                def combine(n):
                    h, t = units[n]
                    nk = CTX if t < 2 else T
                    u = n % 2
                    dve.wait_ge(*act_drained.at(("s", l, h, t, 1)))
                    settled(v.reciprocal(rs[:, u, 6:8], rs[:, u, 4:6]), ("rsum", l, h, t))
                    settled(v.tensor_tensor(rs[:, u, 8:9], rs[:, u, 7:8], nlam(l), ALU.mult), ("lsum", l, h, t))
                    p = prob[:, u]
                    settled(v.tensor_scalar(p[:, 1, 0:nk], p[:, 1, 0:nk], rs[:, u, 8:9], None, ALU.mult), ("p1", l, h, t))
                    v.scalar_tensor_tensor(p[:, 0, 0:nk], p[:, 0, 0:nk], rs[:, u, 6:7], p[:, 1, 0:nk],
                                           ALU.mult, ALU.add).then_inc(*dve_done.tick(("a", l, h, t)))

                for n in range(len(units) + 1):
                    if n < len(units):
                        maxima(n)
                    if n:
                        combine(n - 1)
                lam_init = 0.8 - 0.6 * math.exp(-0.3 * l)
                settled(v.tensor_scalar(stat[:, 0, 0:1], par("g_sub", l)[:, 0:1], 1.0 - lam_init, None, ALU.mult),
                        ("g_sub", l))
                for h in range(NH):
                    dve.wait_ge(*act_drained.at(("osum", l, h)))
                    settled(v.reciprocal(rstd[:, lo:T], rstd[:, lo:T]), ("orstd", l, h))
                    v.scalar_tensor_tensor(mix[:, 2 + h, lo:T], mix[:, 2 + h, lo:T], stat[:, 0, 0:1], rstd[:, lo:T],
                                           ALU.mult, ALU.mult).then_inc(*dve_done.tick(("on", l, h)))
                dve.wait_ge(*dve_done.at(("on", l, NH - 1)))
                v.tensor_copy(stat[:, 1, 0:1], stat[:, 0, 0:1]).then_inc(*dve_done.tick(("mix_attn", l)))

            def conv_norm(l):
                lo = low(l)
                o = full(("cmean", l))
                for m in range(2):
                    ins = v.scalar_tensor_tensor(cy[:, m, lo:T], o[:, lo:T], -1.0 / CW, cy[:, m, lo:T], ALU.mult, ALU.add)
                ins.then_inc(*dve_drained.tick(("cmean", l)))
                dve.wait_ge(*act_drained.at(("cvar", l)))
                settled(v.reciprocal(rstd[:, lo:T], rstd[:, lo:T]), ("crstd", l))
                for m in range(2):
                    ins = v.tensor_tensor(cy[:, m, lo:T], cy[:, m, lo:T], rstd[:, lo:T], ALU.mult)
                ins.then_inc(*dve_done.tick(("cn", l)))

            def residual(l, kind, gate, key):
                for m in range(KD):
                    o = full(key(m))
                    for s in range(low(l) // CTX, 2):
                        seg = slice(s * SEQ, (s + 1) * SEQ)
                        ins = v.scalar_tensor_tensor(X[:, m, seg], o[:, seg], modc[:, l, gate + m, s:s + 1], X[:, m, seg],
                                                     ALU.mult, ALU.add)
                    ins.then_inc(*dve_drained.tick(key(m)))

            def dense():
                for i in range(FT):
                    o = full(("up", i))
                    dve.wait_ge(*act_drained.at(("gate", i)))
                    v.tensor_tensor(U[:, i, :], U[:, i, :], o, ALU.mult).then_inc(*dve_drained.tick(("up", i)))

            def router():
                o = full("logits")[:, 0:2 * NE].rearrange("p (b e) -> p b e", b=2)

                def wide(t):
                    return t.unsqueeze(2).to_broadcast([P, 2, NE])

                ordb = order.unsqueeze(1).to_broadcast([P, 2, NE])
                settled(v.tensor_tensor(rt[:, 0], o, par("b_router").unsqueeze(1).to_broadcast([P, 2, NE]), ALU.add), "bias")
                settled(v.tensor_reduce(r1[:, 0], rt[:, 0], AX_X, ALU.max), "lmax")
                v.tensor_tensor(rt[:, 0], rt[:, 0], wide(r1[:, 0]), ALU.subtract).then_inc(*dve_drained.tick("logits"))
                dve.wait_ge(*act_done.at("router_exp"))
                settled(v.tensor_reduce(r1[:, 1], rt[:, 1], AX_X, ALU.add), "psum")
                settled(v.reciprocal(r1[:, 1], r1[:, 1]), "rpsum")
                settled(v.tensor_tensor(rt[:, 2], rt[:, 1], wide(r1[:, 1]), ALU.mult), "probs")
                for i in range(2):
                    settled(v.tensor_reduce(r1[:, 2 + i], rt[:, 2], AX_X, ALU.max), ("top", i))
                    settled(v.tensor_tensor(rt[:, 3], rt[:, 2], wide(r1[:, 2 + i]), ALU.is_ge), ("is_top", i))
                    settled(v.tensor_tensor(rt[:, 3], rt[:, 3], ordb, ALU.mult), ("rank", i))
                    settled(v.tensor_reduce(r1[:, 4], rt[:, 3], AX_X, ALU.max), ("first", i))
                    settled(v.tensor_tensor(rt[:, 4 + i], rt[:, 3], wide(r1[:, 4]), ALU.is_equal), ("chosen", i))
                    if i == 0:
                        settled(v.scalar_tensor_tensor(rt[:, 2], rt[:, 4], -2.0, rt[:, 2], ALU.mult, ALU.add), "out")
                settled(v.tensor_tensor(rt[:, 6], rt[:, 4], rt[:, 5], ALU.add), "chosen")
                settled(v.tensor_tensor(r1[:, 5], r1[:, 2], r1[:, 3], ALU.add), "topsum")
                settled(v.reciprocal(r1[:, 5], r1[:, 5]), "rtopsum")
                for i in range(2):
                    settled(v.tensor_tensor(r1[:, 6 + i], r1[:, 2 + i], r1[:, 5], ALU.mult), ("share", i))
                    settled(v.tensor_tensor(rt[:, 4 + i], rt[:, 4 + i], wide(r1[:, 6 + i]), ALU.mult), ("shares", i))
                v.memset(slot_no, -1.0)
                settled(v.memset(share, 0.0), "slots0")
                by_expert = "p b e -> p e b"
                for r in range(PASSES):
                    ins = v.tensor_tensor(share[:, r * NE:(r + 1) * NE, :], rt[:, 4].rearrange(by_expert),
                                          rt[:, 5].rearrange(by_expert), ALU.add)
                o = full("rank")
                rank = o[:, 0:2 * NE].rearrange("p (b e) -> p b e", b=2)
                settled(v.tensor_scalar(rt[:, 7], rank, 1.0, None, ALU.add), "rank1")
                settled(v.tensor_tensor(rt[:, 7], rt[:, 7], rt[:, 6], ALU.mult), "rank_chosen")
                for r in range(PASSES):
                    ins = v.tensor_scalar(slot_no[:, r * NE:(r + 1) * NE, :], rt[:, 7].rearrange(by_expert),
                                          -1.0 - r * P, None, ALU.add)
                settled(v.tensor_reduce(r1[:, 4, 0:1], o[:, 2 * NE:3 * NE], AX_X, ALU.max), "most")
                settled(v.tensor_scalar(r1[:, 4, 0:1], r1[:, 4, 0:1], P + 0.5, float(NE), ALU.is_gt, ALU.mult), "round2")
                v.tensor_scalar(trips, r1[:, 4, 0:1], float(NE), None, ALU.add).then_inc(*dve_done.tick("trips"))
                dve.wait_ge(*dve_done.at("trips"))
                dve.wait_ge(*pe_done.at(("h_tok", KD - 1)))
                v.memset(y_slot, 0.0)
                v.memset(from_slot, 0.0).then_inc(*dve_done.tick("moe_start"))
                dve.wait_ge(*dve_done.at("moe_start"))
                dve.sem_inc(y_dve, 1)
                dve.sem_inc(from_slot_ready, 1)
                dve.sem_inc(glu_done, ET)
                dve.sem_inc(x_added, 2)

            def moe():
                n = dve.value_load(trips[0:1, :], min_val=NE, max_val=PASSES * NE)
                slots = field(con, CONST, "slots")

                def column(table, i, b):
                    return table[:, bass.ds(i, 1), b]

                def build_slots(i, count):
                    for b in range(2):
                        ins = v.tensor_scalar(to_slot[:, b, :], slots, column(slot_no, i, b), None, ALU.is_equal)
                    ins.then_inc(slots_built, 1)

                def take_input(count):
                    dve.wait_ge(gathered, count)
                    v.tensor_copy(h_slot[:, 4:8, :], ps[:, 5, :].rearrange("p (k n) -> p k n", k=4)).then_inc(h_dve, 1)

                def add_output(i):
                    for q in range(4):
                        dve.wait_ge(scattered, i * 4 + (q + 1))
                        for m in range(2):
                            k = 2 * q + m
                            ins = v.scalar_tensor_tensor(X[:, k, CTX:T], ps[:, 6 + q % 2, m * SEQ:(m + 1) * SEQ],
                                                         modc[:, 1, 40 + k, 1:2], X[:, k, CTX:T], ALU.mult, ALU.add)
                        ins.then_inc(x_added, 1)

                build_slots(0, 1)
                take_input(1)
                with dve.Fori(0, n) as i:
                    for t in range(ET):
                        last = t - 4 + ET if t >= 4 else max(x for x in range(ET) if x % 4 == t)
                        dve.wait_ge(down_done, i * ET + (last + 1))
                        dve.wait_ge(silu_done, i * ET + (t + 1))
                        v.tensor_tensor(ehid[:, t % 4, :], esilu[:, t % 4, :], ps[:, 2 + t % 2, P:2 * P], ALU.mult)\
                            .then_inc(glu_done, 1)
                        if t == 1:
                            dve.wait_ge(shares_turned, i + 1)
                            for b in range(2):
                                ins = v.tensor_scalar(shares[:, b, :], slots, column(slot_no, i, b), column(share, i, b),
                                                      ALU.is_equal, ALU.mult)
                            ins.then_inc(shares_built, 1)
                        if t == 2:
                            dve.wait_ge(x_added, i * 4 + 2)
                            add_output(i)
                        if t == 5:
                            dve.wait_ge(shares_turned, i + 2)
                            v.tensor_copy(from_slot, ps[:, 4, 0:2 * P]).then_inc(from_slot_ready, 1)
                            dve.wait_ge(gathered, i + 1)
                            build_slots(i + 1, i + 2)
                    take_input(i + 2)
                    dve.wait_ge(down_done, i * ET + 2 * ET)
                    v.tensor_copy(y_slot[:, 512:1024], ps[:, 1, :]).then_inc(y_dve, 1)
                dve.wait_ge(x_added, n * 4 + 2)
                add_output(n)
                dve.wait_ge(x_added, n * 4 + 6)
                v.tensor_copy(r1[:, 4, 0:1], r1[:, 4, 1:2]).then_inc(*dve_done.tick("x_final"))

            def nlam(l):
                return lam[:, l, 0:1]

            dve.wait_ge(sem_small, 16)
            q = par("lam").rearrange("p (l a d) -> p l a d", l=DEPTH, a=4)
            pr = lprod[:, 256:512].rearrange("p (a d) -> p a d", a=2 * DEPTH)
            for l in range(DEPTH):
                for i in range(2):
                    ins = v.tensor_tensor(pr[:, 2 * l + i], q[:, l, 2 * i], q[:, l, 2 * i + 1], ALU.mult)
            settled(ins, "lamprod")
            for l in range(DEPTH):
                ins = v.tensor_reduce(lam[:, l, 2:4], pr[:, 2 * l:2 * l + 2], AX_X, ALU.add)
            settled(ins, "lamdot")
            dve.wait_ge(*act_done.at("lamexp"))
            for l in range(DEPTH):
                lam_init = 0.8 - 0.6 * math.exp(-0.3 * l)
                settled(v.tensor_tensor(lam[:, l, 2:3], lam[:, l, 1:2], lam[:, l, 0:1], ALU.subtract), ("lamdiff", l))
                settled(v.tensor_scalar(lam[:, l, 0:1], lam[:, l, 2:3], -lam_init, None, ALU.add), ("nlam", l))
            for l in range(DEPTH):
                if l == 0:
                    modulation(0)
                norm(l, 0)
                project(l)
                mlstm(l)
                attention(l)
                conv_norm(l)
                if l == 0:
                    modulation(1)
                residual(l, "y", 16, lambda m: ("y", l, m))
                dve.wait_ge(*dve_drained.at(("y", l, KD - 1)))
                norm(l, 1)
                if l == 0:
                    dense()
                    residual(0, "ffn", 40, lambda m: ("ffn", m))
                    dve.wait_ge(*dve_drained.at(("ffn", KD - 1)))
            router()
            moe()
            dve.wait_ge(*act_done.at("final_std"))
            settled(v.reciprocal(rstd[:, 0:SEQ], rstd[:, 0:SEQ]), "final_rstd")
            for k in range(KD):
                ins = v.scalar_tensor_tensor(h2[:, k, :], X[:, k, CTX:T], par("g_final")[:, k:k + 1], rstd[:, 0:SEQ],
                                             ALU.mult, ALU.mult)
            ins.then_inc(*dve_done.tick("final"))

        @block.gpsimd
        def _(pool):
            g = nc.gpsimd
            for l in range(DEPTH):
                s0 = low(l) // CTX
                pool.wait_ge(*act_done.at(("h", l, 0)))
                g.memset(upad[:, :, :, 0:PAD], 0.0)
                g.memset(upad[:, :, :, PAD + SEQ:], 0.0)
                g.memset(vm_all[:, NB * NH * (DH + 1):], 1.0)
                g.memset(vm[:, :, :, DH:DH + 1], 1.0).then_inc(*pool_done.tick(("pads", l)))
                for m in range(2):
                    pool.wait_ge(*dve_drained.at(("ca", l, m)))
                    w = par("w_dw", l).rearrange("p (m j) -> p m j", m=2)[:, m]
                    y = cy[:, m, :].rearrange("p (s t) -> p s t", s=2)[:, s0:2]
                    for j in range(TAPS):
                        u = upad[:, m, s0:2, j:j + SEQ]
                        if j:
                            pool.wait_ge(*pool_done.at(("tap", l, m, j - 1)))
                        if j == 0:
                            ins = g.tensor_scalar(y, u, w[:, 0:1], par("b_dw", l)[:, m:m + 1], ALU.mult, ALU.add)
                        else:
                            p = tap.rearrange("p (s t) -> p s t", s=2)[:, s0:2]
                            g.tensor_scalar(p, u, w[:, j:j + 1], None, ALU.mult)\
                             .then_inc(*pool_done.tick(("product", l, m, j)))
                            pool.wait_ge(*pool_done.at(("product", l, m, j)))
                            ins = g.tensor_tensor(y, y, p, ALU.add)
                        ins.then_inc(*pool_done.tick(("tap", l, m, j) if (m, j) != (1, TAPS - 1) else ("conv", l)))


def constants():
    con = np.zeros((P, NCONST), np.float32)

    def put(name, value):
        a, n = CONST[name]
        con[:value.shape[0], a:a + n] = value.reshape(value.shape[0], n)

    put("ident", np.eye(P, dtype=np.float32))
    put("ones", np.ones((P, P), np.float32))
    i = np.arange(P)
    put("mask_f", np.where(i[None, :] >= i[:, None], 0.0, NEG).astype(np.float32))
    put("mask_b", np.where(i[None, :] <= i[:, None], 0.0, NEG).astype(np.float32))
    axis, half, n = (i % 64) // 32, (i % 32) // 16, i % 16
    inv = (np.float32(10000.0) ** (-(2 * n).astype(np.float32) / np.float32(32))).astype(np.float32)
    t = np.arange(SEQ)
    pos = np.where(axis[:, None] == 0, (t // 64)[None, :], (t % 64)[None, :]).astype(np.float32)
    ang = pos * inv[:, None]
    put("cos", np.cos(ang).astype(np.float32))
    put("sin", (np.where(half[:, None] == 0, -1.0, 1.0) * np.sin(ang)).astype(np.float32))
    put("reset", np.broadcast_to((np.arange(T) % P != 0).astype(np.float32), (P, T)))
    pick = np.zeros((P, 2 * NH, P), np.float32)
    for r in range(2 * NH):
        pick[32 * (r // NH) + r % NH, r] = 1.0
    put("pick", pick)
    put("before", (i[:, None] < i[None, :]).astype(np.float32))
    put("slots", np.broadcast_to(i.astype(np.float32), (P, P)))
    put("order", np.broadcast_to(np.arange(NE, 0, -1).astype(np.float32), (P, NE)))
    put("eps", np.full((P, 1), EPS, np.float32))
    put("one", np.ones((P, 1), np.float32))
    return con


def column_chunks(w, width):
    return w.reshape(KD, P, -1, width).transpose(2, 1, 0, 3).reshape(-1, P, KD * width)


def feature_major(v):
    v = v.reshape(v.shape[:-1] + (v.shape[-1] // P, P))
    return np.moveaxis(v, -1, 0).reshape(P, -1)


def lay_out(i):
    small = np.zeros((P, NSMALL), np.float32)

    def put(name, value):
        a, n = SMALL[name]
        small[:value.shape[0], a:a + n] = value.reshape(value.shape[0], n)

    put("c", np.stack([feature_major(i["c_ctx"]), feature_major(i["c"][0])], axis=-1))
    for name, src in (("b_mod", "b_mod"), ("g1", "g_norm1"), ("g2", "g_norm2"), ("g_mlstm", "g_mlstm"),
                      ("g_sub", "g_subln"), ("b_dw", "b_dw"), ("g_ln", "g_conv_ln"), ("b_ln", "b_conv_ln"),
                      ("g_final", "g_final")):
        put(name, feature_major(i[src]))
    bg = np.zeros((P, DEPTH), np.float32)
    gates = np.zeros((DEPTH, P, KD, GATE_ROWS), np.float32)
    for r in range(4):
        bg[32 * r:32 * r + NH] = i["b_gates"][:, NH * r:NH * (r + 1)].T
        cols = i["w_in"][:, :, GATE_COL + NH * r:GATE_COL + NH * (r + 1)]
        gates[:, :, :, 32 * r:32 * r + NH] = cols.reshape(DEPTH, KD, P, NH).transpose(0, 2, 1, 3)
    put("b_gates", bg)
    lam = np.stack([i["lambda_q1"], i["lambda_k1"], i["lambda_q2"], i["lambda_k2"]], axis=1)
    put("lam", np.broadcast_to(lam.reshape(1, -1), (P, lam.size)))
    put("w_dw", i["w_dw"].reshape(DEPTH, TAPS, 2, P).transpose(3, 0, 2, 1).reshape(P, -1))
    put("w_router", i["w_router"][0].reshape(KD, P, NE).transpose(1, 0, 2).reshape(P, -1))
    put("b_router", np.broadcast_to(i["b_router"][0], (P, NE)))
    x = np.concatenate([i["ctx"][0], i["x"][0]], axis=0)
    down = np.zeros((3 * KD * P, D), np.float32)
    down[:FF] = i["w_ffn_down"][0]
    exp_gu = [i[n][0].reshape(NE, KD, P, ET, P).transpose(0, 3, 2, 1, 4).reshape(NE, ET, P, KD * P)
              for n in ("w_exp_gate", "w_exp_up")]
    exp_dn = i["w_exp_down"][0].reshape(NE, ET, P, D)
    return {
        "con": constants(),
        "small": small,
        "x": x.T.reshape(KD, P, T).transpose(1, 0, 2).reshape(P, KD * T),
        "gates": gates.reshape(DEPTH, P, KD * GATE_ROWS),
        "mod": np.stack([column_chunks(w, CHUNK) for w in i["w_mod"]]),
        "in": np.stack([np.concatenate([column_chunks(w[:, IN_COL[n]:IN_COL[n] + CHUNK], CHUNK) for n in IN_ORDER])
                        for w in i["w_in"]]),
        "out": np.stack([column_chunks(w, CHUNK) for w in i["w_out"]]),
        "gate": column_chunks(i["w_ffn_gate"][0], CHUNK),
        "up": column_chunks(i["w_ffn_up"][0], CHUNK),
        "down": down.reshape(3, KD, P, D // CHUNK, CHUNK).transpose(3, 0, 2, 1, 4).reshape(D // CHUNK, 3, P, SLOT),
        "experts": np.concatenate(exp_gu + [exp_dn], axis=3),
    }


def kernel(**inputs):
    import concourse.bacc as _bacc
    from concourse.bass_utils import run_bass_kernel_spmd as _run

    arrays = {k: np.ascontiguousarray(v) for k, v in lay_out({k: np.asarray(v) for k, v in inputs.items()}).items()}
    plan = {}
    for complete in (False, True):
        nc = _bacc.Bacc("TRN2", target_bir_lowering=False, num_devices=1)
        A = {n: nc.dram_tensor(n, a.shape, F32, kind="ExternalInput").ap() for n, a in arrays.items()}
        A["out_0"] = nc.dram_tensor("out_0", (P, KD * SEQ), F32, kind="ExternalOutput").ap()
        plan["complete"] = complete
        build(nc, A, plan)
    r = _run(nc, [arrays], core_ids=[0])
    y = r.results[0]["out_0"].reshape(P, KD, SEQ)
    return y.transpose(2, 1, 0).reshape(1, SEQ, D)
```

```python
import math
from contextlib import ExitStack

import numpy as np
import concourse.bass as bass
from concourse import mybir

F32 = mybir.dt.float32
F32R = mybir.dt.float32r
ALU = mybir.AluOpType
ACT = mybir.ActivationFunctionType
AX_X = mybir.AxisListType.X

P = 128
D = 1024
KD = D // P
SEQ = 256
CTX = 256
T = CTX + SEQ
NB = T // P
DEPTH = 2
NH = 4
DH = 64
DV = 128
MW = NH * DH
CW = 256
TAPS = 31
PAD = TAPS // 2
FF = 2816
FT = FF // P
NE = 8
FE = 1408
ET = FE // P
EPS = 1e-6
NEG = -1e30

CHUNK = 256
SLOT = KD * CHUNK
RING = 4
SPLIT = 2
ESLOT = 3 * KD * P
NBANK = 7
MOD_CHUNKS = 6 * D // CHUNK
VCOLS = 96
VPAD = VCOLS - (DH + 1)
CONV_STEP = (7, 3)
OUT_ORDER = (3, 0, 1, 2)
MIX_ORDER = (0, 1, 6, 7, 5, 2, 3, 4)
GATE_ROWS = P

UH = 12
PRODUCTS = ((0, 0), (0, 1), (1, 0))

IN_ORDER = ["mk", "mq", "mv", "cg", "ca", "ak0", "ak1", "aq0", "aq1", "av0", "av1", "mo"]
IN_COL = {"mq": 0, "mk": 256, "mv": 512, "mo": 768, "aq0": 1040, "aq1": 1296, "ak0": 1552,
          "ak1": 1808, "av0": 2064, "av1": 2320, "ca": 2576, "cg": 2832}
GATE_COL = 1024


def fields(sizes):
    at, out = 0, {}
    for name, n in sizes:
        out[name] = (at, n)
        at += n
    return out, at


CONST, NCONST = fields([("ident", P), ("ones", P), ("mask_f", P), ("mask_b", P), ("cos", SEQ), ("sin", SEQ),
                        ("reset", T), ("pick", NH * 2 * P), ("before", P), ("slots", P), ("order", NE), ("eps", 1), ("one", 1)])
SMALL, NSMALL = fields([("c", 2 * KD), ("b_mod", DEPTH * 48), ("g1", DEPTH * KD), ("g2", DEPTH * KD),
                        ("b_gates", DEPTH), ("g_mlstm", DEPTH * 2), ("lam", DEPTH * 4 * DH), ("g_sub", DEPTH),
                        ("w_dw", DEPTH * 2 * TAPS), ("b_dw", DEPTH * 2), ("g_ln", DEPTH * 2), ("b_ln", DEPTH * 2),
                        ("g_final", KD), ("w_router", KD * NE), ("b_router", NE)])


def sequence_block(direction, block):
    return block if direction == 0 else [1, 0, 3, 2][block]


def block_pairs(direction, source, layer):
    low = 0 if layer < DEPTH - 1 else 2
    j = sequence_block(direction, source)
    targets = [t for t in range(low, NB) if sequence_block(direction, t) >= j]
    runs = []
    for t in targets:
        if runs and runs[-1][1] == t:
            runs[-1][1] = t + 1
        else:
            runs.append([t, t + 1])
    return runs


class Signal:

    def __init__(self, plan, handle, name):
        self.plan, self.handle, self.name, self.count = plan, handle, name, 0

    def tick(self, key):
        self.count += 1
        self.plan[self.name, key] = self.count
        return self.handle, 1

    def at(self, key):
        return self.handle, self.plan[self.name, key] if self.plan.get("complete") else 1


def build(nc, A, plan):
    with ExitStack() as ctx:
        def sb(name, shape, dtype=F32, where=ctx):
            return where.enter_context(nc.sbuf_tensor("sb_" + name, shape, dtype))

        def signal(name):
            return Signal(plan, ctx.enter_context(nc.semaphore(name)), name)

        def semaphore(name):
            return ctx.enter_context(nc.semaphore(name))

        X = sb("X", [P, KD, T])
        con = sb("con", [P, NCONST])
        small = sb("small", [P, NSMALL])
        rstd = sb("rstd", [P, T])
        modc = sb("modc", [P, DEPTH, 48, 2])
        gain = sb("gain", [P, DEPTH, 2, KD, 2])
        cond = sb("cond", [P, KD, 2])
        with ExitStack() as over:
            e_hi = sb("e_hi", [P, 4, P], F32R, over)
        with ExitStack() as over:
            u_hi_mid = sb("u_hi_mid", [P, 2, T], F32R, over)
        kq = sb("kq", [P, NB, T])
        with ExitStack() as over:
            wg_lo = sb("wg_lo", [P, KD, GATE_ROWS], F32R, over)
            wg_hi = sb("wg_hi", [P, KD, GATE_ROWS], F32R, over)
        with ExitStack() as over:
            e_lo = sb("e_lo", [P, 4, P], F32R, over)
            esilu = sb("esilu", [P, 4, P], F32, over)
            ew_hi = sb("ew_hi", [P, 2, KD * P], F32R, over)
        rows_n = sb("rows_n", [P, 6, T])
        cols = sb("cols", [P, 2, NB, 64])
        tiny = sb("tiny", [P, 512])
        with ExitStack() as over:
            h_lo = sb("h_lo", [P, KD, T], F32R, over)
        H = sb("H", [P, KD * T])
        with ExitStack() as over:
            w_lo = sb("w_lo", [P, RING, KD, CHUNK], F32R, over)
            w_hi = sb("w_hi", [P, SPLIT, KD, CHUNK], F32R, over)
            with ExitStack() as late:
                u_hi_late = sb("u_hi_late", [P, FT - UH - 2, T], F32R, late)
            h_hi = sb("h_hi", [P, KD, T], F32R, over)
            u_lo = sb("u_lo", [P, FT, T], F32R, over)
            u_hi = sb("u_hi", [P, UH, T], F32R, over)
        ew_lo = []
        with ExitStack() as over:
            for f in range(ET):
                sb(f"ew_gate_up_{f}", [P, 2 * KD * P], F32, over)
                ew_lo.append(sb(f"ew_lo_{f}", [P, KD * P], F32R, over))
        arena = sb("arena", [P, ET * ESLOT])
        ps = ctx.enter_context(nc.psum_tensor("ps", [P, 8, 512], F32))

        hT = H[:, :].rearrange("p (k t) -> p k t", k=KD)
        mix = hT
        hsum = H[:, 6 * T:8 * T].rearrange("p (b h v) -> p b h v", b=NB, h=NH)
        h2 = H[:, 0:KD * SEQ].rearrange("p (k t) -> p k t", k=KD)
        comb = H[:, KD * SEQ:2 * KD * SEQ].rearrange("p (e t) -> p e t", e=NE)
        ring = arena[:, 0:RING * SLOT].rearrange("p (s n) -> p s n", s=RING)
        experts = arena[:, :].rearrange("p (f n) -> p f n", f=ET)
        work = arena[:, (RING + SPLIT) * SLOT + KD * T:ET * ESLOT]
        sq = work[:, 0:KD * T].rearrange("p (k t) -> p k t", k=KD)
        U = work[:, 0:FT * T].rearrange("p (f t) -> p f t", f=FT)
        top = [0]

        def take(n):
            top[0] += n
            return work[:, top[0] - n:top[0]]

        mq = take(2 * T).rearrange("p (m t) -> p m t", m=2)
        mk = take(2 * T).rearrange("p (m t) -> p m t", m=2)
        mo = take(2 * T).rearrange("p (m t) -> p m t", m=2)
        aq = take(4 * T).rearrange("p (m t) -> p m t", m=4)
        ak = take(4 * T).rearrange("p (m t) -> p m t", m=4)
        vm_all = take(NB * NH * (DH + 1) + VPAD)
        vm = vm_all[:, 0:NB * NH * (DH + 1)].rearrange("p (b h v) -> p b h v", b=NB, h=NH)
        va = take(NB * NH * DV).rearrange("p (b n) -> p b n", b=NB)
        upad = take(2 * 2 * (SEQ + 2 * PAD)).rearrange("p (m s t) -> p m s t", m=2, s=2)
        cy = take(2 * T).rearrange("p (m t) -> p m t", m=2)
        w_gates = rows_n[:, 0:2, :].rearrange("p a t -> p (a t)").rearrange("p (k n) -> p k n", k=KD)
        tap = take(T)
        scratch = take(2 * NB * T)
        gate_raw = scratch[:, 0:T]
        gate_ls = scratch[:, T:2 * T]
        li = scratch[0:64, 2 * T:3 * T]
        lf = scratch[0:64, 3 * T:4 * T]
        row_r = scratch[0:64, 4 * T:8 * T].rearrange("p (j t) -> p j t", j=NB)
        row_a, row_em = kq[0:64, 0, :], kq[0:64, 1, :]
        row_b, row_m = kq[0:64, 2, :], kq[0:64, 3, :]
        W = scratch.rearrange("p (u b t) -> p u b t", u=2, b=NB)
        prob = scratch[:, 0:4 * T].rearrange("p (u c t) -> p u c t", u=2, c=2)
        probT = scratch[:, 4 * T:6 * T].rearrange("p (u b q) -> p u b q", u=2, b=NB)
        orstd = rows_n[:, 0:NH, :]
        hsq = kq[:, 0:2, :].rearrange("p a t -> p (a t)")
        modrow = rows_n[64:66, 4:6, :].rearrange("p a t -> p (a t)").rearrange("p (u n) -> p u n", n=CHUNK)
        ehid = rows_n[:, 0, :].rearrange("p (u t) -> p u t", u=4)
        h_tok = H[:, KD * SEQ:2 * KD * SEQ].rearrange("p (b n) -> p b n", b=2)
        h_slot = H[:, 0:KD * P].rearrange("p (k n) -> p k n", k=KD)
        y_slot = H[:, KD * P:2 * KD * P]
        to_slot = kq[:, 3, 0:2 * P].rearrange("p (b n) -> p b n", b=2)
        shares = kq[:, 1, 0:2 * P].rearrange("p (b n) -> p b n", b=2)
        from_slot = kq[:, 2, 0:2 * P]
        PASSES = SEQ // P

        def field(t, table, name):
            a, n = table[name]
            return t[:, a:a + n]

        def par(name, l=None):
            t = field(small, SMALL, name)
            return t if l is None else t.rearrange("p (l n) -> p l n", l=DEPTH)[:, l]

        ident, ones = field(con, CONST, "ident"), field(con, CONST, "ones")
        mask = [field(con, CONST, "mask_f"), field(con, CONST, "mask_b")]
        cos, sin = field(con, CONST, "cos"), field(con, CONST, "sin")
        reset = field(con, CONST, "reset")[0:64, :]
        pick = field(con, CONST, "pick").rearrange("p (i n) -> p i n", i=2 * NH)[0:64]
        order = field(con, CONST, "order")
        eps, one = field(con, CONST, "eps"), field(con, CONST, "one")
        lam = tiny[:, 0:8].rearrange("p (l n) -> p l n", l=DEPTH)
        rs = tiny[:, 8:32].rearrange("p (u n) -> p u n", u=2)
        den = tiny[:, 32:64].rearrange("p (a b) -> p a b", a=2 * NH)
        stat = tiny[:, 64:128].rearrange("p (a n) -> p a n", a=4)
        rt = tiny[:, 128:256].rearrange("p (a b e) -> p a b e", a=8, b=2)
        slot_no = tiny[:, 256:256 + 2 * (PASSES * NE + 1)].rearrange("p (i b) -> p i b", b=2)
        share = tiny[:, 300:300 + 2 * (PASSES * NE + 1)].rearrange("p (i b) -> p i b", b=2)
        trips = tiny[:, 344:345].bitcast(mybir.dt.int32)
        r1 = tiny[:, 384:400].rearrange("p (a b) -> p a b", a=8)
        lprod = tiny[:, 0:512]

        sem_small = semaphore("parameters_loaded")
        sem_con = semaphore("constants_loaded")
        sem_x = semaphore("tokens_loaded")
        sem_gw = [semaphore(f"gate_weights_loaded_{l}") for l in range(DEPTH)]
        sem_slot = [semaphore(f"ring_slot_loaded_{s}") for s in range(RING)]
        sem_exp = [semaphore(f"expert_tile_loaded_{f}") for f in range(ET)]
        sem_out = semaphore("output_stored")
        pe_done = signal("pe_done")
        act_drained = signal("act_drained")
        dve_drained = signal("dve_drained")
        act_done = signal("act_done")
        dve_done = signal("dve_done")
        pool_done = signal("pool_done")
        gu_full = semaphore("gate_up_full")
        silu_done = semaphore("silu_done")
        glu_done = semaphore("glu_done")
        down_leading = semaphore("down_leading")
        down_split = semaphore("down_split")
        hidden = semaphore("hidden")
        down_done = semaphore("down_done")
        slots_built = semaphore("slots_built")
        gathered = semaphore("gathered")
        h_act = semaphore("h_slot_act")
        h_dve = semaphore("h_slot_dve")
        shares_built = semaphore("shares_built")
        shares_turned = semaphore("shares_turned")
        from_slot_ready = semaphore("from_slot_ready")
        y_act = semaphore("y_slot_act")
        y_dve = semaphore("y_slot_dve")
        scattered = semaphore("scattered")
        x_added = semaphore("x_added")

        block = ctx.enter_context(nc.Block())

        chunks = [("mod", 0, i) for i in range(MOD_CHUNKS)]
        for l in range(DEPTH):
            chunks += [("in", l, n) for n in IN_ORDER]
            if l == 0:
                chunks += [("mod", 1, i) for i in range(MOD_CHUNKS)]
            chunks += [("out", l, i) for i in range(D // CHUNK)]
            if l == 0:
                chunks += [(k, 0, i) for i in range(FF // CHUNK) for k in ("gate", "up")]
                chunks += [("down", 0, (i, j)) for i in range(D // CHUNK) for j in range(3)]
        slot_of = {c: n for n, c in enumerate(chunks)}

        def last_product(chunk):
            kind, l, i = chunk
            if kind == "in":
                return (i, l, NB - 1) if i in ("mv", "av0", "av1") else (i, l, 1)
            if kind == "out":
                return ("y", l, 2 * i + 1)
            if kind == "down":
                return chunk if i[1] < 2 else ("ffn", 2 * i[0] + 1)
            return (kind, 2 * i + 1) if kind in ("gate", "up") else chunk

        split_chunks = [c for c in chunks if c[0] in ("in", "gate", "up", "down")]
        split_of = {c: n for n, c in enumerate(split_chunks)}

        def hidden_hi(f):
            if f < UH:
                return u_hi[:, f, :]
            return u_hi_mid[:, f - UH, :] if f < UH + 2 else u_hi_late[:, f - UH - 2, :]

        def chunk_view(chunk):
            return ring[:, slot_of[chunk] % RING, :].rearrange("p (k n) -> p k n", k=KD)

        def low(l):
            return 0 if l < DEPTH - 1 else CTX

        @block.sync
        def _(sp):
            sp.dma_start(small[:, :], A["small"]).then_inc(sem_small, 16)
            for n, (kind, l, i) in enumerate(chunks):
                if n == 4:
                    sp.dma_start(con[:, :], A["con"]).then_inc(sem_con, 16)
                    sp.dma_start(X[:, :, :], A["x"].rearrange("p (k t) -> p k t", k=KD)).then_inc(sem_x, 16)
                if kind == "in" and i == IN_ORDER[0]:
                    if l > 0:
                        sp.wait_ge(*dve_done.at(("mix_attn", l - 1, OUT_ORDER[-1])))
                    sp.dma_start(w_gates, A["gates"][l].rearrange("p (k n) -> p k n", k=KD)).then_inc(sem_gw[l], 16)
                if n >= RING:
                    sp.wait_ge(*pe_done.at(last_product(chunks[n - RING])))
                width = SLOT
                if kind == "mod":
                    src = A["mod"][l, i]
                elif kind == "in":
                    src = A["in"][l, IN_ORDER.index(i)]
                elif kind == "out":
                    src = A["out"][l, i]
                elif kind in ("gate", "up"):
                    src = A[kind][i]
                else:
                    src = A["down"][i[0], i[1]]
                    width = min(KD, FT - KD * i[1]) * CHUNK
                sp.dma_start(ring[:, n % RING, 0:width], src[:, 0:width]).then_inc(sem_slot[n % RING], 16)

            sp.wait_ge(*act_done.at(("h", 1, 1, KD - 1)))
            for f in range(ET):
                sp.dma_start(experts[:, f, :], A["experts"][0, f]).then_inc(sem_exp[f], 16)
            sp.wait_ge(*dve_done.at("trips"))
            n = sp.value_load(trips[0:1, :], min_val=NE, max_val=PASSES * NE)
            with sp.Fori(1, n) as i:
                e = sp.snap(sp.to_reg(i & (NE - 1)), min_val=0, max_val=NE - 1)
                for f in range(ET):
                    sp.wait_ge(down_done, i * ET + (f + 1))
                    sp.dma_start(experts[:, f, :], A["experts"][bass.ds(e, 1), f].rearrange("a p n -> (a p) n"))\
                      .then_inc(sem_exp[f], 16)
            sp.wait_ge(*dve_done.at("final"))
            sp.dma_start(A["out_0"].rearrange("p (k t) -> p k t", k=KD), h2).then_inc(sem_out, 16)
            sp.wait_ge(sem_out, 16)

        @block.tensor
        def _(pe):
            opened = []

            def open_bank(key):
                n = len(opened)
                if n >= NBANK:
                    last = opened[n - NBANK]
                    drainer = act_drained if ("act_drained", last) in plan else dve_drained
                    pe.wait_ge(*drainer.at(last))
                opened.append(key)
                plan["bank", key] = n % NBANK
                return ps[:, n % NBANK, :]

            def loaded(chunk):
                n = slot_of[chunk]
                pe.wait_ge(sem_slot[n % RING], 16 * (n // RING + 1))
                return ring[:, n % RING, :].rearrange("p (k n) -> p k n", k=KD)

            def split(chunk):
                pe.wait_ge(*dve_done.at(("split", chunk)))
                return w_hi[:, split_of[chunk] % SPLIT], w_lo[:, slot_of[chunk] % RING]

            def product(o, k, left, right, first=0, final=KD - 1):
                for n, (a, b) in enumerate(PRODUCTS):
                    ins = pe.matmul(o, left[a], right[b],
                                    start=(k == first and n == 0), stop=(k == final and n == len(PRODUCTS) - 1))
                return ins

            def modulation(l, i):
                w = loaded(("mod", l, i))
                if i == 0 and l == 0:
                    pe.wait_ge(*act_done.at("cond"))
                o = open_bank(("mod", l, i))
                for k in range(KD):
                    ins = pe.matmul(o[0:2, 0:CHUNK], cond[:, k, :], w[:, k, :], start=(k == 0), stop=(k == KD - 1))
                ins.then_inc(*pe_done.tick(("mod", l, i)))
                if i:
                    turn_modulation(l, i - 1)
                if i == MOD_CHUNKS - 1:
                    turn_modulation(l, i)

            def turn_modulation(l, i):
                pe.wait_ge(*act_drained.at(("mod", l, i)))
                if i == 0 and l > 0:
                    pe.wait_ge(*dve_done.at(("modc", l - 1)))
                if i == 0 and l == 0:
                    pe.wait_ge(sem_con, 16)
                for m in range(2):
                    at = 2 * (2 * i + m)
                    ins = pe.transpose(ps[:, 7, at:at + 2], modrow[:, i % 4, m * P:(m + 1) * P], ident[64:66, 64:66])
                ins.then_inc(*pe_done.tick(("modT", l, i)))

            def norm(l, which):
                lo = low(l) if which else 0
                if l == 0:
                    pe.wait_ge(sem_con, 16)
                for half in range(2):
                    pe.wait_ge(*act_done.at(("sq", l, which, half)))
                    if half == 0:
                        o = open_bank(("ssq", l, which))
                    for k in range(4 * half, 4 * half + 4):
                        ins = pe.matmul(o[:, 0:T - lo], ones, sq[:, k, 0:T - lo], start=(k == 0), stop=(k == KD - 1))
                ins.then_inc(*pe_done.tick(("ssq", l, which)))

            def project(l):
                pe.wait_ge(*dve_done.at(("wg", l)))
                o = open_bank(("gates", l))
                for k in range(KD):
                    pe.wait_ge(*dve_done.at(("h_split", l, 0, k)))
                    ins = product(o, k, (wg_hi[:, k, :], wg_lo[:, k, :]), (h_hi[:, k, :], h_lo[:, k, :]))
                ins.then_inc(*pe_done.tick(("gates", l)))
                for name in IN_ORDER:
                    hi, lo = split(("in", l, name))
                    if name in ("mv", "av0", "av1"):
                        for b in range(NB):
                            o = open_bank((name, l, b))
                            t = slice(b * P, (b + 1) * P)
                            for k in range(KD):
                                ins = product(o[:, 0:CHUNK], k, (h_hi[:, k, t], h_lo[:, k, t]), (hi[:, k, :], lo[:, k, :]))
                            ins.then_inc(*pe_done.tick((name, l, b)))
                    else:
                        t = slice(0 if name in ("mk", "ak0", "ak1") else low(l), T)
                        for m in range(2):
                            o = open_bank((name, l, m))
                            c = slice(m * P, (m + 1) * P)
                            for k in range(KD):
                                ins = product(o[:, t], k, (hi[:, k, c], lo[:, k, c]), (h_hi[:, k, t], h_lo[:, k, t]))
                            ins.then_inc(*pe_done.tick((name, l, m)))

            filler = {0: [(1, i) for i in range(MOD_CHUNKS)], 1: []}

            def fill(l, n):
                for _ in range(n):
                    if filler[l]:
                        modulation(*filler[l].pop(0))

            def mlstm(l):
                pe.wait_ge(*dve_done.at(("rows", l)))
                o = open_bank(("cols", l)).rearrange("p (a b r) -> p a b r", a=2, b=NB)
                for a in range(2):
                    for b in range(NB):
                        ins = pe.transpose(o[:, a, b, :], rows_n[0:64, 4 + a, b * P:(b + 1) * P], ident[0:64, 0:64])
                ins.then_inc(*pe_done.tick(("cols", l)))

                def products(h):
                    r0, m = DH * (h % 2), h // 2
                    for s in range(NB):
                        a = max(low(l), CTX if s >= 2 else 0)
                        o = open_bank(("kq", l, h, s))
                        pe.matmul(o[:, a:T], mk[r0:r0 + DH, m, s * P:(s + 1) * P], mq[r0:r0 + DH, m, a:T],
                                  start=True, stop=True).then_inc(*pe_done.tick(("kq", l, h, s)))
                    for d in range(2):
                        row = d * NH + h
                        for s in range(NB):
                            j = sequence_block(d, s)
                            o = open_bank(("dec", l, h, d, s))
                            for a, b in block_pairs(d, s, l):
                                spans = [(a, b)]
                                if a <= s < b:
                                    spans = [(x, y) for x, y in ((a, s), (s + 1, b)) if y > x]
                                    pe.matmul(o[:, s * P:(s + 1) * P], pick[:, row, :],
                                              rows_n[0:64, j, s * P:(s + 1) * P], start=True, stop=False)
                                    ins = pe.matmul(o[:, s * P:(s + 1) * P], ident, mask[d], start=False, stop=True)
                                for x, y in spans:
                                    ins = pe.matmul(o[:, x * P:y * P], pick[:, row, :],
                                                    rows_n[0:64, j, x * P:y * P], start=True, stop=True)
                            ins.then_inc(*pe_done.tick(("dec", l, h, d, s)))

                def sums(h):
                    for d in range(2):
                        pe.wait_ge(*dve_done.at(("w", l, h, d, NB - 1)))
                        o = open_bank(("pv", l, h, d)).rearrange("p (b c) -> p b c", b=NB)
                        for t in range(low(l) // P, NB):
                            src = [s for s in range(NB) if sequence_block(d, s) <= sequence_block(d, t)]
                            for s in src:
                                at = (s * NH + h) * (DH + 1)
                                ins = pe.matmul(o[:, t, 0:VCOLS], W[:, d, s, t * P:(t + 1) * P], vm_all[:, at:at + VCOLS],
                                                start=(s == src[0]), stop=(s == src[-1]))
                        ins.then_inc(*pe_done.tick(("pv", l, h, d)))

                pe.wait_ge(*act_drained.at(("mq", l, 1)))
                for h in range(NH):
                    products(h)
                    fill(l, 2)
                    if h == 0:
                        pe.wait_ge(*act_drained.at(("mv", l, NB - 1)))
                        pe.wait_ge(*pool_done.at(("pads", l)))
                    sums(h)
                pe.wait_ge(*dve_done.at(("hn", l)))
                for m in range(2):
                    o = open_bank(("hT", l, m))
                    for b in range(low(l) // P, NB):
                        ins = pe.transpose(o[:, b * P:(b + 1) * P],
                                           hsum[:, b, 2 * m:2 * m + 2, :].rearrange("p h v -> p (h v)"), ident)
                    ins.then_inc(*pe_done.tick(("hT", l, m)))

            def attention(l):
                units = [(h, t) for h in range(NH) for t in range(low(l) // P, NB)]

                def scores(n):
                    h, t = units[n]
                    nk = CTX if t < 2 else T
                    for c in range(2):
                        o = open_bank(("s", l, h, t, c))
                        pe.matmul(o[:, 0:nk], aq[c * DH:(c + 1) * DH, h, t * P:(t + 1) * P],
                                  ak[c * DH:(c + 1) * DH, h, 0:nk], start=True, stop=True)\
                          .then_inc(*pe_done.tick(("s", l, h, t, c)))

                def turn(n):
                    h, t = units[n]
                    nk = CTX if t < 2 else T
                    pe.wait_ge(*dve_done.at(("a", l, h, t)))
                    o = open_bank(("aT", l, h, t))
                    for b in range(nk // P):
                        ins = pe.transpose(o[:, b * P:(b + 1) * P], prob[:, n % 2, 0, b * P:(b + 1) * P], ident)
                    ins.then_inc(*pe_done.tick(("aT", l, h, t)))

                def values(n):
                    h, t = units[n]
                    nb = 2 if t < 2 else NB
                    pe.wait_ge(*act_drained.at(("aT", l, h, t)))
                    o = open_bank(("o", l, h, t))
                    for b in range(nb):
                        ins = pe.matmul(o[:, 0:P], va[:, b, h * DV:(h + 1) * DV], probT[:, n % 2, b, :],
                                        start=(b == 0), stop=(b == nb - 1))
                    ins.then_inc(*pe_done.tick(("o", l, h, t)))

                def sum_squares(h):
                    pe.wait_ge(*act_done.at(("osq", l, h)))
                    o = open_bank(("osum", l, h))
                    pe.matmul(o[:, lo:T], ones, kq[:, 2 + h % 2, lo:T], start=True, stop=True)\
                      .then_inc(*pe_done.tick(("osum", l, h)))

                lo = low(l)
                pe.wait_ge(*dve_done.at(("rope", l, "aq1")))
                pe.wait_ge(*act_drained.at(("av1", l, NB - 1)))
                for n in range(len(units) + 2):
                    if n == CONV_STEP[l]:
                        conv_mean(l)
                    if n == CONV_STEP[l] + 2:
                        conv_variance(l)
                    if n < len(units):
                        scores(n)
                    fill(l, 1)
                    if 1 <= n <= len(units):
                        turn(n - 1)
                    if n >= 2:
                        values(n - 2)
                    if n >= 3 and units[n - 3][1] == NB - 1:
                        sum_squares(units[n - 3][0])
                fill(l, MOD_CHUNKS)
                sum_squares(NH - 1)

            def conv_mean(l):
                lo = low(l)
                pe.wait_ge(*pool_done.at(("conv", l)))
                o = open_bank(("cmean", l))
                for m in range(2):
                    ins = pe.matmul(o[:, lo:T], ones, cy[:, m, lo:T], start=(m == 0), stop=(m == 1))
                ins.then_inc(*pe_done.tick(("cmean", l)))

            def conv_variance(l):
                lo = low(l)
                pe.wait_ge(*act_done.at(("csq", l)))
                o = open_bank(("cvar", l))
                for m in range(2):
                    ins = pe.matmul(o[:, lo:T], ones, kq[:, m, lo:T], start=(m == 0), stop=(m == 1))
                ins.then_inc(*pe_done.tick(("cvar", l)))

            def output(l):
                lo = low(l)
                pe.wait_ge(*act_done.at(("mix_conv", l)))
                pe.wait_ge(*dve_drained.at(("hT", l, 1)))
                early = {}
                for i in range(2):
                    w = loaded(("out", l, i))
                    for m in range(2):
                        early[i, m] = open_bank(("y", l, 2 * i + m))
                        for k in MIX_ORDER[:4]:
                            pe.matmul(early[i, m][:, lo:T], w[:, k, m * P:(m + 1) * P], mix[:, k, lo:T],
                                      start=(k == MIX_ORDER[0]), stop=False)
                for i in range(D // CHUNK):
                    w = loaded(("out", l, i))
                    for m in range(2):
                        o = early[i, m] if i < 2 else open_bank(("y", l, 2 * i + m))
                        for k in MIX_ORDER[4 if i < 2 else 0:]:
                            if (i, m) == (0, 0):
                                pe.wait_ge(*dve_done.at(("mix_attn", l, k - 2)))
                            ins = pe.matmul(o[:, lo:T], w[:, k, m * P:(m + 1) * P], mix[:, k, lo:T],
                                            start=(k == MIX_ORDER[0]), stop=(k == MIX_ORDER[-1]))
                        ins.then_inc(*pe_done.tick(("y", l, 2 * i + m)))

            def dense():
                for i in range(FF // CHUNK):
                    for kind in ("gate", "up"):
                        hi, lo = split((kind, 0, i))
                        for m in range(2):
                            o = open_bank((kind, 2 * i + m))
                            c = slice(m * P, (m + 1) * P)
                            for k in range(KD):
                                if (i, kind, m) == (0, "gate", 0):
                                    pe.wait_ge(*dve_done.at(("h_split", 0, 1, k)))
                                ins = product(o, k, (hi[:, k, c], lo[:, k, c]), (h_hi[:, k, :], h_lo[:, k, :]))
                            ins.then_inc(*pe_done.tick((kind, 2 * i + m)))
                for i in range(D // CHUNK):
                    o = [open_bank(("ffn", 2 * i + m)) for m in range(2)]
                    for j in range(3):
                        hi, lo = split(("down", 0, (i, j)))
                        for m in range(2):
                            c = slice(m * P, (m + 1) * P)
                            for k in range(KD * j, min(FT, KD * j + KD)):
                                if (i, m) == (0, 0):
                                    pe.wait_ge(*dve_done.at(("u_split", k)))
                                q = k - KD * j
                                ins = product(o[m], k, (hi[:, q, c], lo[:, q, c]), (hidden_hi(k), u_lo[:, k, :]),
                                              final=FT - 1)
                            if j == 2 and m == 0:
                                ins.then_inc(*pe_done.tick(("ffn", 2 * i)))
                        if j < 2:
                            ins.then_inc(*pe_done.tick(("down", 0, (i, j))))
                    ins.then_inc(*pe_done.tick(("ffn", 2 * i + 1)))

            def router():
                pe.wait_ge(*act_done.at(("h", 1, 1, KD - 1)))
                o = open_bank("logits")
                w = par("w_router").rearrange("p (k e) -> p k e", k=KD)
                for b in range(2):
                    for k in range(KD):
                        ins = pe.matmul(o[:, b * NE:(b + 1) * NE], h2[:, k, b * P:(b + 1) * P], w[:, k, :],
                                        start=(k == 0), stop=(k == KD - 1))
                ins.then_inc(*pe_done.tick("logits"))
                for k in range(KD):
                    o = open_bank(("h_tok", k))
                    for b in range(2):
                        ins = pe.transpose(o[:, b * P:(b + 1) * P], h2[:, k, b * P:(b + 1) * P], ident)
                    ins.then_inc(*pe_done.tick(("h_tok", k)))
                pe.wait_ge(*dve_done.at("chosen"))
                o = open_bank("rank")
                before = field(con, CONST, "before")
                pe.matmul(o[:, 0:NE], before, rt[:, 6, 0], start=True, stop=True)
                pe.matmul(o[:, NE:2 * NE], before, rt[:, 6, 1], start=True, stop=False)
                pe.matmul(o[:, NE:2 * NE], ones, rt[:, 6, 0], start=False, stop=True)
                for b in range(2):
                    ins = pe.matmul(o[:, 2 * NE:3 * NE], ones, rt[:, 6, b], start=(b == 0), stop=(b == 1))
                ins.then_inc(*pe_done.tick("rank"))

            def moe():
                pe.wait_ge(*dve_done.at("moe_start"))
                pe.wait_ge(*act_drained.at(("h_tok", KD - 1)))
                n = pe.value_load(trips[0:1, :], min_val=NE, max_val=PASSES * NE)
                pe.sem_inc(down_done, ET)
                pe.sem_inc(shares_turned, 1)

                def gather(count):
                    pe.wait_ge(slots_built, count)
                    for k in range(KD):
                        for b in range(2):
                            ins = pe.matmul(ps[:, 4 + k // 4, (k % 4) * P:(k % 4 + 1) * P], h_tok[:, b, k * P:(k + 1) * P],
                                            to_slot[:, b, :], start=(b == 0), stop=(b == 1))
                    ins.then_inc(gathered, 1)

                def scatter(i):
                    pe.wait_ge(from_slot_ready, i + 1)
                    for q in range(4):
                        pe.wait_ge(x_added, i * 4 + (q + 1))
                        for m in range(2):
                            ins = pe.matmul(ps[:, 6 + q % 2, m * SEQ:(m + 1) * SEQ], y_slot[:, (2 * q + m) * P:(2 * q + m + 1) * P],
                                            from_slot, start=True, stop=True)
                        ins.then_inc(scattered, 1)

                gather(1)
                with pe.Fori(0, n) as i:
                    def down(f):
                        pe.wait_ge(glu_done, i * ET + (ET + f + 1))
                        if f == 0:
                            pe.wait_ge(y_act, i + 1)
                            pe.wait_ge(y_dve, i + 1)
                        pe.wait_ge(down_split, i * ET + (f + 1))
                        left = (e_hi[:, f % 4, :], e_lo[:, f % 4, :])
                        right = (ew_hi[:, f % 2, :], ew_lo[f])
                        for n, (a, b) in enumerate(PRODUCTS):
                            for m in range(2):
                                ins = pe.matmul(ps[:, m, :], left[a], right[b][:, m * 512:(m + 1) * 512],
                                                start=(f == 0 and n == 0), stop=(f == ET - 1 and n == len(PRODUCTS) - 1))
                        ins.then_inc(down_done, 1)

                    for f in range(ET):
                        pe.wait_ge(sem_exp[f], i * 16 + 16)
                        if f == 0:
                            pe.wait_ge(h_act, i + 1)
                            pe.wait_ge(h_dve, i + 1)
                        last = f - 2 + ET if f >= 2 else max(x for x in range(ET) if x % 2 == f)
                        pe.wait_ge(glu_done, i * ET + (last + 1))
                        for a in range(2):
                            w = experts[:, f, a * KD * P:(a + 1) * KD * P].rearrange("p (k n) -> p k n", k=KD)
                            for k in range(KD):
                                ins = pe.matmul(ps[:, 2 + f % 2, a * P:(a + 1) * P], w[:, k, :], h_slot[:, k, :],
                                                start=(k == 0), stop=(k == KD - 1))
                        ins.then_inc(gu_full, 1)
                        if f:
                            down(f - 1)
                        if f == 2:
                            scatter(i)
                        if f == 5:
                            pe.wait_ge(shares_built, i + 1)
                            for b in range(2):
                                ins = pe.transpose(ps[:, 4, b * P:(b + 1) * P], shares[:, b, :], ident)
                            ins.then_inc(shares_turned, 1)
                    pe.wait_ge(from_slot_ready, i + 2)
                    gather(i + 2)
                    down(ET - 1)
                pe.wait_ge(y_act, n + 1)
                pe.wait_ge(y_dve, n + 1)
                scatter(n)

            for i in range(MOD_CHUNKS):
                modulation(0, i)
            for l in range(DEPTH):
                norm(l, 0)
                project(l)
                mlstm(l)
                attention(l)
                output(l)
                norm(l, 1)
                if l == 0:
                    dense()
            router()
            moe()
            pe.wait_ge(*act_done.at("final_sq"))
            for k in range(KD):
                ins = pe.matmul(ps[:, 0, 0:SEQ], ones, experts[:, 0, k * SEQ:(k + 1) * SEQ],
                                start=(k == 0), stop=(k == KD - 1))
            ins.then_inc(*pe_done.tick("final_ssq"))

        @block.scalar
        def _(act):
            f = nc.scalar.activation

            def full(key):
                act.wait_ge(*pe_done.at(key))
                return ps[:, plan.get(("bank", key), 0), :]

            def norm(l, which):
                lo = low(l) if which else 0
                if which == 1:
                    act.wait_ge(*dve_drained.at(("y", l, KD - 1)))
                elif l == 0:
                    act.wait_ge(sem_con, 16)
                    act.wait_ge(sem_x, 16)
                else:
                    act.wait_ge(*dve_drained.at(("ffn", KD - 1)))
                for half in range(2):
                    k = slice(4 * half, 4 * half + 4)
                    f(sq[:, k, 0:T - lo], X[:, k, lo:T], ACT.Square).then_inc(*act_done.tick(("sq", l, which, half)))
                o = full(("ssq", l, which))
                f(rstd[:, 0:T - lo], o[:, 0:T - lo], ACT.Sqrt, scale=1.0 / D, bias=eps)\
                    .then_inc(*act_drained.tick(("ssq", l, which)))
                if which == 0:
                    act.wait_ge(*dve_done.at(("modc", l)))
                dst = h2 if lo else hT
                for k in range(KD):
                    act.wait_ge(*dve_done.at(("xn", l, which, k)))
                    for s in range(lo // CTX, 2):
                        a = s * SEQ - lo
                        ins = f(dst[:, k, a:a + SEQ], sq[:, k, a:a + SEQ], ACT.Identity,
                                scale=gain[:, l, which, k, s:s + 1], bias=modc[:, l, 24 * which + k, s:s + 1])
                    ins.then_inc(*act_done.tick(("h", l, which, k)))

            filler = {0: [(1, i) for i in range(MOD_CHUNKS)], 1: []}

            def modulation_rows(l, i):
                o = full(("mod", l, i))
                f(modrow[:, i % 4, :], o[0:2, 0:CHUNK], ACT.Copy).then_inc(*act_drained.tick(("mod", l, i)))

            def fill(l, n):
                for _ in range(n):
                    if filler[l]:
                        modulation_rows(*filler[l].pop(0))

            def project(l):
                lo, R = low(l), GATE_ROWS
                o = full(("gates", l))
                f(gate_raw[0:R, :], o[0:R, :], ACT.Identity, bias=par("b_gates")[0:R, l:l + 1])\
                    .then_inc(*act_drained.tick(("gates", l)))
                act.wait_ge(*act_drained.at(("gates", l)))
                f(gate_ls[0:R, :], gate_raw[0:R, :], ACT.Abs).then_inc(*act_done.tick(("gabs", l)))
                act.wait_ge(*act_done.at(("gabs", l)))
                f(gate_ls[0:R, :], gate_ls[0:R, :], ACT.Exp, scale=-1.0).then_inc(*act_done.tick(("gexp", l)))
                act.wait_ge(*act_done.at(("gexp", l)))
                f(gate_ls[0:R, :], gate_ls[0:R, :], ACT.Ln, bias=one[0:R, :]).then_inc(*act_done.tick(("gln", l)))
                for name in IN_ORDER:
                    if name == "mv":
                        for b in range(NB):
                            o = full((name, l, b))
                            f(vm[:, b, :, 0:DH], o[:, 0:MW].rearrange("p (h v) -> p h v", h=NH), ACT.Copy)\
                                .then_inc(*act_drained.tick((name, l, b)))
                        act.wait_ge(*dve_done.at(("row_m", l)))
                        f(row_em, row_m, ACT.Exp, scale=-1.0).then_inc(*act_done.tick(("row_em", l)))
                    elif name in ("av0", "av1"):
                        for b in range(NB):
                            o = full((name, l, b))
                            i = CHUNK * int(name[-1])
                            f(va[:, b, i:i + CHUNK], o[:, 0:CHUNK], ACT.Copy).then_inc(*act_drained.tick((name, l, b)))
                    elif name == "ca":
                        continue
                    else:
                        for m in range(2):
                            o = full((name, l, m))
                            if name == "mk":
                                f(mk[:, m, :], o, ACT.Copy, scale=DH ** -0.5).then_inc(*act_drained.tick((name, l, m)))
                            elif name == "mq":
                                f(mq[:, m, lo:T], o[:, lo:T], ACT.Copy).then_inc(*act_drained.tick((name, l, m)))
                            elif name in ("ak0", "ak1"):
                                f(ak[:, 2 * int(name[-1]) + m, :], o, ACT.Copy).then_inc(*act_drained.tick((name, l, m)))
                            elif name in ("aq0", "aq1"):
                                f(aq[:, 2 * int(name[-1]) + m, lo:T], o[:, lo:T], ACT.Copy)\
                                    .then_inc(*act_drained.tick((name, l, m)))
                            elif name == "cg":
                                f(mo[:, m, lo:T], o[:, lo:T], ACT.Sigmoid).then_inc(*act_drained.tick((name, l, m)))
                            else:
                                act.wait_ge(*dve_drained.at(("ca", l, m)))
                                f(mo[:, m, lo:T], o[:, lo:T], ACT.Sigmoid).then_inc(*act_drained.tick((name, l, m)))

            def mlstm(l):
                lo = low(l)
                for h in range(NH):
                    for s in range(NB):
                        a = max(lo, CTX if s >= 2 else 0)
                        o = full(("kq", l, h, s))
                        if h and s == 0:
                            act.wait_ge(*dve_done.at(("w", l, h - 1, 1, NB - 1)))
                        f(kq[:, s, a:T], o[:, a:T], ACT.Copy).then_inc(*act_drained.tick(("kq", l, h, s)))
                    for d in range(2):
                        col = 32 * d + h
                        if h:
                            act.wait_ge(*pe_done.at(("pv", l, h - 1, d)))
                        elif d == 0:
                            act.wait_ge(*dve_drained.at(("cols", l)))
                        for s in range(NB):
                            o = full(("dec", l, h, d, s))
                            for a, b in block_pairs(d, s, l):
                                ins = f(W[:, d, s, a * P:b * P], o[:, a * P:b * P], ACT.Exp,
                                        bias=cols[:, 0, s, col:col + 1])
                            ins.then_inc(*act_drained.tick(("dec", l, h, d, s)))
                    fill(l, 2)
                act.wait_ge(*dve_done.at(("hvar", l)))
                g = (NB - lo // P) * NH
                f(stat[:, 2, 0:g], stat[:, 1, 0:g], ACT.Sqrt, scale=1.0 / DH, bias=eps).then_inc(*act_done.tick(("hstd", l)))

            def attention(l):
                lo = low(l)
                units = [(h, t) for h in range(NH) for t in range(lo // P, NB)]
                scale = DH ** -0.5

                def take_sum(h, func, **how):
                    o = full(("osum", l, h))
                    f(orstd[:, h, lo:T], o[:, lo:T], func, **how).then_inc(*act_drained.tick(("osum", l, h)))

                for n in range(len(units) + 2):
                    if n < len(units):
                        h, t = units[n]
                        nk = CTX if t < 2 else T
                        if n == 0:
                            act.wait_ge(*pe_done.at(("pv", l, NH - 1, 1)))
                        if n >= 2:
                            act.wait_ge(*pe_done.at(("aT", l) + units[n - 2]))
                        for c in range(2):
                            o = full(("s", l, h, t, c))
                            act.wait_ge(*dve_done.at(("smax", l, h, t, c)))
                            f(prob[:, n % 2, c, 0:nk], o[:, 0:nk], ACT.Exp, scale=scale, bias=rs[:, n % 2, 2 + c:3 + c],
                              accum_out=rs[:, n % 2, 4 + c:5 + c]).then_inc(*act_drained.tick(("s", l, h, t, c)))
                    if n == CONV_STEP[l] + 1:
                        conv_squares(l)
                    if n == CONV_STEP[l] + 2:
                        conv_deviation(l)
                    if n == CONV_STEP[l] + 4:
                        conv_output(l)
                    fill(l, 1)
                    if 1 <= n <= len(units):
                        h, t = units[n - 1]
                        nk = CTX if t < 2 else T
                        o = full(("aT", l, h, t))
                        if n >= 3:
                            act.wait_ge(*pe_done.at(("o", l) + units[n - 3]))
                        f(probT[:, (n - 1) % 2, 0:nk // P, :], o[:, 0:nk].rearrange("p (b q) -> p b q", q=P), ACT.Copy)\
                            .then_inc(*act_drained.tick(("aT", l, h, t)))
                    if n >= 2:
                        h, t = units[n - 2]
                        o = full(("o", l, h, t))
                        f(mix[:, 2 + h, t * P:(t + 1) * P], o[:, 0:P], ACT.Copy).then_inc(*act_drained.tick(("o", l, h, t)))
                        if t == NB - 1:
                            act.wait_ge(*act_drained.at(("o", l, h, t)))
                            if h >= 2:
                                act.wait_ge(*pe_done.at(("osum", l, h - 2)))
                            f(kq[:, 2 + h % 2, lo:T], mix[:, 2 + h, lo:T], ACT.Square).then_inc(*act_done.tick(("osq", l, h)))
                    if n >= 3 and units[n - 3][1] == NB - 1:
                        take_sum(units[n - 3][0], ACT.Copy)
                fill(l, MOD_CHUNKS)
                take_sum(NH - 1, ACT.Sqrt, scale=1.0 / DV, bias=eps)
                act.wait_ge(*act_drained.at(("osum", l, NH - 1)))
                for h in range(NH - 1):
                    ins = f(orstd[:, h, lo:T], orstd[:, h, lo:T], ACT.Sqrt, scale=1.0 / DV, bias=eps)
                    ins.then_inc(*act_done.tick(("ostd", l, h)))

            def conv_squares(l):
                lo = low(l)
                act.wait_ge(*dve_drained.at(("cmean", l)))
                f(kq[:, 0:2, lo:T], cy[:, :, lo:T], ACT.Square).then_inc(*act_done.tick(("csq", l)))

            def conv_deviation(l):
                lo = low(l)
                o = full(("cvar", l))
                f(rstd[:, lo:T], o[:, lo:T], ACT.Sqrt, scale=1.0 / CW, bias=eps).then_inc(*act_drained.tick(("cvar", l)))

            def conv_output(l):
                lo = low(l)
                act.wait_ge(*dve_done.at(("cn", l)))
                act.wait_ge(*pe_done.at(("hT", l, 1)))
                for m in range(2):
                    ins = f(mix[:, 6 + m, lo:T], cy[:, m, lo:T], ACT.Silu, scale=par("g_ln", l)[:, m:m + 1],
                            bias=par("b_ln", l)[:, m:m + 1])
                ins.then_inc(*act_done.tick(("mix_conv", l)))

            def dense():
                def leading(i):
                    act.wait_ge(*dve_drained.at(("up", i)))
                    f(hidden_hi(i), U[:, i, :], ACT.Copy).then_inc(*act_done.tick(("u_hi", i)))

                for i in range(FT):
                    o = full(("gate", i))
                    f(U[:, i, :], o, ACT.Silu).then_inc(*act_drained.tick(("gate", i)))
                    if i % 2 and i > 2 and i - 2 < UH + 2:
                        leading(i - 3)
                        leading(i - 2)
                act.wait_ge(*pe_done.at(("up", FT - 1)))
                for i in range(UH + 2, FT):
                    leading(i)

            def moe():
                act.wait_ge(*dve_done.at("moe_start"))
                n = act.value_load(trips[0:1, :], min_val=NE, max_val=PASSES * NE)
                act.sem_inc(y_act, 1)

                def take_input(count):
                    act.wait_ge(gathered, count)
                    f(h_slot[:, 0:4, :], ps[:, 4, :].rearrange("p (k n) -> p k n", k=4), ACT.Copy).then_inc(h_act, 1)

                take_input(1)
                with act.Fori(0, n) as i:
                    for t in range(ET):
                        act.wait_ge(sem_exp[t], i * 16 + 16)
                        last = t - 2 + ET if t >= 2 else max(x for x in range(ET) if x % 2 == t)
                        act.wait_ge(down_done, i * ET + (last + 1))
                        f(ew_hi[:, t % 2, :], experts[:, t, 2 * KD * P:], ACT.Copy).then_inc(down_leading, 1)
                        act.wait_ge(gu_full, i * ET + (t + 1))
                        last = t - 4 + ET if t >= 4 else max(x for x in range(ET) if x % 4 == t)
                        act.wait_ge(glu_done, i * ET + (last + 1))
                        f(esilu[:, t % 4, :], ps[:, 2 + t % 2, 0:P], ACT.Silu).then_inc(silu_done, 1)
                    take_input(i + 2)
                    act.wait_ge(down_done, i * ET + 2 * ET)
                    f(y_slot[:, 0:512], ps[:, 0, :], ACT.Copy).then_inc(y_act, 1)

            act.wait_ge(sem_small, 16)
            f(cond[:, :, :], par("c").rearrange("p (k s) -> p k s", k=KD), ACT.Silu).then_inc(*act_done.tick("cond"))
            for i in range(MOD_CHUNKS):
                modulation_rows(0, i)
            act.wait_ge(*dve_done.at("lamdot"))
            for l in range(DEPTH):
                ins = f(lam[:, l, 0:2], lam[:, l, 2:4], ACT.Exp)
            ins.then_inc(*act_done.tick("lamexp"))
            for l in range(DEPTH):
                norm(l, 0)
                project(l)
                mlstm(l)
                attention(l)
                norm(l, 1)
                if l == 0:
                    dense()
            act.wait_ge(*dve_drained.at("logits"))
            f(rt[:, 1], rt[:, 0], ACT.Exp).then_inc(*act_done.tick("router_exp"))
            for k in range(KD):
                o = full(("h_tok", k))
                f(h_tok[:, :, k * P:(k + 1) * P], o[:, 0:2 * P].rearrange("p (b n) -> p b n", b=2), ACT.Copy)\
                    .then_inc(*act_drained.tick(("h_tok", k)))
            moe()
            act.wait_ge(*dve_done.at("x_final"))
            f(experts[:, 0, 0:KD * SEQ].rearrange("p (k t) -> p k t", k=KD), X[:, :, CTX:T], ACT.Square)\
                .then_inc(*act_done.tick("final_sq"))
            act.wait_ge(*pe_done.at("final_ssq"))
            f(rstd[:, 0:SEQ], ps[:, 0, 0:SEQ], ACT.Sqrt, scale=1.0 / D, bias=eps).then_inc(*act_done.tick("final_std"))

        @block.vector
        def _(dve):
            v = nc.vector

            def full(key):
                dve.wait_ge(*pe_done.at(key))
                return ps[:, plan.get(("bank", key), 0), :]

            def settled(ins, key):
                ins.then_inc(*dve_done.tick(key))
                dve.wait_ge(*dve_done.at(key))

            def modulation(l):
                dve.wait_ge(*pe_done.at(("modT", l, MOD_CHUNKS - 1)))
                b = par("b_mod", l).unsqueeze(2).to_broadcast([P, 48, 2])
                settled(v.tensor_tensor(modc[:, l], ps[:, 7, 0:96].rearrange("p (m s) -> p m s", s=2), b, ALU.add),
                        ("modv", l))
                for which, g in ((0, "g1"), (1, "g2")):
                    at = 24 * which + KD
                    ins = v.scalar_tensor_tensor(gain[:, l, which], modc[:, l, at:at + KD, :], 1.0,
                                                 par(g, l).unsqueeze(2).to_broadcast([P, KD, 2]), ALU.add, ALU.mult)
                ins.then_inc(*dve_done.tick(("modc", l)))

            def norm(l, which):
                lo = low(l) if which else 0
                if which == 0:
                    dve.wait_ge(sem_gw[l], 16)
                    leading_bits(wg_hi[:, :, :], wg_lo[:, :, :], w_gates, ("wg", l))
                if (l, which) != (1, 1):
                    split(("gate", 0, 0) if which else ("in", l, IN_ORDER[0]))
                dve.wait_ge(*act_drained.at(("ssq", l, which)))
                settled(v.reciprocal(rstd[:, 0:T - lo], rstd[:, 0:T - lo]), ("rstd", l, which))
                dve.wait_ge(*pe_done.at(("ssq", l, which)))
                for k in range(KD):
                    v.tensor_tensor(sq[:, k, 0:T - lo], X[:, k, lo:T], rstd[:, 0:T - lo], ALU.mult)\
                        .then_inc(*dve_done.tick(("xn", l, which, k)))
                if (l, which) == (1, 1):
                    return
                for k in range(KD):
                    dve.wait_ge(*act_done.at(("h", l, which, k)))
                    leading_bits(h_hi[:, k, :], h_lo[:, k, :], hT[:, k, :], ("h_split", l, which, k))

            def leading_bits(hi, lo, x, key):
                settled(v.tensor_copy(hi, x), ("hi", key))
                v.tensor_tensor(lo, x, hi.bitcast(F32), ALU.subtract).then_inc(*dve_done.tick(key))

            def split(chunk):
                n, s = slot_of[chunk], split_of[chunk]
                if s >= SPLIT:
                    dve.wait_ge(*pe_done.at(last_product(split_chunks[s - SPLIT])))
                dve.wait_ge(sem_slot[n % RING], 16 * (n // RING + 1))
                kind, l, i = chunk
                k = slice(0, min(KD, FT - KD * i[1]) if kind == "down" else KD)
                leading_bits(w_hi[:, s % SPLIT, k], w_lo[:, n % RING, k], chunk_view(chunk)[:, k], ("split", chunk))

            def gate_rows(l):
                R = GATE_ROWS
                settled(v.memset(scratch[0:64, 2 * T:8 * T], 0.0), ("clear", l))
                split(("in", l, IN_ORDER[1]))
                dve.wait_ge(*act_done.at(("gln", l)))
                settled(v.scalar_tensor_tensor(gate_ls[0:R, :], gate_raw[0:R, :], 0.0, gate_ls[0:R, :],
                                               ALU.min, ALU.subtract), ("logsig", l))
                v.tensor_copy(li[0:NH, :], gate_raw[0:NH, :])
                v.tensor_copy(lf[0:NH, :], gate_ls[32:32 + NH, :])
                for s in range(2):
                    seg = slice(s * SEQ, (s + 1) * SEQ)
                    v.tensor_copy(li[32:32 + NH, seg], gate_raw[64:64 + NH, seg][:, ::-1])
                    ins = v.tensor_copy(lf[32:32 + NH, seg], gate_ls[96:96 + NH, seg][:, ::-1])
                settled(ins, ("gates_seq", l))
                settled(v.tensor_tensor_scan(row_b, reset, lf, 0.0, ALU.mult, ALU.add), ("row_b", l))
                settled(v.tensor_tensor_scan(row_m, lf, li, NEG, ALU.add, ALU.max), ("row_m", l))
                split(("in", l, IN_ORDER[2]))
                v.tensor_tensor(row_a, li, row_b, ALU.subtract)
                for j in range(NB):
                    blk = slice(j * P, (j + 1) * P)
                    ins = v.tensor_tensor(row_r[:, j, blk], row_b[:, blk], row_m[:, blk], ALU.subtract)
                settled(ins, ("row_r", l))
                for j in reversed(range(NB - 1)):
                    later = slice((j + 1) * P, T)
                    settled(v.tensor_scalar(row_r[:, j, later], row_r[:, j + 1, later],
                                            row_b[:, (j + 1) * P - 1:(j + 1) * P], None, ALU.add), ("row_r", l, j))
                split(("in", l, IN_ORDER[3]))
                dve.wait_ge(*act_done.at(("row_em", l)))
                v.tensor_copy(rows_n[0:32, 0:4, :], row_r[0:32])
                v.tensor_copy(rows_n[0:32, 4:6, :], kq[0:32, 0:2, :])
                for s in range(2):
                    seg = slice(s * SEQ, (s + 1) * SEQ)
                    v.tensor_copy(rows_n[32:64, 0:4, seg], row_r[32:64, :, seg][:, :, ::-1])
                    ins = v.tensor_copy(rows_n[32:64, 4:6, seg], kq[32:64, 0:2, seg][:, :, ::-1])
                ins.then_inc(*dve_done.tick(("rows", l)))

            def rope(l, name):
                x = (ak if name[:2] == "ak" else aq)[:, 2 * int(name[-1]):2 * int(name[-1]) + 2, CTX:T]
                y = rstd[:, :].rearrange("p (m t) -> p m t", m=2)
                dve.wait_ge(*act_drained.at((name, l, 1)))
                settled(v.stream_shuffle(y, x, [i ^ 16 for i in range(32)]), ("partner", l, name))
                v.tensor_tensor(x, x, cos.unsqueeze(1).to_broadcast([P, 2, SEQ]), ALU.mult)
                settled(v.tensor_tensor(y, y, sin.unsqueeze(1).to_broadcast([P, 2, SEQ]), ALU.mult), ("ropesin", l, name))
                settled(v.tensor_tensor(x, x, y, ALU.add), ("rope", l, name))

            def project(l):
                gate_rows(l)
                for n, name in enumerate(IN_ORDER):
                    if n >= 3 and n + 1 < len(IN_ORDER):
                        split(("in", l, IN_ORDER[n + 1]))
                    if n and IN_ORDER[n - 1] in ("ak0", "ak1", "aq0", "aq1"):
                        rope(l, IN_ORDER[n - 1])
                    if name == "ca":
                        conv_input(l)

            def conv_input(l):
                dve.wait_ge(*pool_done.at(("pads", l)))
                for m in range(2):
                    o = full(("ca", l, m))
                    dve.wait_ge(*act_drained.at(("cg", l, m)))
                    s = slice(low(l) // CTX, 2)
                    v.tensor_tensor(upad[:, m, s, PAD:PAD + SEQ], o.rearrange("p (s t) -> p s t", s=2)[:, s],
                                    mo[:, m, :].rearrange("p (s t) -> p s t", s=2)[:, s], ALU.mult)\
                        .then_inc(*dve_drained.tick(("ca", l, m)))

            def mlstm(l):
                t0 = low(l) // P
                o = full(("cols", l))
                v.tensor_copy(cols[:, :, :, :].rearrange("p a b r -> p (a b r)"), o).then_inc(*dve_drained.tick(("cols", l)))
                dve.wait_ge(*dve_drained.at(("cols", l)))

                def head_sums(h):
                    for d in range(2):
                        i, col = 2 * h + d, 32 * d + h
                        o = full(("pv", l, h, d)).rearrange("p (b c) -> p b c", b=NB)
                        settled(v.scalar_tensor_tensor(den[:, i, t0:NB], o[:, t0:NB, DH], -1.0, cols[:, 1, t0:NB, col],
                                                       ALU.mult, ALU.max), ("nden", l, h, d))
                        settled(v.tensor_tensor(den[:, i, t0:NB], o[:, t0:NB, DH], den[:, i, t0:NB], ALU.max),
                                ("den", l, h, d))
                        settled(v.reciprocal(den[:, i, t0:NB], den[:, i, t0:NB]), ("rden", l, h, d))
                        for t in range(t0, NB):
                            if d == 0:
                                ins = v.tensor_scalar(hsum[:, t, h, :], o[:, t, 0:DH], den[:, i, t:t + 1], None, ALU.mult)
                            else:
                                ins = v.scalar_tensor_tensor(hsum[:, t, h, :], o[:, t, 0:DH], den[:, i, t:t + 1],
                                                             hsum[:, t, h, :], ALU.mult, ALU.add)
                        ins.then_inc(*dve_drained.tick(("pv", l, h, d)))
                        dve.wait_ge(*dve_drained.at(("pv", l, h, d)))

                for h in range(NH):
                    for d in range(2):
                        for s in range(NB):
                            dve.wait_ge(*act_drained.at(("dec", l, h, d, s)))
                            for a, b in block_pairs(d, s, l):
                                w = W[:, d, s, a * P:b * P]
                                ins = v.tensor_tensor(w, w, kq[:, s, a * P:b * P], ALU.mult)
                            ins.then_inc(*dve_done.tick(("w", l, h, d, s)))
                    if h == 0:
                        dve.wait_ge(*pe_done.at(("mo", l, 1)))
                    head_sums(h)
                g = (NB - t0) * NH
                x = hsum.rearrange("p b h v -> p (b h) v")[:, t0 * NH:NB * NH, :]
                x2 = hsq.rearrange("p (g v) -> p g v", v=DH)[:, 0:g, :]

                def spread(i):
                    return stat[:, i, 0:g].unsqueeze(2).to_broadcast([P, g, DH])

                settled(v.tensor_reduce(stat[:, 0, 0:g], x, AX_X, ALU.add), ("hsum", l))
                settled(v.tensor_scalar(stat[:, 0, 0:g], stat[:, 0, 0:g], 1.0 / DH, None, ALU.mult), ("hmean", l))
                settled(v.tensor_tensor(x, x, spread(0), ALU.subtract), ("hcen", l))
                settled(v.tensor_tensor(x2, x, x, ALU.mult), ("hsq", l))
                settled(v.tensor_reduce(stat[:, 1, 0:g], x2, AX_X, ALU.add), ("hvar", l))
                dve.wait_ge(*act_done.at(("hstd", l)))
                settled(v.reciprocal(stat[:, 3, 0:g], stat[:, 2, 0:g]), ("hrstd", l))
                v.tensor_tensor(x, x, spread(3), ALU.mult).then_inc(*dve_done.tick(("hn", l)))
                lo = low(l)
                for m in range(2):
                    o = full(("hT", l, m))
                    dve.wait_ge(*act_drained.at(("mo", l, m)))
                    v.scalar_tensor_tensor(mix[:, m, lo:T], o[:, lo:T], par("g_mlstm", l)[:, m:m + 1], mo[:, m, lo:T],
                                           ALU.mult, ALU.mult).then_inc(*dve_drained.tick(("hT", l, m)))

            def attention(l):
                lo = low(l)
                units = [(h, t) for h in range(NH) for t in range(lo // P, NB)]

                def maxima(n):
                    h, t = units[n]
                    nk = CTX if t < 2 else T
                    u = n % 2
                    for c in range(2):
                        o = full(("s", l, h, t, c))
                        settled(v.tensor_reduce(rs[:, u, c:c + 1], o[:, 0:nk], AX_X, ALU.max), ("max", l, h, t, c))
                        v.tensor_scalar(rs[:, u, 2 + c:3 + c], rs[:, u, c:c + 1], -DH ** -0.5, None, ALU.mult)\
                            .then_inc(*dve_done.tick(("smax", l, h, t, c)))

                def combine(n):
                    h, t = units[n]
                    nk = CTX if t < 2 else T
                    u = n % 2
                    dve.wait_ge(*act_drained.at(("s", l, h, t, 1)))
                    settled(v.reciprocal(rs[:, u, 6:8], rs[:, u, 4:6]), ("rsum", l, h, t))
                    settled(v.tensor_tensor(rs[:, u, 8:9], rs[:, u, 7:8], nlam(l), ALU.mult), ("lsum", l, h, t))
                    p = prob[:, u]
                    settled(v.tensor_scalar(p[:, 1, 0:nk], p[:, 1, 0:nk], rs[:, u, 8:9], None, ALU.mult), ("p1", l, h, t))
                    v.scalar_tensor_tensor(p[:, 0, 0:nk], p[:, 0, 0:nk], rs[:, u, 6:7], p[:, 1, 0:nk],
                                           ALU.mult, ALU.add).then_inc(*dve_done.tick(("a", l, h, t)))

                for n in range(len(units) + 1):
                    if n < len(units):
                        maxima(n)
                    if n == CONV_STEP[l]:
                        conv_centre(l)
                    if n == CONV_STEP[l] + 3:
                        conv_scale(l)
                    if n:
                        combine(n - 1)
                lam_init = 0.8 - 0.6 * math.exp(-0.3 * l)
                settled(v.tensor_scalar(stat[:, 0, 0:1], par("g_sub", l)[:, 0:1], 1.0 - lam_init, None, ALU.mult),
                        ("g_sub", l))
                for h in OUT_ORDER:
                    dve.wait_ge(*(act_done.at(("ostd", l, h)) if h < NH - 1 else act_drained.at(("osum", l, h))))
                    settled(v.reciprocal(orstd[:, h, lo:T], orstd[:, h, lo:T]), ("orstd", l, h))
                    v.scalar_tensor_tensor(mix[:, 2 + h, lo:T], mix[:, 2 + h, lo:T], stat[:, 0, 0:1], orstd[:, h, lo:T],
                                           ALU.mult, ALU.mult).then_inc(*dve_done.tick(("mix_attn", l, h)))

            def conv_centre(l):
                lo = low(l)
                o = full(("cmean", l))
                for m in range(2):
                    ins = v.scalar_tensor_tensor(cy[:, m, lo:T], o[:, lo:T], -1.0 / CW, cy[:, m, lo:T], ALU.mult, ALU.add)
                ins.then_inc(*dve_drained.tick(("cmean", l)))

            def conv_scale(l):
                lo = low(l)
                dve.wait_ge(*act_drained.at(("cvar", l)))
                settled(v.reciprocal(rstd[:, lo:T], rstd[:, lo:T]), ("crstd", l))
                for m in range(2):
                    ins = v.tensor_tensor(cy[:, m, lo:T], cy[:, m, lo:T], rstd[:, lo:T], ALU.mult)
                ins.then_inc(*dve_done.tick(("cn", l)))

            def residual(l, kind, gate, key, tiles=range(KD)):
                for m in tiles:
                    o = full(key(m))
                    for s in range(low(l) // CTX, 2):
                        seg = slice(s * SEQ, (s + 1) * SEQ)
                        ins = v.scalar_tensor_tensor(X[:, m, seg], o[:, seg], modc[:, l, gate + m, s:s + 1], X[:, m, seg],
                                                     ALU.mult, ALU.add)
                    ins.then_inc(*dve_drained.tick(key(m)))

            def dense():
                def remainder(f):
                    dve.wait_ge(*act_done.at(("u_hi", f)))
                    v.tensor_tensor(u_lo[:, f, :], U[:, f, :], hidden_hi(f).bitcast(F32), ALU.subtract)\
                        .then_inc(*dve_done.tick(("u_split", f)))

                split(("up", 0, 0))
                for i in range(FF // CHUNK):
                    split(("gate", 0, i + 1) if i + 1 < FF // CHUNK else ("down", 0, (0, 0)))
                    for m in (2 * i, 2 * i + 1):
                        o = full(("up", m))
                        dve.wait_ge(*act_drained.at(("gate", m)))
                        v.tensor_tensor(U[:, m, :], U[:, m, :], o, ALU.mult).then_inc(*dve_drained.tick(("up", m)))
                    if 0 < i and 2 * i <= UH + 2:
                        remainder(2 * i - 2)
                        remainder(2 * i - 1)
                    split(("up", 0, i + 1) if i + 1 < FF // CHUNK else ("down", 0, (0, 1)))
                for f in range(UH + 2, FT):
                    remainder(f)
                for i in range(D // CHUNK):
                    for j in range(3):
                        if (i, j) > (0, 1):
                            split(("down", 0, (i, j)))
                        if i and j == 1:
                            residual(0, "ffn", 40, lambda m: ("ffn", m), range(2 * i - 2, 2 * i))
                residual(0, "ffn", 40, lambda m: ("ffn", m), range(KD - 2, KD))

            def router():
                o = full("logits")[:, 0:2 * NE].rearrange("p (b e) -> p b e", b=2)

                def wide(t):
                    return t.unsqueeze(2).to_broadcast([P, 2, NE])

                ordb = order.unsqueeze(1).to_broadcast([P, 2, NE])
                settled(v.tensor_tensor(rt[:, 0], o, par("b_router").unsqueeze(1).to_broadcast([P, 2, NE]), ALU.add), "bias")
                settled(v.tensor_reduce(r1[:, 0], rt[:, 0], AX_X, ALU.max), "lmax")
                v.tensor_tensor(rt[:, 0], rt[:, 0], wide(r1[:, 0]), ALU.subtract).then_inc(*dve_drained.tick("logits"))
                dve.wait_ge(*act_done.at("router_exp"))
                settled(v.tensor_reduce(r1[:, 1], rt[:, 1], AX_X, ALU.add), "psum")
                settled(v.reciprocal(r1[:, 1], r1[:, 1]), "rpsum")
                settled(v.tensor_tensor(rt[:, 2], rt[:, 1], wide(r1[:, 1]), ALU.mult), "probs")
                for i in range(2):
                    settled(v.tensor_reduce(r1[:, 2 + i], rt[:, 2], AX_X, ALU.max), ("top", i))
                    settled(v.tensor_tensor(rt[:, 3], rt[:, 2], wide(r1[:, 2 + i]), ALU.is_ge), ("is_top", i))
                    settled(v.tensor_tensor(rt[:, 3], rt[:, 3], ordb, ALU.mult), ("rank", i))
                    settled(v.tensor_reduce(r1[:, 4], rt[:, 3], AX_X, ALU.max), ("first", i))
                    settled(v.tensor_tensor(rt[:, 4 + i], rt[:, 3], wide(r1[:, 4]), ALU.is_equal), ("chosen", i))
                    if i == 0:
                        settled(v.scalar_tensor_tensor(rt[:, 2], rt[:, 4], -2.0, rt[:, 2], ALU.mult, ALU.add), "out")
                settled(v.tensor_tensor(rt[:, 6], rt[:, 4], rt[:, 5], ALU.add), "chosen")
                settled(v.tensor_tensor(r1[:, 5], r1[:, 2], r1[:, 3], ALU.add), "topsum")
                settled(v.reciprocal(r1[:, 5], r1[:, 5]), "rtopsum")
                for i in range(2):
                    settled(v.tensor_tensor(r1[:, 6 + i], r1[:, 2 + i], r1[:, 5], ALU.mult), ("share", i))
                    settled(v.tensor_tensor(rt[:, 4 + i], rt[:, 4 + i], wide(r1[:, 6 + i]), ALU.mult), ("shares", i))
                v.memset(slot_no, -1.0)
                settled(v.memset(share, 0.0), "slots0")
                by_expert = "p b e -> p e b"
                for r in range(PASSES):
                    ins = v.tensor_tensor(share[:, r * NE:(r + 1) * NE, :], rt[:, 4].rearrange(by_expert),
                                          rt[:, 5].rearrange(by_expert), ALU.add)
                o = full("rank")
                rank = o[:, 0:2 * NE].rearrange("p (b e) -> p b e", b=2)
                settled(v.tensor_scalar(rt[:, 7], rank, 1.0, None, ALU.add), "rank1")
                settled(v.tensor_tensor(rt[:, 7], rt[:, 7], rt[:, 6], ALU.mult), "rank_chosen")
                for r in range(PASSES):
                    ins = v.tensor_scalar(slot_no[:, r * NE:(r + 1) * NE, :], rt[:, 7].rearrange(by_expert),
                                          -1.0 - r * P, None, ALU.add)
                settled(v.tensor_reduce(r1[:, 4, 0:1], o[:, 2 * NE:3 * NE], AX_X, ALU.max), "most")
                settled(v.tensor_scalar(r1[:, 4, 0:1], r1[:, 4, 0:1], P + 0.5, float(NE), ALU.is_gt, ALU.mult), "round2")
                v.tensor_scalar(trips, r1[:, 4, 0:1], float(NE), None, ALU.add).then_inc(*dve_done.tick("trips"))
                dve.wait_ge(*dve_done.at("trips"))
                dve.wait_ge(*pe_done.at(("h_tok", KD - 1)))
                v.memset(y_slot, 0.0)
                v.memset(from_slot, 0.0).then_inc(*dve_done.tick("moe_start"))
                dve.wait_ge(*dve_done.at("moe_start"))
                dve.sem_inc(y_dve, 1)
                dve.sem_inc(from_slot_ready, 1)
                dve.sem_inc(glu_done, ET)
                dve.sem_inc(x_added, 2)

            def moe():
                n = dve.value_load(trips[0:1, :], min_val=NE, max_val=PASSES * NE)
                slots = field(con, CONST, "slots")

                def column(table, i, b):
                    return table[:, bass.ds(i, 1), b]

                def build_slots(i, count):
                    for b in range(2):
                        ins = v.tensor_scalar(to_slot[:, b, :], slots, column(slot_no, i, b), None, ALU.is_equal)
                    ins.then_inc(slots_built, 1)

                def take_input(count):
                    dve.wait_ge(gathered, count)
                    v.tensor_copy(h_slot[:, 4:8, :], ps[:, 5, :].rearrange("p (k n) -> p k n", k=4)).then_inc(h_dve, 1)

                def add_output(i):
                    for q in range(4):
                        dve.wait_ge(scattered, i * 4 + (q + 1))
                        for m in range(2):
                            k = 2 * q + m
                            ins = v.scalar_tensor_tensor(X[:, k, CTX:T], ps[:, 6 + q % 2, m * SEQ:(m + 1) * SEQ],
                                                         modc[:, 1, 40 + k, 1:2], X[:, k, CTX:T], ALU.mult, ALU.add)
                        ins.then_inc(x_added, 1)

                build_slots(0, 1)
                take_input(1)
                with dve.Fori(0, n) as i:
                    for t in range(ET):
                        dve.wait_ge(down_leading, i * ET + (t + 1))
                        v.tensor_tensor(ew_lo[t][:, :], experts[:, t, 2 * KD * P:], ew_hi[:, t % 2, :].bitcast(F32),
                                        ALU.subtract).then_inc(down_split, 1)
                        last = t - 4 + ET if t >= 4 else max(x for x in range(ET) if x % 4 == t)
                        dve.wait_ge(down_done, i * ET + (last + 1))
                        dve.wait_ge(silu_done, i * ET + (t + 1))
                        up = ps[:, 2 + t % 2, P:2 * P]
                        v.tensor_tensor(ehid[:, t % 4, :], esilu[:, t % 4, :], up, ALU.mult)
                        v.tensor_tensor(e_hi[:, t % 4, :], esilu[:, t % 4, :], up, ALU.mult).then_inc(hidden, 1)
                        dve.wait_ge(hidden, i * ET + (t + 1))
                        v.tensor_tensor(e_lo[:, t % 4, :], ehid[:, t % 4, :], e_hi[:, t % 4, :].bitcast(F32), ALU.subtract)\
                            .then_inc(glu_done, 1)
                        if t == 1:
                            dve.wait_ge(shares_turned, i + 1)
                            for b in range(2):
                                ins = v.tensor_scalar(shares[:, b, :], slots, column(slot_no, i, b), column(share, i, b),
                                                      ALU.is_equal, ALU.mult)
                            ins.then_inc(shares_built, 1)
                        if t == 2:
                            dve.wait_ge(x_added, i * 4 + 2)
                            add_output(i)
                        if t == 5:
                            dve.wait_ge(shares_turned, i + 2)
                            v.tensor_copy(from_slot, ps[:, 4, 0:2 * P]).then_inc(from_slot_ready, 1)
                            dve.wait_ge(gathered, i + 1)
                            build_slots(i + 1, i + 2)
                    take_input(i + 2)
                    dve.wait_ge(down_done, i * ET + 2 * ET)
                    v.tensor_copy(y_slot[:, 512:1024], ps[:, 1, :]).then_inc(y_dve, 1)
                dve.wait_ge(x_added, n * 4 + 2)
                add_output(n)
                dve.wait_ge(x_added, n * 4 + 6)
                v.tensor_copy(r1[:, 4, 0:1], r1[:, 4, 1:2]).then_inc(*dve_done.tick("x_final"))

            def nlam(l):
                return lam[:, l, 0:1]

            dve.wait_ge(sem_small, 16)
            q = par("lam").rearrange("p (l a d) -> p l a d", l=DEPTH, a=4)
            pr = lprod[:, 256:512].rearrange("p (a d) -> p a d", a=2 * DEPTH)
            for l in range(DEPTH):
                for i in range(2):
                    ins = v.tensor_tensor(pr[:, 2 * l + i], q[:, l, 2 * i], q[:, l, 2 * i + 1], ALU.mult)
            settled(ins, "lamprod")
            for l in range(DEPTH):
                ins = v.tensor_reduce(lam[:, l, 2:4], pr[:, 2 * l:2 * l + 2], AX_X, ALU.add)
            settled(ins, "lamdot")
            dve.wait_ge(*act_done.at("lamexp"))
            for l in range(DEPTH):
                lam_init = 0.8 - 0.6 * math.exp(-0.3 * l)
                settled(v.tensor_tensor(lam[:, l, 2:3], lam[:, l, 1:2], lam[:, l, 0:1], ALU.subtract), ("lamdiff", l))
                settled(v.tensor_scalar(lam[:, l, 0:1], lam[:, l, 2:3], -lam_init, None, ALU.add), ("nlam", l))
            for l in range(DEPTH):
                if l == 0:
                    modulation(0)
                norm(l, 0)
                project(l)
                mlstm(l)
                attention(l)
                if l == 0:
                    modulation(1)
                residual(l, "y", 16, lambda m: ("y", l, m))
                dve.wait_ge(*dve_drained.at(("y", l, KD - 1)))
                norm(l, 1)
                if l == 0:
                    dense()
                    dve.wait_ge(*dve_drained.at(("ffn", KD - 1)))
            router()
            moe()
            dve.wait_ge(*act_done.at("final_std"))
            settled(v.reciprocal(rstd[:, 0:SEQ], rstd[:, 0:SEQ]), "final_rstd")
            for k in range(KD):
                ins = v.scalar_tensor_tensor(h2[:, k, :], X[:, k, CTX:T], par("g_final")[:, k:k + 1], rstd[:, 0:SEQ],
                                             ALU.mult, ALU.mult)
            ins.then_inc(*dve_done.tick("final"))

        @block.gpsimd
        def _(pool):
            g = nc.gpsimd
            for l in range(DEPTH):
                s0 = low(l) // CTX
                pool.wait_ge(*act_done.at(("h", l, 0, KD - 1)))
                g.memset(upad[:, :, :, 0:PAD], 0.0)
                g.memset(upad[:, :, :, PAD + SEQ:], 0.0)
                g.memset(vm_all[:, NB * NH * (DH + 1):], 1.0)
                g.memset(vm[:, :, :, DH:DH + 1], 1.0).then_inc(*pool_done.tick(("pads", l)))
                for m in range(2):
                    pool.wait_ge(*dve_drained.at(("ca", l, m)))
                    w = par("w_dw", l).rearrange("p (m j) -> p m j", m=2)[:, m]
                    y = cy[:, m, :].rearrange("p (s t) -> p s t", s=2)[:, s0:2]
                    for j in range(TAPS):
                        u = upad[:, m, s0:2, j:j + SEQ]
                        if j:
                            pool.wait_ge(*pool_done.at(("tap", l, m, j - 1)))
                        if j == 0:
                            ins = g.tensor_scalar(y, u, w[:, 0:1], par("b_dw", l)[:, m:m + 1], ALU.mult, ALU.add)
                        else:
                            p = tap.rearrange("p (s t) -> p s t", s=2)[:, s0:2]
                            g.tensor_scalar(p, u, w[:, j:j + 1], None, ALU.mult)\
                             .then_inc(*pool_done.tick(("product", l, m, j)))
                            pool.wait_ge(*pool_done.at(("product", l, m, j)))
                            ins = g.tensor_tensor(y, y, p, ALU.add)
                        ins.then_inc(*pool_done.tick(("tap", l, m, j) if (m, j) != (1, TAPS - 1) else ("conv", l)))


def constants():
    con = np.zeros((P, NCONST), np.float32)

    def put(name, value):
        a, n = CONST[name]
        con[:value.shape[0], a:a + n] = value.reshape(value.shape[0], n)

    put("ident", np.eye(P, dtype=np.float32))
    put("ones", np.ones((P, P), np.float32))
    i = np.arange(P)
    put("mask_f", np.where(i[None, :] >= i[:, None], 0.0, NEG).astype(np.float32))
    put("mask_b", np.where(i[None, :] <= i[:, None], 0.0, NEG).astype(np.float32))
    axis, half, n = (i % 64) // 32, (i % 32) // 16, i % 16
    inv = (np.float32(10000.0) ** (-(2 * n).astype(np.float32) / np.float32(32))).astype(np.float32)
    t = np.arange(SEQ)
    pos = np.where(axis[:, None] == 0, (t // 64)[None, :], (t % 64)[None, :]).astype(np.float32)
    ang = pos * inv[:, None]
    put("cos", np.cos(ang).astype(np.float32))
    put("sin", (np.where(half[:, None] == 0, -1.0, 1.0) * np.sin(ang)).astype(np.float32))
    put("reset", np.broadcast_to((np.arange(T) % P != 0).astype(np.float32), (P, T)))
    pick = np.zeros((P, 2 * NH, P), np.float32)
    for r in range(2 * NH):
        pick[32 * (r // NH) + r % NH, r] = 1.0
    put("pick", pick)
    put("before", (i[:, None] < i[None, :]).astype(np.float32))
    put("slots", np.broadcast_to(i.astype(np.float32), (P, P)))
    put("order", np.broadcast_to(np.arange(NE, 0, -1).astype(np.float32), (P, NE)))
    put("eps", np.full((P, 1), EPS, np.float32))
    put("one", np.ones((P, 1), np.float32))
    return con


def column_chunks(w, width):
    return w.reshape(KD, P, -1, width).transpose(2, 1, 0, 3).reshape(-1, P, KD * width)


def feature_major(v):
    v = v.reshape(v.shape[:-1] + (v.shape[-1] // P, P))
    return np.moveaxis(v, -1, 0).reshape(P, -1)


def lay_out(i):
    small = np.zeros((P, NSMALL), np.float32)

    def put(name, value):
        a, n = SMALL[name]
        small[:value.shape[0], a:a + n] = value.reshape(value.shape[0], n)

    put("c", np.stack([feature_major(i["c_ctx"]), feature_major(i["c"][0])], axis=-1))
    for name, src in (("b_mod", "b_mod"), ("g1", "g_norm1"), ("g2", "g_norm2"), ("g_mlstm", "g_mlstm"),
                      ("g_sub", "g_subln"), ("b_dw", "b_dw"), ("g_ln", "g_conv_ln"), ("b_ln", "b_conv_ln"),
                      ("g_final", "g_final")):
        put(name, feature_major(i[src]))
    bg = np.zeros((P, DEPTH), np.float32)
    gates = np.zeros((DEPTH, P, KD, GATE_ROWS), np.float32)
    for r in range(4):
        bg[32 * r:32 * r + NH] = i["b_gates"][:, NH * r:NH * (r + 1)].T
        cols = i["w_in"][:, :, GATE_COL + NH * r:GATE_COL + NH * (r + 1)]
        gates[:, :, :, 32 * r:32 * r + NH] = cols.reshape(DEPTH, KD, P, NH).transpose(0, 2, 1, 3)
    put("b_gates", bg)
    lam = np.stack([i["lambda_q1"], i["lambda_k1"], i["lambda_q2"], i["lambda_k2"]], axis=1)
    put("lam", np.broadcast_to(lam.reshape(1, -1), (P, lam.size)))
    put("w_dw", i["w_dw"].reshape(DEPTH, TAPS, 2, P).transpose(3, 0, 2, 1).reshape(P, -1))
    put("w_router", i["w_router"][0].reshape(KD, P, NE).transpose(1, 0, 2).reshape(P, -1))
    put("b_router", np.broadcast_to(i["b_router"][0], (P, NE)))
    x = np.concatenate([i["ctx"][0], i["x"][0]], axis=0)
    down = np.zeros((3 * KD * P, D), np.float32)
    down[:FF] = i["w_ffn_down"][0]
    exp_gu = [i[n][0].reshape(NE, KD, P, ET, P).transpose(0, 3, 2, 1, 4).reshape(NE, ET, P, KD * P)
              for n in ("w_exp_gate", "w_exp_up")]
    exp_dn = i["w_exp_down"][0].reshape(NE, ET, P, D)
    return {
        "con": constants(),
        "small": small,
        "x": x.T.reshape(KD, P, T).transpose(1, 0, 2).reshape(P, KD * T),
        "gates": gates.reshape(DEPTH, P, KD * GATE_ROWS),
        "mod": np.stack([column_chunks(w, CHUNK) for w in i["w_mod"]]),
        "in": np.stack([np.concatenate([column_chunks(w[:, IN_COL[n]:IN_COL[n] + CHUNK], CHUNK) for n in IN_ORDER])
                        for w in i["w_in"]]),
        "out": np.stack([column_chunks(w, CHUNK) for w in i["w_out"]]),
        "gate": column_chunks(i["w_ffn_gate"][0], CHUNK),
        "up": column_chunks(i["w_ffn_up"][0], CHUNK),
        "down": down.reshape(3, KD, P, D // CHUNK, CHUNK).transpose(3, 0, 2, 1, 4).reshape(D // CHUNK, 3, P, SLOT),
        "experts": np.concatenate(exp_gu + [exp_dn], axis=3),
    }


def kernel(**inputs):
    import concourse.bacc as _bacc
    from concourse.bass_utils import run_bass_kernel_spmd as _run

    arrays = {k: np.ascontiguousarray(v) for k, v in lay_out({k: np.asarray(v) for k, v in inputs.items()}).items()}
    plan = {}
    for complete in (False, True):
        nc = _bacc.Bacc("TRN2", target_bir_lowering=False, num_devices=1)
        A = {n: nc.dram_tensor(n, a.shape, F32, kind="ExternalInput").ap() for n, a in arrays.items()}
        A["out_0"] = nc.dram_tensor("out_0", (P, KD * SEQ), F32, kind="ExternalOutput").ap()
        plan["complete"] = complete
        build(nc, A, plan)
    r = _run(nc, [arrays], core_ids=[0])
    y = r.results[0]["out_0"].reshape(P, KD, SEQ)
    return y.transpose(2, 1, 0).reshape(1, SEQ, D)
```
